# Optimizing a Trainium2 kernel written in Bass

```python
import jax
import jax.numpy as jnp
from jax import lax
import numpy as np
import math
import jax, jax.numpy as jnp

D_MODEL = 1024
BATCH = 1
SEQ = 1024
DEPTH = 2

CHUNK = 64
N_META = 16
N_HEADS_A = 8
HEAD_DIM = 64
D_A = N_HEADS_A * HEAD_DIM
N_IDX_HEADS = 8
IDX_DIM = HEAD_DIM
TOPK_MAX = 256
POOL_WINDOWS = (2, 4, 8, 16)
N_POOL_GROUPS = len(POOL_WINDOWS)
D_B = D_MODEL // 2
POOL_GROUP_DIM = D_B // N_POOL_GROUPS
Q_BLOCK = 128
ROPE_THETA = 10000.0
EPS = 1e-6
NEG_INF = -1e30
IN_WIDTHS = (D_A, HEAD_DIM, HEAD_DIM, D_A, D_B, D_B, N_IDX_HEADS * IDX_DIM, IDX_DIM, N_IDX_HEADS, 2 * D_MODEL)
D_IN = sum(IN_WIDTHS)


def rms_norm(x, g):
    xf = x.astype(jnp.float32)
    y = xf * lax.rsqrt(jnp.mean(xf * xf, axis=-1, keepdims=True) + EPS)
    return (y * g.astype(jnp.float32)).astype(x.dtype)

def rope_tables(length, dim):
    inv_freq = 1.0 / (ROPE_THETA ** (jnp.arange(0, dim, 2, dtype=jnp.float32) / dim))
    ang = jnp.arange(length, dtype=jnp.float32)[:, None] * inv_freq[None, :]
    ang = jnp.concatenate([ang, ang], axis=-1)
    return jnp.cos(ang), jnp.sin(ang)

def apply_rope(x, cos, sin):
    half = x.shape[-1] // 2
    xf = x.astype(jnp.float32)
    rot = jnp.concatenate([-xf[..., half:], xf[..., :half]], axis=-1)
    return (xf * cos + rot * sin).astype(x.dtype)

def chunk_id(pos):
    return jnp.where(pos < N_META, 0, 1 + (pos - N_META) // CHUNK)

def indexer_sparse_attention(q, k, v, q_idx, k_idx, w_idx, k_top):
    B, T = q.shape[0], q.shape[1]
    n_blk = -(-T // Q_BLOCK)
    t_pad = n_blk * Q_BLOCK

    def to_blocks(a):
        a = jnp.pad(a, [(0, 0), (0, t_pad - T)] + [(0, 0)] * (a.ndim - 2))
        return jnp.moveaxis(a.reshape((B, n_blk, Q_BLOCK) + a.shape[2:]), 1, 0)

    key_chunk = chunk_id(jnp.arange(T))
    query_chunk = chunk_id(jnp.arange(t_pad)).reshape(n_blk, Q_BLOCK)
    k_idx_f = k_idx.astype(jnp.float32)
    idx_scale = (N_IDX_HEADS ** -0.5) * (IDX_DIM ** -0.5)
    attn_scale = HEAD_DIM ** -0.5
    gather = jax.vmap(lambda table, ids: table[ids])

    def one_block(args):
        qb, qib, wib, qcb = args
        s = jnp.einsum('bqhd,bkd->bqhk', qib.astype(jnp.float32), k_idx_f)
        score = jnp.einsum('bqhk,bqh->bqk', jax.nn.relu(s), wib.astype(jnp.float32) * idx_scale)
        visible = key_chunk[None, :] <= qcb[:, None]
        score = jnp.where(visible[None], score, NEG_INF)
        _, sel = lax.top_k(score, k_top)
        valid = key_chunk[sel] <= qcb[None, :, None]
        kg = gather(k, sel)
        vg = gather(v, sel)
        logits = jnp.einsum('bqhd,bqkd->bqhk', qb, kg).astype(jnp.float32) * attn_scale
        logits = jnp.where(valid[:, :, None, :], logits, NEG_INF)
        p = jax.nn.softmax(logits, axis=-1).astype(vg.dtype)
        return jnp.einsum('bqhk,bqkd->bqhd', p, vg)

    out = lax.map(one_block, (to_blocks(q), to_blocks(q_idx), to_blocks(w_idx), query_chunk))
    return jnp.moveaxis(out, 0, 1).reshape(B, t_pad, N_HEADS_A, HEAD_DIM)[:, :T]

def multiscale_pool(u, pool_w, pool_b, pool_s):
    B, T, C = u.shape
    G = POOL_GROUP_DIM
    uf = u.astype(jnp.float32)
    cs = jnp.concatenate([jnp.zeros((B, 1, C), jnp.float32), jnp.cumsum(uf, axis=1)], axis=1)
    t1 = jnp.arange(1, T + 1, dtype=jnp.float32)
    means = []
    for g, w in enumerate(POOL_WINDOWS):
        csg = cs[..., g * G:(g + 1) * G]
        lag = jnp.concatenate([jnp.zeros((B, w, G), jnp.float32), csg[:, :T + 1 - w]], axis=1)
        cnt = jnp.minimum(t1, float(w))
        means.append((csg[:, 1:] - lag[:, 1:]) / cnt[None, :, None])
    pooled = (jnp.concatenate(means, axis=-1) - uf).astype(u.dtype).reshape(B, T, N_POOL_GROUPS, G)
    mixed = jnp.einsum('btgc,gcd->btgd', pooled, pool_w) + pool_b.reshape(N_POOL_GROUPS, G)
    return mixed.reshape(B, T, C) * pool_s

def hybrid_layer(x, norm_g, w_in, qn_g, kn_g, pool_w, pool_b, pool_s, w_a, w_b, w_out, cos, sin, k_top):
    B, T, _ = x.shape
    h = rms_norm(x, norm_g)
    proj = jnp.einsum('btd,de->bte', h, w_in)
    q, k, v, gate_a, u_b, gate_b, q_idx, k_idx, w_idx, merge = jnp.split(
        proj, np.cumsum(IN_WIDTHS)[:-1].tolist(), axis=-1)
    cos_h, sin_h = cos[:, None, :], sin[:, None, :]
    q = apply_rope(rms_norm(q.reshape(B, T, N_HEADS_A, HEAD_DIM), qn_g), cos_h, sin_h)
    k = apply_rope(rms_norm(k, kn_g), cos, sin)
    q_idx = apply_rope(q_idx.reshape(B, T, N_IDX_HEADS, IDX_DIM), cos_h, sin_h)
    k_idx = apply_rope(k_idx, cos, sin)
    attn = indexer_sparse_attention(q, k, v, q_idx, k_idx, w_idx, k_top).reshape(B, T, D_A)
    y_a = jnp.einsum('bte,ed->btd', attn * jax.nn.silu(gate_a), w_a)
    pooled = multiscale_pool(u_b, pool_w, pool_b, pool_s)
    y_b = jnp.einsum('bte,ed->btd', pooled * jax.nn.silu(gate_b), w_b)
    g_a, g_b = jnp.split(jax.nn.sigmoid(merge), 2, axis=-1)
    return x + jnp.einsum('btd,de->bte', g_a * y_a + g_b * y_b, w_out)

def first_inputs(seed: int = 0) -> dict:
    key = jax.random.key(seed)
    ks = jax.random.split(key, 12)

    def nrm(k, shape, scale):
        return scale * jax.random.normal(k, shape, jnp.float32)

    return {
        'x': nrm(ks[0], (BATCH, SEQ, D_MODEL), 1.0),
        'meta_tokens': nrm(ks[1], (N_META, D_MODEL), 1.0),
        'norm_gain': 1.0 + nrm(ks[2], (DEPTH, D_MODEL), 0.05),
        'w_in': nrm(ks[3], (DEPTH, D_MODEL, D_IN), D_MODEL ** -0.5),
        'q_norm_gain': 1.0 + nrm(ks[4], (DEPTH, HEAD_DIM), 0.05),
        'k_norm_gain': 1.0 + nrm(ks[5], (DEPTH, HEAD_DIM), 0.05),
        'pool_w': nrm(ks[6], (DEPTH, N_POOL_GROUPS, POOL_GROUP_DIM, POOL_GROUP_DIM), POOL_GROUP_DIM ** -0.5),
        'pool_b': nrm(ks[7], (DEPTH, D_B), 0.02),
        'pool_scale': 1.0 + nrm(ks[8], (DEPTH, D_B), 0.1),
        'w_branch_a': nrm(ks[9], (DEPTH, D_A, D_MODEL), D_A ** -0.5),
        'w_branch_b': nrm(ks[10], (DEPTH, D_B, D_MODEL), D_B ** -0.5),
        'w_out': nrm(ks[11], (DEPTH, D_MODEL, D_MODEL), D_MODEL ** -0.5),
    }

def first_block(x, meta_tokens, norm_gain, w_in, q_norm_gain, k_norm_gain, pool_w, pool_b, pool_scale,
              w_branch_a, w_branch_b, w_out):
    B, S, _ = x.shape
    k_top = min(TOPK_MAX, S // 4)
    meta = jnp.broadcast_to(meta_tokens.astype(x.dtype)[None], (B, N_META, D_MODEL))
    h = jnp.concatenate([meta, x], axis=1)
    T = S + N_META
    cos, sin = rope_tables(T, HEAD_DIM)
    for l in range(DEPTH):
        h = hybrid_layer(h, norm_gain[l], w_in[l], q_norm_gain[l], k_norm_gain[l], pool_w[l], pool_b[l],
                         pool_scale[l], w_branch_a[l], w_branch_b[l], w_out[l], cos, sin, k_top)
    return h[:, N_META:]


DEPTH_2 = 1

GRID_W = 64
NA_HEADS = 8
NA_KH_MAX = 8
NA_KW = 16
NA_WIDTH = NA_HEADS * HEAD_DIM
SWA_Q_HEADS = 8
SWA_KV_HEADS = 2
SWA_WINDOW = 128
SWA_BLOCK = 128
SWA_Q_WIDTH = SWA_Q_HEADS * HEAD_DIM
SWA_KV_WIDTH = SWA_KV_HEADS * HEAD_DIM
ROPE_THETA_2 = 500000.0
ROPE_DIM = HEAD_DIM // 4
D_FF = 4 * D_MODEL
IN_WIDTH = 3 * NA_WIDTH + SWA_Q_WIDTH + 2 * SWA_KV_WIDTH + 2 * D_MODEL
IN_SPLITS = [
    NA_WIDTH,
    2 * NA_WIDTH,
    3 * NA_WIDTH,
    3 * NA_WIDTH + SWA_Q_WIDTH,
    3 * NA_WIDTH + SWA_Q_WIDTH + SWA_KV_WIDTH,
    3 * NA_WIDTH + SWA_Q_WIDTH + 2 * SWA_KV_WIDTH,
    3 * NA_WIDTH + SWA_Q_WIDTH + 2 * SWA_KV_WIDTH + D_MODEL,
]
DEEPNORM_ALPHA = (2.0 * DEPTH_2) ** 0.25
DEEPNORM_BETA = (8.0 * DEPTH_2) ** -0.25
LN_EPS = 1e-5
MASK_VALUE = -1e30


def layer_norm(x, g, b):
    xf = x.astype(jnp.float32)
    mu = jnp.mean(xf, axis=-1, keepdims=True)
    xc = xf - mu
    var = jnp.mean(xc * xc, axis=-1, keepdims=True)
    y = xc * lax.rsqrt(var + LN_EPS) * g.astype(jnp.float32) + b.astype(jnp.float32)
    return y.astype(x.dtype)

def partial_rotary(x, pos):
    half = ROPE_DIM // 2
    inv_freq = jnp.power(ROPE_THETA_2, -jnp.arange(0, ROPE_DIM, 2, dtype=jnp.float32) / ROPE_DIM)
    ang = pos.astype(jnp.float32)[:, None] * inv_freq[None, :]
    cos = jnp.cos(ang)[:, None, :]
    sin = jnp.sin(ang)[:, None, :]
    xr = x[..., :ROPE_DIM].astype(jnp.float32)
    x1, x2 = xr[..., :half], xr[..., half:]
    rot = jnp.concatenate([x1 * cos - x2 * sin, x2 * cos + x1 * sin], axis=-1)
    return jnp.concatenate([rot.astype(x.dtype), x[..., ROPE_DIM:]], axis=-1)

def neighbourhood_attention(q, k, v, rpb):
    B, S, H, Dh = q.shape
    rows = S // GRID_W
    kh = min(NA_KH_MAX, rows)
    kw = NA_KW
    qg = q.reshape(B, rows, GRID_W, H, Dh)
    kg = k.reshape(B, rows, GRID_W, H, Dh)
    vg = v.reshape(B, rows, GRID_W, H, Dh)
    cols = jnp.arange(GRID_W)
    col_start = jnp.clip(cols - kw // 2, 0, GRID_W - kw)
    col_idx = col_start[:, None] + jnp.arange(kw)[None, :]
    dc = col_idx - cols[:, None]
    scale = Dh ** -0.5

    def one_row(r):
        rs = jnp.clip(r - kh // 2, 0, rows - kh)
        kr = lax.dynamic_slice_in_dim(kg, rs, kh, axis=1)
        vr = lax.dynamic_slice_in_dim(vg, rs, kh, axis=1)
        kn = kr[:, :, col_idx]
        vn = vr[:, :, col_idx]
        qr = lax.dynamic_index_in_dim(qg, r, axis=1, keepdims=False)
        s = jnp.einsum('bwhd,bkwjhd->bhwkj', qr, kn).astype(jnp.float32) * scale
        dr = rs + jnp.arange(kh) - r
        bias = rpb[:, (dr + NA_KH_MAX - 1)[None, :, None], (dc + kw - 1)[:, None, :]]
        s = s + bias.astype(jnp.float32)[None]
        p = jax.nn.softmax(s.reshape(B, H, GRID_W, kh * kw), axis=-1)
        p = p.reshape(B, H, GRID_W, kh, kw).astype(v.dtype)
        return jnp.einsum('bhwkj,bkwjhd->bwhd', p, vn)

    out = lax.map(one_row, jnp.arange(rows))
    return jnp.moveaxis(out, 0, 1).reshape(B, S, H * Dh)

def windowed_gqa_with_sink(q, k, v, sink):
    B, S, Hq, Dh = q.shape
    G = k.shape[2]
    rep = Hq // G
    blk = SWA_BLOCK
    nb = S // blk
    qb = q.reshape(B, nb, blk, G, rep, Dh)
    pad = ((0, 0), (blk, blk), (0, 0), (0, 0))
    kp = jnp.pad(k, pad).reshape(B, nb + 2, blk, G, Dh)
    vp = jnp.pad(v, pad).reshape(B, nb + 2, blk, G, Dh)
    kb = jnp.concatenate([kp[:, :-2], kp[:, 1:-1], kp[:, 2:]], axis=2)
    vb = jnp.concatenate([vp[:, :-2], vp[:, 1:-1], vp[:, 2:]], axis=2)
    s = jnp.einsum('bnqgrd,bnkgd->bngrqk', qb, kb).astype(jnp.float32) * (Dh ** -0.5)
    qpos = jnp.arange(nb)[:, None] * blk + jnp.arange(blk)[None, :]
    kpos = jnp.arange(nb)[:, None] * blk - blk + jnp.arange(3 * blk)[None, :]
    rel = kpos[:, None, :] - qpos[:, :, None]
    valid = (jnp.abs(rel) <= SWA_WINDOW) & (kpos[:, None, :] >= 0) & (kpos[:, None, :] < S)
    s = jnp.where(valid[None, :, None, None], s, MASK_VALUE)
    sink_l = sink.astype(jnp.float32).reshape(1, 1, G, rep, 1, 1)
    m = jnp.maximum(jnp.max(s, axis=-1, keepdims=True), sink_l)
    e = jnp.exp(s - m)
    p = e / (jnp.sum(e, axis=-1, keepdims=True) + jnp.exp(sink_l - m))
    o = jnp.einsum('bngrqk,bnkgd->bnqgrd', p.astype(v.dtype), vb)
    return o.reshape(B, S, Hq * Dh)

def second_inputs(seed: int = 0) -> dict:
    key = jax.random.key(seed)
    ks = jax.random.split(key, 24)
    f32 = jnp.float32
    beta = DEEPNORM_BETA

    def nrm(k, shape, scale):
        return jax.random.normal(k, shape, f32) * scale

    col_scale = jnp.concatenate([
        jnp.ones((2 * NA_WIDTH,), f32), jnp.full((NA_WIDTH,), beta, f32),
        jnp.ones((SWA_Q_WIDTH + SWA_KV_WIDTH,), f32), jnp.full((SWA_KV_WIDTH,), beta, f32),
        jnp.ones((2 * D_MODEL,), f32)])
    w_in = nrm(ks[1], (DEPTH_2, D_MODEL, IN_WIDTH), D_MODEL ** -0.5) * col_scale
    return {
        "x": jax.random.normal(ks[0], (BATCH, SEQ, D_MODEL), f32),
        "ln0_g": 1.0 + nrm(ks[2], (D_MODEL,), 0.05),
        "ln0_b": nrm(ks[3], (D_MODEL,), 0.02),
        "w_in": w_in,
        "b_in": nrm(ks[4], (DEPTH_2, IN_WIDTH), 0.02),
        "na_rpb": nrm(ks[5], (DEPTH_2, NA_HEADS, 2 * NA_KH_MAX - 1, 2 * NA_KW - 1), 0.1),
        "swa_sink": nrm(ks[6], (DEPTH_2, SWA_Q_HEADS), 0.5),
        "w_branch_na": nrm(ks[7], (DEPTH_2, NA_WIDTH, D_MODEL), NA_WIDTH ** -0.5 * beta),
        "w_branch_swa": nrm(ks[8], (DEPTH_2, SWA_Q_WIDTH, D_MODEL), SWA_Q_WIDTH ** -0.5 * beta),
        "w_out": nrm(ks[9], (DEPTH_2, D_MODEL, D_MODEL), D_MODEL ** -0.5 * beta),
        "b_out": nrm(ks[10], (DEPTH_2, D_MODEL), 0.02),
        "ln1_g": 1.0 + nrm(ks[11], (DEPTH_2, D_MODEL), 0.05),
        "ln1_b": nrm(ks[12], (DEPTH_2, D_MODEL), 0.02),
        "w_ff1": nrm(ks[13], (DEPTH_2, D_MODEL, D_FF), D_MODEL ** -0.5 * beta),
        "b_ff1": nrm(ks[14], (DEPTH_2, D_FF), 0.02),
        "w_ff2": nrm(ks[15], (DEPTH_2, D_FF, D_MODEL), D_FF ** -0.5 * beta),
        "b_ff2": nrm(ks[16], (DEPTH_2, D_MODEL), 0.02),
        "ln2_g": 1.0 + nrm(ks[17], (DEPTH_2, D_MODEL), 0.05),
        "ln2_b": nrm(ks[18], (DEPTH_2, D_MODEL), 0.02),
    }

def second_block(x, ln0_g, ln0_b, w_in, b_in, na_rpb, swa_sink, w_branch_na, w_branch_swa,
              w_out, b_out, ln1_g, ln1_b, w_ff1, b_ff1, w_ff2, b_ff2, ln2_g, ln2_b):
    B, S, _ = x.shape
    pos = jnp.arange(S)
    h = layer_norm(x, ln0_g, ln0_b)
    for l in range(DEPTH_2):
        proj = h @ w_in[l] + b_in[l]
        qa, ka, va, qb, kb, vb, ga, gb = jnp.split(proj, IN_SPLITS, axis=-1)
        qa = qa.reshape(B, S, NA_HEADS, HEAD_DIM)
        ka = ka.reshape(B, S, NA_HEADS, HEAD_DIM)
        va = va.reshape(B, S, NA_HEADS, HEAD_DIM)
        qb = partial_rotary(qb.reshape(B, S, SWA_Q_HEADS, HEAD_DIM), pos)
        kb = partial_rotary(kb.reshape(B, S, SWA_KV_HEADS, HEAD_DIM), pos)
        vb = vb.reshape(B, S, SWA_KV_HEADS, HEAD_DIM)
        y_na = neighbourhood_attention(qa, ka, va, na_rpb[l]) @ w_branch_na[l]
        y_swa = windowed_gqa_with_sink(qb, kb, vb, swa_sink[l]) @ w_branch_swa[l]
        mixed = jax.nn.sigmoid(ga) * y_na + jax.nn.sigmoid(gb) * y_swa
        attn_out = mixed @ w_out[l] + b_out[l]
        h = layer_norm(DEEPNORM_ALPHA * h + attn_out, ln1_g[l], ln1_b[l])
        u = jnp.square(jax.nn.relu(h @ w_ff1[l] + b_ff1[l]))
        ffn_out = u @ w_ff2[l] + b_ff2[l]
        h = layer_norm(DEEPNORM_ALPHA * h + ffn_out, ln2_g[l], ln2_b[l])
    return h


def setup_inputs(seed=0):
    out = dict(first_inputs(seed))
    for name, value in second_inputs(seed + 1).items():
        if name != "x":
            out[name + "_2"] = value
    return out


def reference(
    x, meta_tokens, norm_gain, w_in, q_norm_gain, k_norm_gain, pool_w, pool_b, pool_scale,
    w_branch_a, w_branch_b, w_out, ln0_g_2, ln0_b_2, w_in_2, b_in_2, na_rpb_2, swa_sink_2,
    w_branch_na_2, w_branch_swa_2, w_out_2, b_out_2, ln1_g_2, ln1_b_2, w_ff1_2, b_ff1_2,
    w_ff2_2, b_ff2_2, ln2_g_2, ln2_b_2,
):
    x = first_block(
        x, meta_tokens, norm_gain, w_in, q_norm_gain, k_norm_gain, pool_w, pool_b, pool_scale,
        w_branch_a, w_branch_b, w_out,
    )
    return second_block(
        x, ln0_g_2, ln0_b_2, w_in_2, b_in_2, na_rpb_2, swa_sink_2, w_branch_na_2,
        w_branch_swa_2, w_out_2, b_out_2, ln1_g_2, ln1_b_2, w_ff1_2, b_ff1_2, w_ff2_2, b_ff2_2,
        ln2_g_2, ln2_b_2,
    )


_drawn_inputs = setup_inputs


def setup_inputs(seed=0):
    import zlib

    import numpy as np

    out = dict(_drawn_inputs(seed))
    spreads = {}
    factors = {'meta_tokens': 3.588,
     'q_norm_gain': 8.0,
     'k_norm_gain': 8.0,
     'pool_b': 6.192,
     'ln0_b_2': 2.797,
     'b_in_2': 8.0,
     'na_rpb_2': 8.0,
     'swa_sink_2': 8.0,
     'w_branch_na_2': 3.879,
     'w_branch_swa_2': 4.924,
     'w_out_2': 3.046,
     'b_out_2': 3.352,
     'ln1_b_2': 2.782,
     'b_ff1_2': 7.003,
     'b_ff2_2': 3.33,
     'ln2_b_2': 2.794}
    for name, (base, spread) in spreads.items():
        noise = np.random.default_rng([zlib.crc32(name.encode()), seed]).standard_normal(out[name].shape)
        drawn = base * np.exp(spread * noise) if base else spread * noise
        out[name] = jnp.asarray(drawn.astype(out[name].dtype))
    for name, factor in factors.items():
        out[name] = (out[name] * factor).astype(out[name].dtype)
    return out
```

```python
from contextlib import ExitStack

import numpy as np
import concourse.bass as bass
from concourse import mybir

F32 = mybir.dt.float32
F32R = mybir.dt.float32r
ALU = mybir.AluOpType
ACT = mybir.ActivationFunctionType
P = 128
D = 1024
KC = D // P
SEQ = 1024
META = 16
T = SEQ + META
TP = 1044
PIECE1 = TP // 3
DEPTH = 2
HEADS, HD = 8, 64
CHUNK, TOPK = 64, 256
NQ = SEQ // P
WINDOWS = (2, 4, 8, 16)
EPS, LN_EPS = 1e-6, 1e-5
NEG = -1e30
TAKEN = -3e38
ALPHA = 2.0 ** 0.25
FF = 4 * D
RAW = 2
GRID = 64
BANK = 512
SCALE = HD ** -0.5
IDX_SCALE = (HEADS ** -0.5) * (HD ** -0.5)
Q0, K0, GA0, U0, GB0, QI0, KI0, MG0 = 0, 512, 640, 1152, 1664, 2176, 2688, 2760
NAQ0, NAK0, NAV0, SWQ0, SWK0, SWV0, MG2 = 0, 512, 1024, 1536, 2048, 2176, 2304


def visible(j):
    return META + P * (j + 1)


SCORE_AT = {}
_at = 0
for _j in range(1, NQ):
    SCORE_AT[_j] = _at
    _at += visible(_j)
SCORE_COLS = _at


class Signals:

    def __init__(self, ctx, nc, known):
        self.ctx, self.nc, self.known = ctx, nc, known
        self.sems, self.count, self.seen = {}, {}, {}

    def sem(self, name):
        if name not in self.sems:
            self.sems[name] = self.ctx.enter_context(self.nc.semaphore(name))
            self.count[name] = 0
        return self.sems[name]

    def inc(self, name, *key, by=1):
        s = self.sem(name)
        self.count[name] += by
        assert (name, *key) not in self.seen, (name, key)
        self.seen[(name, *key)] = self.count[name]
        return s, by

    def dma(self, name, *key):
        return self.inc(name, *key, by=16)

    def at(self, name, *key):
        if self.known is not None:
            return self.sem(name), self.known[(name, *key)]
        return self.sem(name), 1


def program(nc, a, known):
    ctx = ExitStack()
    with ctx:
        S = Signals(ctx, nc, known)

        def sb(name, shape, dt=F32, into=ctx):
            return into.enter_context(nc.sbuf_tensor(name, shape, dt))

        ident = sb("ident", [P, P])
        rot1 = sb("rot1", [P, P])
        rot2 = sb("rot2", [P, P])
        headmean = sb("headmean", [P, P])
        allmean = sb("allmean", [P, P])
        gain = sb("gain", [P, DEPTH, KC])
        qk_gain = sb("qk_gain", [P, DEPTH, 2])
        pool_b = sb("pool_b", [P, DEPTH, 4])
        pool_s = sb("pool_s", [P, DEPTH, 4])
        pool_bs = sb("pool_bs", [P, DEPTH, 4])
        edge = sb("edge", [P, 4, 16])
        ln_g = sb("ln_g", [P, 3, KC])
        ln_b = sb("ln_b", [P, 3, KC])
        b_in2 = sb("b_in2", [P, 34])
        b_ff1 = sb("b_ff1", [P, FF // P])
        b_o = sb("b_o", [P, 2, KC])
        sink = sb("sink", [P, 2, HEADS])
        top8 = sb("top8", [P, NQ, 8])
        widx = sb("widx", [P, NQ, HEADS])
        rowmax = sb("rowmax", [P, 2])
        negmax = sb("negmax", [P, 4])
        rowsum = sb("rowsum", [P, 4])
        sinkexp = sb("sinkexp", [P, 4])
        rowinv = sb("rowinv", [P, 4])
        zeros = sb("zeros", [2, 64])
        raw = sb("raw", [P, RAW, KC * P])
        wsp = sb("wsp", [P, 2, 2, KC * P], F32R)
        tm = sb("tm", [P, 4, TP])
        H = sb("H", [P, 2, KC, TP], F32R)
        X = sb("X", [P, KC, TP])
        QS = sb("QS", [P, KC, TP], F32R)
        KK = sb("KK", [P, 2, TP], F32R)
        V = sb("V", [P, 9, HD])
        SC = sb("SC", [P, SCORE_COLS])

        def over(first, names):
            out, at = [], first
            for name, shape, dt in names:
                at = -(-at // 32) * 32
                out.append(nc.alloc_sbuf_tensor_at(name, shape, dt, offset=at))
                at += 4 * int(np.prod(shape[1:]))
            return out

        x_at, chunk = nc.sbuf_base - 4 * (2 * KC * TP + 2 * TP + 9 * HD + SCORE_COLS), 4 * TP
        z_at = x_at + KC * chunk
        QIPB, = over(x_at, [("QIPB", [P, KC, TP], F32R)])
        trig1, pw = over(x_at + 5 * chunk, [("trig1", [P, 2, TP], F32), ("pw", [P, 4, P], F32)])
        Lb, Pb, PT, Ob, mask0 = over(x_at, [("Lb", [P, 2, 1040], F32), ("Pb", [P, 2, 9 * P], F32),
                                            ("PT", [P, 2, 9, P], F32), ("Ob", [P, 2, P], F32),
                                            ("mask0", [P, visible(0)], F32)])
        Q2, K2, V2, bias_e, bias_i, colmask, rowmask, swmask, trig2 = over(z_at, [
            ("Q2", [P, 2, SEQ], F32R), ("K2", [P, 2, 2, SEQ], F32R), ("V2", [P, NQ, P], F32),
            ("bias_e", [P, 2, 14, GRID], F32), ("bias_i", [P, 2, 9, GRID], F32), ("colmask", [P, 14, GRID], F32),
            ("rowmask", [P, 9, GRID], F32), ("swmask", [P, 3 * P], F32), ("trig2", [P, 2, SEQ], F32)])
        sb("z_rest", [P, (2 * KC * SEQ - KC * TP - 2 * TP - 9 * HD - SCORE_COLS)])
        SP2, = over(z_at, [("SP2", [P, 2, KC, SEQ], F32R)])

        big = [ctx.enter_context(nc.psum_tensor(f"big{i}", [P, 3 * BANK], F32)) for i in range(2)]
        small = [ctx.enter_context(nc.psum_tensor(f"small{i}", [P, BANK], F32)) for i in range(2)]

        def dram(name, shape):
            return nc.dram_tensor(name, shape, F32, kind="Internal").ap()

        xT_d = dram("xT_scratch", [KC, P, TP])
        ga_d = dram("gate_a_scratch", [KC, P, TP])
        gb_d = dram("gate_b_scratch", [KC, P, TP])
        sg_d = dram("silu_scratch", [4, P, TP])
        at_d = dram("attention_scratch", [KC, P, SEQ])
        rpb_d = dram("rpb_scratch", [64 + HEADS * 15 * 31 + 64])
        band_d = dram("band_scratch", [HEADS, 15, GRID, GRID])

        tm_flat = [tm[:, i, :] for i in range(4)]

        def ps3(s, rows=slice(0, P)):
            return big[s][rows, :].rearrange("p (b n) -> p b n", b=3)[:, :, 0:PIECE1]

        def v3(ap):
            return ap.rearrange("p (b n) -> p b n", b=3)

        def ps2(s, rows=slice(0, P)):
            return big[s][rows, 0:SEQ]

        pieces1 = [(i * BANK, i * PIECE1, PIECE1) for i in range(3)]
        pieces2 = [(i * BANK, i * BANK, BANK) for i in range(2)]

        loads = []

        def wsrc(w, l, col, n, rows):
            return w[l][:, col:col + n].rearrange("(k p) n -> p k n", p=P), n, rows

        for l in range(DEPTH):
            for c in range(4):
                loads.append((("q", l, c), *wsrc(a["w_in"], l, Q0 + c * P, P, 8)))
            loads.append((("ki", l), *wsrc(a["w_in"], l, KI0, 72, 8)))
            for c in range(4):
                loads.append((("qi", l, c), *wsrc(a["w_in"], l, QI0 + c * P, P, 8)))
            loads.append((("kv", l), *wsrc(a["w_in"], l, K0, P, 8)))
            for g in range(4):
                loads.append((("u", l, g), *wsrc(a["w_in"], l, U0 + g * P, P, 8)))
                loads.append((("gateb", l, g), *wsrc(a["w_in"], l, GB0 + g * P, P, 8)))
            for c in range(4):
                loads.append((("gatea", l, c), *wsrc(a["w_in"], l, GA0 + c * P, P, 8)))
            for m in range(8):
                loads.append((("mb", l, m), *wsrc(a["w_in"], l, MG0 + D + m * P, P, 8)))
                loads.append((("yb", l, m), *wsrc(a["w_branch_b"], l, m * P, P, 4)))
            for m in range(8):
                loads.append((("ma", l, m), *wsrc(a["w_in"], l, MG0 + m * P, P, 8)))
            for m in range(8):
                loads.append((("ya", l, m), *wsrc(a["w_branch_a"], l, m * P, P, 4)))
            for m in range(8):
                loads.append((("out", l, m), *wsrc(a["w_out"], l, m * P, P, 8)))
        w2 = a["w_in_2"]
        for m in range(16):
            loads.append((("m2", m), *wsrc(w2, 0, MG2 + m * P, P, 8)))
        for c in range(4):
            for what, col in (("naq", NAQ0), ("nak", NAK0), ("nav", NAV0)):
                loads.append(((what, c), *wsrc(w2, 0, col + c * P, P, 8)))
        for what, col in (("swk", SWK0), ("swv", SWV0)):
            loads.append(((what, 0), *wsrc(w2, 0, col, P, 8)))
        for c in range(4):
            loads.append((("swq", c), *wsrc(w2, 0, SWQ0 + c * P, P, 8)))
        for m in range(8):
            loads.append((("y1", m), *wsrc(a["w_branch_na_2"], 0, m * P, P, 4)))
            loads.append((("y2", m), *wsrc(a["w_branch_swa_2"], 0, m * P, P, 4)))
        for m in range(8):
            loads.append((("out2", m), *wsrc(a["w_out_2"], 0, m * P, P, 8)))
        for f in range(4):
            for m in range(8):
                loads.append((("ff1", f, m), *wsrc(a["w_ff1_2"], 0, (8 * f + m) * P, P, 8)))
            for m in range(8):
                src = a["w_ff2_2"][0][f * D:(f + 1) * D, m * P:(m + 1) * P].rearrange("(k p) n -> p k n", p=P)
                loads.append((("ff2", f, m), src, P, 8))
        nload = {job: n for n, (job, *_) in enumerate(loads)}

        def units_first(l):
            for c in range(4):
                for j in [-1, *range(NQ)]:
                    for hh in range(2):
                        n = META if j < 0 else visible(j)
                        q0 = 0 if j < 0 else META + P * j
                        if j <= 0:
                            mask = mask0[:, 0:n] if j == 0 else mask0[:, 0:META]
                        else:
                            mask = SC[:, SCORE_AT[j]:SCORE_AT[j] + n]
                        qa = QS[:, 2 * c + hh, q0:q0 + P]
                        keys = [(o, min(BANK, n - o)) for o in range(0, n, BANK)]
                        kparts = [[(o, w, KK[:, part, o:o + w]) for o, w in keys] for part in range(2)]
                        kts = [(kt, min(P, n - kt * P), V[0:min(P, n - kt * P), kt, :])
                               for kt in range(-(-n // P))]
                        yield dict(block=("a", l), c=c, hh=hh, n=n, q=qa, k=kparts, mask=mask, kts=kts,
                                   sink=None, q0=q0, nq=META if j < 0 else P, h=2 * c + hh)

        def na_rows(t):
            r = 2 * t
            start = [min(max(x - 4, 0), 8) for x in (r, r + 1)]
            return start[0], start[1] + 8 - start[0]

        def units_na():
            for c in range(4):
                for t in range(NQ):
                    for hh in range(2):
                        r0, rows = na_rows(t)
                        n, k0 = rows * GRID, r0 * GRID
                        i0 = r0 - 2 * t + 7
                        m = bias_i[:, hh, :, :] if rows == 9 else bias_e[:, hh, i0 - 1:i0 - 1 + rows, :]
                        m = m.rearrange("p r c -> p (r c)")
                        keys = [(o, min(BANK, n - o)) for o in range(0, n, BANK)]
                        kparts = [[(o, w, K2[:, hh, part, k0 + o:k0 + o + w]) for o, w in keys] for part in range(2)]
                        kts = [(kt, min(P, n - kt * P), V2[0:min(P, n - kt * P), k0 // P + kt, hh * HD:hh * HD + HD])
                               for kt in range(-(-n // P))]
                        yield dict(block=("n",), c=c, hh=hh, n=n, q=Q2[:, hh, t * P:t * P + P], k=kparts, mask=m,
                                   kts=kts, sink=None, q0=t * P, nq=P, h=2 * c + hh, t=t)

        def units_swa():
            for c in range(4):
                for t in range(NQ):
                    for hh in range(2):
                        lo, hi = max(t - 1, 0), min(t + 2, NQ)
                        n, g = (hi - lo) * P, c // 2
                        kparts = [[(0, n, K2[:, g, part, lo * P:hi * P])] for part in range(2)]
                        kts = [(kt, P, V2[:, lo + kt, g * HD:g * HD + HD]) for kt in range(hi - lo)]
                        m0 = (lo - t + 1) * P
                        yield dict(block=("s",), c=c, hh=hh, n=n, q=Q2[:, hh, t * P:t * P + P], k=kparts,
                                   mask=swmask[:, m0:m0 + n], kts=kts, sink=2 * c + hh, q0=t * P, nq=P,
                                   h=2 * c + hh, t=t)

        phases = {("a", 0): list(units_first(0)), ("a", 1): list(units_first(1)),
                  ("n",): list(units_na()), ("s",): list(units_swa())}
        nunit = 0
        for units in phases.values():
            for u in units:
                u["i"] = nunit
                nunit += 1
        score_units = [(c, hh, j) for c in range(4) for hh in range(2) for j in range(1, NQ)]

        def bank_owner(u, kt):
            return "act" if kt // 4 == 1 else "dve"

        def halves_even(buf):
            return lambda part, k: buf[:, 2 * k + part, :]

        def moved_events(u):
            who = {bank_owner(u, kt) for kt, _, _ in u["kts"]}
            return [(f"moved_{e}", u["i"]) for e in sorted(who)]

        def moves(u, engine):
            out = []
            for bank in range(3):
                kts = [k for k in u["kts"] if k[0] // 4 == bank and bank_owner(u, k[0]) == engine]
                full = [k[0] for k in kts if k[1] == P]
                if full:
                    out.append((full[0], len(full), P))
                out += [(k[0], 1, k[1]) for k in kts if k[1] < P]
            return out

        psum_of = {}

        block = ctx.enter_context(nc.Block())

        @block.sync
        def _(sp):
            consts = [(ident[:], a["c_ident"]), (rot1[:], a["c_rot1"]), (rot2[:], a["c_rot2"]),
                      (headmean[:], a["c_headmean"]), (allmean[:], a["c_allmean"]),
                      (edge[:], a["c_edge"]),
                      (gain[:], a["norm_gain"].rearrange("l (k p) -> p l k", p=P)),
                      (pool_b[:], a["pool_b"].rearrange("l (k p) -> p l k", p=P)),
                      (pool_s[:], a["pool_scale"].rearrange("l (k p) -> p l k", p=P)),
                      (b_in2[:], a["b_in_2"][0].rearrange("(k p) -> p k", p=P)),
                      (b_ff1[:], a["b_ff1_2"][0].rearrange("(k p) -> p k", p=P)),
                      (b_o[:, 0, :], a["b_out_2"][0].rearrange("(k p) -> p k", p=P)),
                      (b_o[:, 1, :], a["b_ff2_2"][0].rearrange("(k p) -> p k", p=P)),
                      (sink[:, 0, :], bass.AP(a["swa_sink_2"].tensor, 0, [[0, P], [1, HEADS]]))]
            for i, name in enumerate(("ln0", "ln1", "ln2")):
                for dst, part in ((ln_g, "g"), (ln_b, "b")):
                    src = a[f"{name}_{part}_2"]
                    src = src if i == 0 else src[0]
                    consts.append((dst[:, i, :], src.rearrange("(k p) -> p k", p=P)))
            for half in range(2):
                for which, name in enumerate(("q_norm_gain", "k_norm_gain")):
                    consts.append((qk_gain[half * HD:(half + 1) * HD, :, which], a[name].rearrange("l d -> d l")))
            for i, (dst, src) in enumerate(consts):
                sp.dma_start(dst, src, allow_slow_non_contiguous=True).then_inc(*S.dma("constants", i))
            sp.wait_ge(*S.at("constants", len(consts) - 1))
            sp.nop().then_inc(*S.inc("constants_here"))
            for n, (job, src, cols, rows) in enumerate(loads):
                if n >= RAW:
                    sp.wait_ge(*S.at("weight_lo", n - RAW))
                sp.dma_start(raw[:, n % RAW, :].rearrange("p (k n) -> p k n", k=KC)[:, 0:rows, 0:cols], src)\
                    .then_inc(*S.dma(f"weights{n % RAW}", n))
            sp.wait_ge(*S.at("output0", 6))
            sp.wait_ge(*S.at("output1", 7))

        @block.tensor
        def _(pe):
            free = {0: None, 1: None}
            turn = [0]

            def claim(key, emptied_by):
                s = psum_of[key] = turn[0] % 2
                turn[0] += 1
                if free[s] is not None:
                    for e in free[s]:
                        pe.wait_ge(*S.at(*e))
                free[s] = emptied_by
                return s

            def project(job, rhs, pieces, emptied_by):
                n = nload[job]
                _, _, cols, rows = loads[n]
                s = claim(job, emptied_by)
                pe.wait_ge(*S.at("weight_lo", n))
                w = [wsp[:, n % 2, part, :].rearrange("p (k n) -> p k n", k=KC) for part in range(2)]
                mm = None
                for k in range(rows):
                    for i, (wp, xp) in enumerate(((0, 0), (0, 1), (1, 0))):
                        for o, t0, width in pieces:
                            mm = pe.matmul(big[s][0:cols, o:o + width], w[wp][:, k, 0:cols],
                                           rhs(xp, k)[:, t0:t0 + width],
                                           start=(k == 0 and i == 0), stop=(k == rows - 1 and i == 2))
                mm.then_inc(*S.inc("projected", job))

            def plain(name, key, lhsT, rhs_list, pieces, emptied_by, waits, rows=P):
                s = claim((name, *key), emptied_by)
                mm = None
                for i, rhs in enumerate(rhs_list):
                    pe.wait_ge(*S.at(*waits[i]))
                    for o, t0, width in pieces:
                        mm = pe.matmul(big[s][0:rows, o:o + width], lhsT, rhs[:, t0:t0 + width],
                                       start=(i == 0), stop=(i == len(rhs_list) - 1))
                    if i < len(rhs_list) - 1:
                        mm.then_inc(*S.inc(name + "_part", *key, i))
                mm.then_inc(*S.inc(name, *key))

            def attention(units):
                def scores(u):
                    if u["i"] >= 1 and u is not units[0]:
                        pe.wait_ge(*S.at("masked", u["i"] - 1))
                    mm = None
                    for part in range(2):
                        for o, w, k in u["k"][part]:
                            mm = pe.matmul(big[0][:, o:o + w], u["q"], k, start=(part == 0), stop=(part == 1))
                    mm.then_inc(*S.inc("logits", u["i"]))

                def transposes(u, prev):
                    pe.wait_ge(*S.at("exped", u["i"]))
                    if prev is not None:
                        for e in moved_events(prev):
                            pe.wait_ge(*S.at(*e))
                    for kt, rows, _ in u["kts"]:
                        mm = pe.transpose(big[1][:, kt * P:(kt + 1) * P], Pb[:, u["i"] % 2, kt * P:(kt + 1) * P],
                                          ident[:])
                    mm.then_inc(*S.inc("turned", u["i"]))

                def values(u, index):
                    for e in moved_events(u):
                        pe.wait_ge(*S.at(*e))
                    if index >= 2:
                        pe.wait_ge(*S.at("normed_out", u["i"] - 2))
                    if index >= 3 and u["hh"] == 1:
                        pe.wait_ge(*S.at("gated", u["i"] - 3))
                    for i, (kt, rows, v) in enumerate(u["kts"]):
                        mm = pe.matmul(small[u["hh"]][:, 0:HD], PT[0:rows, u["i"] % 2, kt, :], v,
                                       start=(i == 0), stop=(i == len(u["kts"]) - 1))
                    mm.then_inc(*S.inc("weighted", u["i"]))

                def turn_back(u0, u1, pair):
                    pe.wait_ge(*S.at("normed_out", u1["i"]))
                    pe.transpose(small[1][:, P:2 * P], Ob[:, pair % 2, :], ident[:])\
                        .then_inc(*S.inc("out_turned", u0["i"]))

                if units[0]["i"] > 0:
                    pe.wait_ge(*S.at("gated", units[0]["i"] - 2))
                for s in range(2):
                    for e in free[s] or []:
                        pe.wait_ge(*S.at(*e))
                for index in range(len(units) + 3):
                    if index < len(units):
                        scores(units[index])
                    if 1 <= index <= len(units):
                        transposes(units[index - 1], units[index - 2] if index >= 2 else None)
                    if index >= 3 and (index - 3) % 2 == 1:
                        turn_back(units[index - 4], units[index - 3], (index - 3) // 2)
                    if 2 <= index <= len(units) + 1:
                        values(units[index - 2], index - 2)
                last = units[-1]
                free[0] = [("masked", last["i"])]
                free[1] = moved_events(last)

            pe.wait_ge(*S.at("constants_here"))
            for j in range(NQ + 1):
                s = claim(("x", j), [("x_turned", j)])
                pe.wait_ge(*S.at(f"x_in{j % 2}", j))
                rows = META if j == 0 else P
                for c in range(KC):
                    mm = pe.transpose(big[s][:, c * P:c * P + rows], tm[0:rows, j % 2, c * P:(c + 1) * P],
                                      ident[0:rows, 0:rows])
                mm.then_inc(*S.inc("x_transposed", j))

            hi_lo = lambda buf: (lambda part, k: buf[:, part, k, :])
            halves = lambda buf: (lambda part, k: buf[:, 4 * part + k, :])
            for l in range(DEPTH):
                plain("mean_square", (l,), allmean[:], [tm[:, c % 2, :] for c in range(KC)], pieces1,
                      [("variance", "rms", l)], [("squared", "rms", l, c) for c in range(KC)])
                pe.wait_ge(*S.at("normed_lo", "rms", l, KC - 1))

                def head_norm_and_rotate(key, y, rows, sq):
                    if sq is not None:
                        plain("head_square", key, headmean[0:rows, 0:rows], [sq], pieces1,
                              [("variance", "head", *key)], [("head_squared", *key)], rows)
                    plain("rotated", key, rot1[0:rows, 0:rows], [y], pieces1, [("rot_times_sin", *key)],
                          [("raw_copied", *key)], rows)

                sc4 = [SC[:, i * TP:(i + 1) * TP] for i in range(4)]
                for c in range(5):
                    if c < 4:
                        project(("q", l, c), hi_lo(H), pieces1, [("raw_copied", "q", l, c)])
                    if c >= 1:
                        head_norm_and_rotate(("q", l, c - 1), sc4[2 * ((c - 1) % 2) + 1], P, sc4[2 * ((c - 1) % 2)])
                project(("ki", l), hi_lo(H), pieces1, [("w_copied", l)])
                plain("rotated", ("ki", l), rot1[0:HD, 0:HD], [tm[0:HD, 3, :]], pieces1,
                      [("rot_times_sin", "ki", l)], [("raw_copied", "ki", l)], HD)
                s = claim(("w", l), [("w_ready", l)])
                pe.wait_ge(*S.at("w_copied", l))
                for j in range(1, NQ):
                    mm = pe.transpose(big[s][:, j * 8:(j + 1) * 8], tm[HD:HD + 8, 3, META + j * P:META + (j + 1) * P],
                                      ident[HD:HD + 8, HD:HD + 8])
                mm.then_inc(*S.inc("w_turned", l))
                for c in range(4):
                    project(("qi", l, c), hi_lo(H), pieces1, [("raw_copied", "qi", l, c)])
                    plain("rotated", ("qi", l, c), rot1[:], [tm[:, 3, :]], pieces1,
                          [("rot_times_sin", "qi", l, c)], [("raw_copied", "qi", l, c)])
                    pe.wait_ge(*S.at("q_stacked", "qi", l, c))
                    pe.wait_ge(*S.at("k_split", "ki", l))
                    for hh in range(2):
                        for j in range(1, NQ):
                            n = visible(j)
                            s = claim(("index", l, c, hh, j), [("relued", l, c, hh, j)])
                            for part in range(2):
                                for o in range(0, n, BANK):
                                    w = min(BANK, n - o)
                                    mm = pe.matmul(big[s][:, o:o + w],
                                                   QIPB[:, 2 * (c % 2) + hh, META + j * P:META + (j + 1) * P],
                                                   KK[:, part, o:o + w], start=(part == 0), stop=(part == 1))
                            mm.then_inc(*S.inc("index_scores", l, c, hh, j))
                project(("kv", l), hi_lo(H), pieces1, [("v_copied", l)])
                head_norm_and_rotate(("k", l), tm[0:HD, 3, :], HD, tm[0:HD, 0, :])
                s = claim(("v", l), [("v_ready", l)])
                pe.wait_ge(*S.at("v_copied", l))
                for kt in range(9):
                    rows = min(P, T - kt * P)
                    mm = pe.transpose(big[s][0:rows, kt * HD:(kt + 1) * HD], tm[HD:P, 3, kt * P:kt * P + rows],
                                      ident[HD:P, HD:P])
                mm.then_inc(*S.inc("v_turned", l))
                for g in range(4):
                    project(("u", l, g), hi_lo(H), pieces1, [("u_copied", l, g)])
                    project(("gateb", l, g), hi_lo(H), pieces1, [("gateb_silu", l, g)])
                    pe.wait_ge(*S.at("pool_weights", l))
                    plain("pool_mixed", (l, g), pw[:, g, :], [tm[:, 0, :]], pieces1, [("pool_scaled", l, g)],
                          [("pooled", l, g)])
                for c in range(4):
                    project(("gatea", l, c), hi_lo(H), pieces1, [("gatea_silu", l, c)])
                for m in range(8):
                    project(("mb", l, m), hi_lo(H), pieces1, [("mb_sigmoid", l, m)])
                    if m == 0:
                        pe.wait_ge(*S.at("pool_lo", l, 3))
                    project(("yb", l, m), halves(QIPB), pieces1, [("yb_copied", l, m)])
                for m in range(8):
                    project(("ma", l, m), hi_lo(H), pieces1, [("ma_sigmoid", l, m)])
                pe.wait_ge(*S.at("q_stacked", "q", l, 3))
                pe.wait_ge(*S.at("k_split", "k", l))
                pe.wait_ge(*S.at("v_ready", l))
                attention(phases[("a", l)])
                pe.wait_ge(*S.at("attn_lo", l, 3))
                for m in range(8):
                    project(("ya", l, m), halves_even(QS), pieces1, [("mix_gated", l, m)])
                pe.wait_ge(*S.at("mix_lo", l, 7))
                for m in range(8):
                    project(("out", l, m), hi_lo(H), pieces1, [("residual", l, m)])

            ln_inputs = [lambda c: ("residual", DEPTH - 1, c), lambda c: ("residual2", c), lambda c: ("residual3", 3, c)]

            def layer_norm(i, x):
                plain("mean", (i,), allmean[:], [x(c) for c in range(KC)], pieces2, [("centered", i, KC - 1)],
                      [ln_inputs[i](c) for c in range(KC)])
                plain("mean_square", ("ln", i), allmean[:], [tm[:, c % 2, :] for c in range(KC)], pieces2,
                      [("variance", "ln", i)], [("squared", "ln", i, c) for c in range(KC)])

            X0 = lambda c: X[:, c, META:META + SEQ]
            X2 = lambda c: X[:, c, 0:SEQ]
            layer_norm(0, X0)
            pe.wait_ge(*S.at("normed_lo", "ln", 0, KC - 1))
            for m in range(16):
                project(("m2", m), hi_lo(H), pieces2, [("m2_sigmoid", m)])

            def turn_values(what, c):
                s = claim(("v", what, c), [("v_ready", what, c)])
                pe.wait_ge(*S.at("v_biased", what, c))
                for kt in range(NQ):
                    mm = pe.transpose(big[s][:, kt * P:(kt + 1) * P], tm[:, (c + 1) % 2, kt * P:(kt + 1) * P], ident[:])
                mm.then_inc(*S.inc("v_turned", what, c))

            def before_na(c):
                project(("naq", c), hi_lo(H), pieces2, [("raw_copied", "naq", c)])
                project(("nak", c), hi_lo(H), pieces2, [("raw_copied", "nak", c)])
                project(("nav", c), hi_lo(H), pieces2, [("v_biased", "nav", c)])
                turn_values("nav", c)
                for e in (("q_stacked", "naq", c), ("k_split", "nak", c), ("v_ready", "nav", c)):
                    pe.wait_ge(*S.at(*e))

            def rotate2(key):
                plain("rotated", key, rot2[:], [tm[:, 3, :]], pieces2, [("rot_times_sin", *key)],
                      [("raw_copied", *key)])

            def by_chunk(kind, before):
                units = phases[(kind,)]
                for c in range(4):
                    part = [u for u in units if u["c"] == c]
                    before(c)
                    attention(part)

            by_chunk("n", before_na)
            project(("swk", 0), hi_lo(H), pieces2, [("raw_copied", "swk", 0)])
            rotate2(("swk", 0))
            project(("swv", 0), hi_lo(H), pieces2, [("v_biased", "swv", 0)])
            turn_values("swv", 0)

            def before_swa(c):
                project(("swq", c), hi_lo(H), pieces2, [("raw_copied", "swq", c)])
                rotate2(("swq", c))
                for e in (("q_stacked", "swq", c), ("k_split", "swk", 0), ("v_ready", "swv", 0)):
                    pe.wait_ge(*S.at(*e))

            by_chunk("s", before_swa)
            pe.wait_ge(*S.at("branches_lo", 7))
            for m in range(8):
                project(("y1", m), lambda part, k: SP2[:, part, k, :], pieces2, [("y1_gated", m)])
                project(("y2", m), lambda part, k: SP2[:, part, 4 + k, :], pieces2, [("y2_gated", m)])
            pe.wait_ge(*S.at("mix2_lo", 7))
            for m in range(8):
                project(("out2", m), hi_lo(H), pieces2, [("residual2", m)])
            layer_norm(1, X2)
            pe.wait_ge(*S.at("normed_lo", "ln", 1, KC - 1))
            for f in range(4):
                for m in range(8):
                    project(("ff1", f, m), hi_lo(H), pieces2, [("hidden_relu", f, m)])
                pe.wait_ge(*S.at("hidden_lo", f, 7))
                for m in range(8):
                    project(("ff2", f, m), hi_lo(SP2), pieces2, [("residual3", f, m)])
            layer_norm(2, X2)
            for t in range(NQ):
                s = claim(("final", t), [("out_copied", t)])
                pe.wait_ge(*S.at("ln_normed", 2, KC - 1))
                for c in range(KC):
                    mm = pe.transpose(big[s][:, c * P:(c + 1) * P], X[:, c, t * P:(t + 1) * P], ident[:])
                mm.then_inc(*S.inc("final_turned", t))


        def chain_temps(key):
            return (2, 3, 0) if key[0] in ("rms", "ln") else (0, 1, 2) if key[1] == "q" else (1, 2, 0)

        def weight_hi(act, n):
            if n < len(loads):
                job, _, cols, rows = loads[n]
                if n >= 2:
                    act.wait_ge(*S.at("projected", loads[n - 2][0]))
                act.wait_ge(*S.at(f"weights{n % RAW}", n))
                view = lambda ap: ap.rearrange("p (k n) -> p k n", k=KC)[:, 0:rows, 0:cols]
                act.activation(view(wsp[:, n % 2, 0, :]), view(raw[:, n % RAW, :]), ACT.Copy)\
                    .then_inc(*S.inc("weight_hi", n))

        def act_attention(act, units, per_chunk, chunk_done):
            for k in range(len(units) + 4):
                if k < len(units):
                    u, i = units[k], units[k]["i"]
                    act.wait_ge(*S.at("shift", i))
                    if i >= 2:
                        act.wait_ge(*S.at("turned", i - 2))
                    if i >= 4:
                        act.wait_ge(*S.at("normed_out", i - 4))
                    act.activation(Pb[:, i % 2, 0:u["n"]], Lb[:, i % 2, 0:u["n"]], ACT.Exp, bias=negmax[:, i % 4:i % 4 + 1],
                                   scale=SCALE, accum_out=rowsum[:, i % 4:i % 4 + 1]).then_inc(*S.inc("exped", i))
                    if u["sink"] is not None:
                        act.activation(sinkexp[:, i % 4:i % 4 + 1], negmax[:, i % 4:i % 4 + 1], ACT.Exp,
                                       bias=sink[:, 0, u["sink"]:u["sink"] + 1]).then_inc(*S.inc("sink_exped", i))
                if 1 <= k <= len(units):
                    move(act, units[k - 1], "act")
                if chunk_done and k >= per_chunk + 3 and (k - 3) % per_chunk == 0:
                    chunk_done((k - 3) // per_chunk - 1)

        def move(eng, u, who):
            parts, i = moves(u, who), u["i"]
            if not parts:
                return
            eng.wait_ge(*S.at("turned", i))
            if i >= 2:
                eng.wait_ge(*S.at("weighted", i - 2))
            for x, (kt, count, rows) in enumerate(parts):
                dst = PT[0:rows, i % 2, kt:kt + count, :]
                src = big[1][0:rows, kt * P:(kt + count) * P].rearrange("p (k n) -> p k n", k=count)
                ins = eng.activation(dst, src, ACT.Copy) if who == "act" else eng.tensor_copy(dst, src)
                ins.then_inc(*(S.inc(f"moved_{who}", i) if x == len(parts) - 1 else S.inc(f"moved_{who}", i, "part", x)))

        @block.scalar
        def _(act):
            weight_hi(act, 0)
            weight_hi(act, 1)

            def after(job):
                weight_hi(act, nload[job] + 2)

            def root(key, rows=slice(0, P), cols=TP):
                sq, rt, _ = chain_temps(key)
                act.wait_ge(*S.at("variance", *key))
                act.activation(tm[rows, rt, 0:cols], tm[rows, sq, 0:cols], ACT.Sqrt).then_inc(*S.inc("rooted", *key))

            act.wait_ge(*S.at("constants_here"))
            for l in range(DEPTH):
                for i in range(4):
                    act.activation(pool_bs[:, l, i:i + 1], pool_b[:, l, i:i + 1], ACT.Copy,
                                   scale=pool_s[:, l, i:i + 1]).then_inc(*S.inc("pool_bias", l, i))
            act.activation(sink[:, 1, :], sink[:, 0, :], ACT.Copy, scale=1.0 / SCALE).then_inc(*S.inc("sink8"))
            for j in range(NQ + 1):
                act.wait_ge(*S.at("x_transposed", j))
                t0, rows = (0, META) if j == 0 else (META + (j - 1) * P, P)
                act.activation(X[:, :, t0:t0 + rows],
                               big[j % 2][:, 0:KC * P].rearrange("p (k n) -> p k n", k=KC)[:, :, 0:rows],
                               ACT.Copy).then_inc(*S.inc("x_turned", j))

            def split_hi(name, key, dst, src, waits):
                for w in waits:
                    act.wait_ge(*S.at(*w))
                act.activation(dst, src, ACT.Copy).then_inc(*S.inc(name, *key))

            for l in range(DEPTH):
                for c in range(KC if l else 0):
                    act.wait_ge(*S.at("residual", l - 1, c))
                    after(("out", l - 1, c))
                for c in range(KC):
                    if l == 0:
                        act.wait_ge(*S.at("x_turned", NQ))
                        act.wait_ge(*S.at("x_padded"))
                    else:
                        act.wait_ge(*S.at("residual", l - 1, c))
                    if c >= 2:
                        act.wait_ge(*S.at("mean_square_part", l, c - 2))
                    elif l > 0:
                        act.wait_ge(*S.at("mix_lo", l - 1, 6 + c))
                    act.activation(tm[:, c % 2, :], X[:, c, :], ACT.Square).then_inc(*S.inc("squared", "rms", l, c))
                root(("rms", l))
                for c in range(KC):
                    split_hi("normed_hi", ("rms", l, c), H[:, 0, c, :], tm[:, 1 + c % 2, :], [("normed", "rms", l, c)])

                sc4 = [SC[:, i * TP:(i + 1) * TP] for i in range(4)]

                def split_q(name, key, src, dst, k, rows=2):
                    act.wait_ge(*S.at("roped", name, *key))
                    for hh in range(2):
                        part = slice(hh * HD, (hh + 1) * HD)
                        act.activation(dst[part, k + hh, :], src[part], ACT.Copy)\
                            .then_inc(*S.inc("q_hi", name, *key, hh))

                def split_k(name, key, src, dst_lo, dst_hi):
                    act.wait_ge(*S.at("roped", name, *key))
                    for half, dst in enumerate((dst_lo, dst_hi)):
                        act.activation(dst, src, ACT.Copy).then_inc(*S.inc("k_hi", name, *key, half))

                for c in range(5):
                    if c < 4:
                        s, x, y = psum_of[("q", l, c)], sc4[2 * (c % 2)], sc4[2 * (c % 2) + 1]
                        act.wait_ge(*S.at("projected", ("q", l, c)))
                        if c >= 2:
                            act.wait_ge(*S.at("q_stacked", "q", l, c - 2))
                        act.activation(v3(x), ps3(s), ACT.Square).then_inc(*S.inc("head_squared", "q", l, c))
                        act.activation(v3(y), ps3(s), ACT.Copy, scale=qk_gain[:, l, 0:1])\
                            .then_inc(*S.inc("raw_copied", "q", l, c))
                        after(("q", l, c))
                    if c >= 1:
                        root(("head", "q", l, c - 1))
                        split_q("q", (l, c - 1), sc4[2 * ((c - 1) % 2)], QS, 2 * (c - 1))
                s, lo64 = psum_of[("ki", l)], slice(0, HD)
                act.wait_ge(*S.at("projected", ("ki", l)))
                act.activation(v3(tm[lo64, 3, :]), ps3(s, lo64), ACT.Copy).then_inc(*S.inc("raw_copied", "ki", l))
                act.activation(v3(tm[HD:HD + 8, 3, :]), ps3(s, slice(HD, HD + 8)), ACT.Copy)\
                    .then_inc(*S.inc("w_copied", l))
                after(("ki", l))
                split_k("ki", (l,), tm[lo64, 2, :], KK[0:HD, 0, :], KK[HD:P, 0, :])
                act.wait_ge(*S.at("w_turned", l))
                act.activation(widx[:, 1:NQ, :],
                               big[psum_of[("w", l)]][:, 8:NQ * 8].rearrange("p (j h) -> p j h", h=8), ACT.Copy,
                               scale=IDX_SCALE).then_inc(*S.inc("w_ready", l))
                nrelu = 0
                for c in range(4):
                    act.wait_ge(*S.at("projected", ("qi", l, c)))
                    act.wait_ge(*S.at("q_stacked", "qi", l, c - 1) if c else S.at("k_split", "ki", l))
                    act.activation(v3(tm[:, 3, :]), ps3(psum_of[("qi", l, c)]), ACT.Copy)\
                        .then_inc(*S.inc("raw_copied", "qi", l, c))
                    after(("qi", l, c))
                    if c == 0:
                        act.wait_ge(*(S.at("x_saved", l - 1, 7) if l else S.at("x_stored")))
                    split_q("qi", (l, c), tm[:, 2, :], QIPB, 2 * (c % 2))
                    for hh in range(2):
                        for j in range(1, NQ):
                            n = visible(j)
                            act.wait_ge(*S.at("index_scores", l, c, hh, j))
                            if nrelu >= 2:
                                act.wait_ge(*S.at("score_added", l, *score_units[nrelu - 2]))
                            act.activation(tm[:, nrelu % 2, 0:n], big[psum_of[("index", l, c, hh, j)]][:, 0:n], ACT.Relu)\
                                .then_inc(*S.inc("relued", l, c, hh, j))
                            nrelu += 1
                s = psum_of[("kv", l)]
                act.wait_ge(*S.at("projected", ("kv", l)))
                act.wait_ge(*S.at("score_added", l, *score_units[-1]))
                act.wait_ge(*S.at("q_stacked", "qi", l, 3))
                act.activation(v3(tm[lo64, 0, :]), ps3(s, lo64), ACT.Square).then_inc(*S.inc("head_squared", "k", l))
                act.activation(v3(tm[lo64, 3, :]), ps3(s, lo64), ACT.Copy, scale=qk_gain[lo64, l, 1:2])\
                    .then_inc(*S.inc("raw_copied", "k", l))
                act.activation(v3(tm[HD:P, 3, :]), ps3(s, slice(HD, P)), ACT.Copy).then_inc(*S.inc("v_copied", l))
                after(("kv", l))
                root(("head", "k", l), lo64)
                split_k("k", (l,), tm[lo64, 1, :], KK[0:HD, 0, :], KK[HD:P, 0, :])
                s = psum_of[("v", l)]
                act.wait_ge(*S.at("v_turned", l))
                act.activation(V[:, 0:8, :], big[s][:, 0:8 * HD].rearrange("p (k d) -> p k d", k=8), ACT.Copy)\
                    .then_inc(*S.inc("v_part", l))
                act.activation(V[0:META, 8, :], big[s][0:META, 8 * HD:9 * HD], ACT.Copy).then_inc(*S.inc("v_ready", l))
                for g in range(4):
                    act.wait_ge(*S.at("projected", ("u", l, g)))
                    act.wait_ge(*S.at("k_split", "k", l) if g == 0 else S.at("pool_mixed", l, g - 1))
                    act.activation(v3(tm[:, 0, :]), ps3(psum_of[("u", l, g)]), ACT.Copy).then_inc(*S.inc("u_copied", l, g))
                    after(("u", l, g))
                    act.wait_ge(*S.at("projected", ("gateb", l, g)))
                    if g:
                        act.wait_ge(*S.at("pool_gated", l, g - 1))
                    act.activation(v3(tm[:, 3, :]), ps3(psum_of[("gateb", l, g)]), ACT.Silu)\
                        .then_inc(*S.inc("gateb_silu", l, g))
                    after(("gateb", l, g))
                    act.wait_ge(*S.at("pool_mixed", l, g))
                    act.wait_ge(*S.at("pool_bias", l, g))
                    act.activation(v3(tm[:, 1, :]), ps3(psum_of[("pool_mixed", l, g)]), ACT.Identity,
                                   scale=pool_s[:, l, g:g + 1], bias=pool_bs[:, l, g:g + 1])\
                        .then_inc(*S.inc("pool_scaled", l, g))
                    split_hi("pool_hi", (l, g), QIPB[:, g, :], tm[:, 1, :], [("pool_gated", l, g)])
                for c in range(4):
                    act.wait_ge(*S.at("projected", ("gatea", l, c)))
                    act.wait_ge(*S.at("pool_lo", l, 3) if c < 2 else S.at(f"gate_out{c % 2}", "a", l, c - 2))
                    act.activation(v3(tm[:, c % 2, :]), ps3(psum_of[("gatea", l, c)]), ACT.Silu)\
                        .then_inc(*S.inc("gatea_silu", l, c))
                    act.wait_ge(*S.at("gatea_silu", l, c))
                    act.dma_start(sg_d[c], tm[:, c % 2, :]).then_inc(*S.dma(f"gate_out{c % 2}", "a", l, c))
                    after(("gatea", l, c))
                for m in range(8):
                    act.wait_ge(*S.at("projected", ("mb", l, m)))
                    act.wait_ge(*S.at("yb_gated", l, m - 2) if m >= 2 else S.at(f"gate_out{m}", "a", l, m + 2))
                    act.activation(v3(tm[:, m % 2, :]), ps3(psum_of[("mb", l, m)]), ACT.Sigmoid)\
                        .then_inc(*S.inc("mb_sigmoid", l, m))
                    after(("mb", l, m))
                    act.wait_ge(*S.at("projected", ("yb", l, m)))
                    if m >= 2:
                        act.wait_ge(*S.at(f"yb_out{m % 2}", l, m - 2))
                    act.activation(v3(tm[:, 2 + m % 2, :]), ps3(psum_of[("yb", l, m)]), ACT.Copy)\
                        .then_inc(*S.inc("yb_copied", l, m))
                    after(("yb", l, m))
                for m in range(8):
                    act.wait_ge(*S.at("projected", ("ma", l, m)))
                    act.wait_ge(*S.at("yb_gated", l, 6 + m) if m < 2 else S.at(f"ma_out{m % 2}", l, m - 2))
                    act.activation(v3(tm[:, m % 2, :]), ps3(psum_of[("ma", l, m)]), ACT.Sigmoid)\
                        .then_inc(*S.inc("ma_sigmoid", l, m))
                    act.wait_ge(*S.at("ma_sigmoid", l, m))
                    act.dma_start(ga_d[m], tm[:, m % 2, :]).then_inc(*S.dma(f"ma_out{m % 2}", l, m))
                    after(("ma", l, m))

                def first_chunk_done(c):
                    split_hi("attn_hi", (l, c), QS[:, 2 * c, :], tm[:, 2 + c % 2, :],
                             [("gated", phases[("a", l)][18 * c + 16]["i"])])

                act_attention(act, phases[("a", l)], 18, first_chunk_done)
                for m in range(8):
                    act.wait_ge(*S.at("projected", ("ya", l, m)))
                    after(("ya", l, m))
                    split_hi("mix_hi", (l, m), H[:, 0, m, :], tm[:, m % 2, :], [("mixed", l, m)])

            def ln(i, c0, waits):
                for c in range(KC):
                    act.wait_ge(*S.at("centered", i, c))
                    if c >= 2:
                        act.wait_ge(*S.at("mean_square_part", "ln", i, c - 2))
                    for w in waits if c < 2 else []:
                        act.wait_ge(*S.at(*w))
                    act.activation(tm[:, c % 2, 0:SEQ], X[:, c, c0:c0 + SEQ], ACT.Square)\
                        .then_inc(*S.inc("squared", "ln", i, c))
                root(("ln", i), cols=SEQ)
                for c in range(KC):
                    act.wait_ge(*S.at("scaled", i, c))
                    act.activation(X[:, c, c0:c0 + SEQ], X[:, c, c0:c0 + SEQ], ACT.Identity, bias=ln_b[:, i, c:c + 1])\
                        .then_inc(*S.inc("ln_normed", i, c))
                    if i < 2:
                        split_hi("normed_hi", ("ln", i, c), H[:, 0, c, 0:SEQ], X[:, c, c0:c0 + SEQ],
                                 [("ln_normed", i, c)])

            for c in range(KC):
                act.wait_ge(*S.at("residual", DEPTH - 1, c))
                after(("out", DEPTH - 1, c))
            ln(0, META, [])
            for m in range(16):
                act.wait_ge(*S.at("projected", ("m2", m)))
                if m >= 2:
                    act.wait_ge(*S.at(f"m2_out{m % 2}", m - 2))
                else:
                    act.wait_ge(*S.at("scaled", 0, KC - 1))
                act.activation(tm[:, m % 2, 0:SEQ], ps2(psum_of[("m2", m)]), ACT.Sigmoid,
                               bias=b_in2[:, MG2 // P + m:MG2 // P + m + 1]).then_inc(*S.inc("m2_sigmoid", m))
                act.wait_ge(*S.at("m2_sigmoid", m))
                act.dma_start((ga_d if m < 8 else gb_d)[m % 8][:, 0:SEQ], tm[:, m % 2, 0:SEQ])\
                    .then_inc(*S.dma(f"m2_out{m % 2}", m))
                after(("m2", m))

            def biased(what, c, col, slot, name, waits):
                act.wait_ge(*S.at("projected", (what, c)))
                for w in waits:
                    act.wait_ge(*S.at(*w))
                act.activation(tm[:, slot, 0:SEQ], ps2(psum_of[(what, c)]), ACT.Identity,
                               bias=b_in2[:, col // P + c:col // P + c + 1]).then_inc(*S.inc(name, what, c))
                after((what, c))

            def store_free(c, kind):
                k = c - 1 + (4 if kind == "s" else 0)
                return [(f"attn_out{k % 2}", k)] if k >= 0 else [("m2_out0", 14), ("m2_out1", 15)]

            def split_k2(what, c, src, waits):
                for w in waits:
                    act.wait_ge(*S.at(*w))
                for hh in range(2):
                    for half in range(2):
                        act.activation(K2[half * HD:(half + 1) * HD, hh, 0, :], src[hh * HD:(hh + 1) * HD, 0:SEQ], ACT.Copy)\
                            .then_inc(*S.inc("k_hi", what, c, hh, half))

            def split_q2(what, c, src, waits):
                for w in waits:
                    act.wait_ge(*S.at(*w))
                for hh in range(2):
                    part = slice(hh * HD, (hh + 1) * HD)
                    act.activation(Q2[part, hh, :], src[part, 0:SEQ], ACT.Copy).then_inc(*S.inc("q_hi", what, c, hh))

            def take_v(what, c):
                act.wait_ge(*S.at("v_turned", what, c))
                act.activation(V2[:, :, :], ps2(psum_of[("v", what, c)]).rearrange("p (k d) -> p k d", k=NQ), ACT.Copy)\
                    .then_inc(*S.inc("v_ready", what, c))

            for c in range(4):
                last = [("k_split", "nak", c - 1)] if c else []
                biased("naq", c, NAQ0, 3, "raw_copied", last + ([("q_stacked", "naq", c - 1)] if c else [("m2_out1", 15)]))
                biased("nak", c, NAK0, 2, "raw_copied", last)
                biased("nav", c, NAV0, (c + 1) % 2, "v_biased", store_free(c, "n"))
                split_q2("naq", c, tm[:, 3, :], [("raw_copied", "naq", c)])
                split_k2("nak", c, tm[:, 2, :], [("raw_copied", "nak", c)])
                take_v("nav", c)
                act_attention(act, [u for u in phases[("n",)] if u["c"] == c], 16, None)
            biased("swk", 0, SWK0, 3, "raw_copied", [("q_stacked", "naq", 3), ("k_split", "nak", 3)])
            biased("swv", 0, SWV0, 1, "v_biased", store_free(0, "s"))
            split_k2("swk", 0, tm[:, 2, :], [("roped", "swk", 0)])
            take_v("swv", 0)
            for c in range(4):
                biased("swq", c, SWQ0, 3, "raw_copied", [("k_split", "swk", 0)] if c == 0 else [("q_stacked", "swq", c - 1)])
                split_q2("swq", c, tm[:, 2, :], [("roped", "swq", c)])
                act_attention(act, [u for u in phases[("s",)] if u["c"] == c], 16, None)
            for k in range(8):
                split_hi("branches_hi", (k,), SP2[:, 0, k, :], tm[:, k % 2, 0:SEQ], [(f"attn_in{k % 2}", k)])
            for m in range(8):
                for job in (("y1", m), ("y2", m)):
                    act.wait_ge(*S.at("projected", job))
                    after(job)
                split_hi("mix2_hi", (m,), H[:, 0, m, 0:SEQ], tm[:, m % 2, 0:SEQ], [("mixed2", m)])
            for m in range(8):
                act.wait_ge(*S.at("projected", ("out2", m)))
                after(("out2", m))
            ln(1, 0, [("residual2", 7)])
            for f in range(4):
                for m in range(8):
                    act.wait_ge(*S.at("projected", ("ff1", f, m)))
                    n = f * 8 + m
                    if n >= 2:
                        act.wait_ge(*S.at("hidden_lo", (n - 2) // 8, (n - 2) % 8))
                    else:
                        act.wait_ge(*S.at("scaled", 1, KC - 1))
                    act.activation(tm[:, n % 2, 0:SEQ], ps2(psum_of[("ff1", f, m)]), ACT.Relu, bias=b_ff1[:, n:n + 1])\
                        .then_inc(*S.inc("hidden_relu", f, m))
                    after(("ff1", f, m))
                    act.wait_ge(*S.at("hidden_relu", f, m))
                    act.activation(tm[:, n % 2, 0:SEQ], tm[:, n % 2, 0:SEQ], ACT.Square)\
                        .then_inc(*S.inc("hidden_squared", f, m))
                    split_hi("hidden_hi", (f, m), SP2[:, 0, m, :], tm[:, n % 2, 0:SEQ], [("hidden_squared", f, m)])
                for m in range(8):
                    act.wait_ge(*S.at("projected", ("ff2", f, m)))
                    after(("ff2", f, m))
            ln(2, 0, [("hidden_lo", 3, 7), ("residual3", 3, 7)])
            for t in range(NQ):
                act.wait_ge(*S.at("final_turned", t))
                if t >= 2:
                    act.wait_ge(*S.at(f"output{t % 2}", t - 2))
                else:
                    act.wait_ge(*S.at("scaled", 2, KC - 1))
                act.activation(tm[:, t % 2, 0:D], ps2(psum_of[("final", t)]), ACT.Copy).then_inc(*S.inc("out_copied", t))
                act.wait_ge(*S.at("out_copied", t))
                act.dma_start(a["out"][0, t * P:(t + 1) * P, :], tm[:, t % 2, 0:D]).then_inc(*S.dma(f"output{t % 2}", t))

        @block.gpsimd
        def _(pool):
            def lo_part(ins, name, *key):
                ins.then_inc(*S.inc(name, *key))

            def subtract(name, key, dst, src, hi, waits):
                for w in waits:
                    pool.wait_ge(*S.at(*w))
                pool.tensor_tensor(dst, src, hi.bitcast(F32), ALU.subtract).then_inc(*S.inc(name, *key))

            def weight_lo(n):
                if n < len(loads):
                    _, _, cols, rows = loads[n]
                    view = lambda ap: ap.rearrange("p (k n) -> p k n", k=KC)[:, 0:rows, 0:cols]
                    subtract("weight_lo", (n,), view(wsp[:, n % 2, 1, :]), view(raw[:, n % RAW, :]),
                             view(wsp[:, n % 2, 0, :]), [("weight_hi", n)])

            def after(job):
                weight_lo(nload[job] + 2)

            def load(name, key, dst, src, waits):
                for w in waits:
                    pool.wait_ge(*S.at(*w))
                pool.dma_start(dst, src).then_inc(*S.dma(name, *key))

            store = load

            pool.memset(zeros[:, :], 0.0).then_inc(*S.inc("zeros"))
            n_rpb = HEADS * 15 * 31
            store("rpb_pad", (0,), rpb_d[0:64].rearrange("(a n) -> a n", a=1), zeros[0:1, :], [("zeros",)])
            store("rpb_pad", (1,), rpb_d[64 + n_rpb:].rearrange("(a n) -> a n", a=1), zeros[0:1, :], [])
            store("rpb_pad", (2,), rpb_d[64:64 + n_rpb].rearrange("(a n) -> a n", a=8),
                  a["na_rpb_2"][0].rearrange("h i j -> h (i j)"), [])
            for h in range(HEADS):
                src = bass.AP(rpb_d.tensor, 64 + h * 15 * 31 + 15, [[31, 15], [-1, GRID], [1, GRID]])
                store("bands", (h,), band_d[h], src, [("rpb_pad", 2)])
            weight_lo(0)
            weight_lo(1)
            for j in range(NQ + 1):
                src = a["meta_tokens"] if j == 0 else a["x"][0, (j - 1) * P:j * P, :]
                load(f"x_in{j % 2}", (j,), tm[0:(META if j == 0 else P), j % 2, 0:D], src,
                     [("x_transposed", j - 2)] if j >= 2 else [])
            store("x_stored", (), xT_d.rearrange("k p n -> p k n"), X[:, :, :], [("x_turned", NQ), ("x_padded",)])

            def times_cos(key, dst, src, trig, waits):
                for w in waits:
                    pool.wait_ge(*S.at(*w))
                pool.tensor_tensor(dst, src, trig, ALU.mult).then_inc(*S.inc("times_cos", *key))

            lo64 = slice(0, HD)
            for l in range(DEPTH):
                for c in range(KC):
                    subtract("normed_lo", ("rms", l, c), H[:, 1, c, :], tm[:, 1 + c % 2, :], H[:, 0, c, :],
                             [("normed_hi", "rms", l, c)])
                x_read = [("normed", "rms", l, KC - 1), ("x_saved", l - 1, 7) if l else ("x_stored",)]
                load("pool_weights", (l,), pw[:, :, :], a["pool_w"][l].rearrange("g c d -> c g d"), x_read)
                load("rotary_tables", (l,), trig1[:, :, :], a["c_trig1"], [])
                pool.wait_ge(*S.at("rotary_tables", l))
                sc4 = [SC[:, i * TP:(i + 1) * TP] for i in range(4)]
                for c in range(5):
                    if c < 4:
                        after(("q", l, c))
                    if c >= 1:
                        x, y = sc4[2 * ((c - 1) % 2)], sc4[2 * ((c - 1) % 2) + 1]
                        times_cos(("q", l, c - 1), x, y, trig1[:, 0, :],
                                  [("raw_copied", "q", l, c - 1), ("head_square", "q", l, c - 1)])
                after(("ki", l))
                times_cos(("ki", l), tm[lo64, 2, :], tm[lo64, 3, :], trig1[lo64, 0, :],
                          [("raw_copied", "ki", l), ("q_stacked", "q", l, 3)])
                for c in range(4):
                    after(("qi", l, c))
                    times_cos(("qi", l, c), tm[:, 2, :], tm[:, 3, :], trig1[:, 0, :],
                              [("raw_copied", "qi", l, c)])
                after(("kv", l))
                times_cos(("k", l), tm[lo64, 2, :], tm[lo64, 3, :], trig1[lo64, 0, :],
                          [("rstd", "head", "k", l)])
                for g, w in enumerate(WINDOWS):
                    after(("u", l, g))
                    pool.wait_ge(*S.at("u_copied", l, g))
                    if g:
                        pool.wait_ge(*S.at("pool_lo", l, g - 1))
                    src, d, slot = tm[:, 0, :], 1, 1
                    while d < w:
                        dst = tm[:, slot, :]
                        pool.tensor_copy(dst[:, 0:d], src[:, 0:d]).then_inc(*S.inc("window_edge", l, g, d))
                        pool.tensor_tensor(dst[:, d:TP], src[:, d:TP], src[:, 0:TP - d], ALU.add)\
                            .then_inc(*S.inc("window_sum", l, g, d))
                        pool.wait_ge(*S.at("window_edge", l, g, d))
                        pool.wait_ge(*S.at("window_sum", l, g, d))
                        src, d, slot = dst, 2 * d, 3 - slot
                    pool.tensor_tensor(src[:, 0:16], src[:, 0:16], edge[:, g, :], ALU.mult)\
                        .then_inc(*S.inc("window_count", l, g))
                    pool.wait_ge(*S.at("window_count", l, g))
                    pool.tensor_scalar(src, src, 1.0 / w, None, ALU.mult).then_inc(*S.inc("window_mean", l, g))
                    pool.wait_ge(*S.at("window_mean", l, g))
                    pool.tensor_tensor(tm[:, 0, :], src, tm[:, 0, :], ALU.subtract).then_inc(*S.inc("pooled", l, g))
                    after(("gateb", l, g))
                    pool.wait_ge(*S.at("pool_scaled", l, g))
                    pool.wait_ge(*S.at("gateb_silu", l, g))
                    pool.tensor_tensor(tm[:, 1, :], tm[:, 1, :], tm[:, 3, :], ALU.mult)\
                        .then_inc(*S.inc("pool_gated", l, g))
                    subtract("pool_lo", (l, g), QIPB[:, 4 + g, :], tm[:, 1, :], QIPB[:, g, :], [("pool_hi", l, g)])
                for c in range(4):
                    after(("gatea", l, c))
                for m in range(8):
                    after(("mb", l, m))
                    after(("yb", l, m))
                    pool.wait_ge(*S.at("mb_sigmoid", l, m))
                    pool.wait_ge(*S.at("yb_copied", l, m))
                    y = tm[:, 2 + m % 2, :]
                    pool.tensor_tensor(y, y, tm[:, m % 2, :], ALU.mult).then_inc(*S.inc("yb_gated", l, m))
                    store(f"yb_out{m % 2}", (l, m), gb_d[m], y, [("yb_gated", l, m)])
                for m in range(8):
                    after(("ma", l, m))
                load("mask0_in", (l,), mask0[:, :], a["c_mask0"], [("projected", ("yb", l, 7))])
                units = phases[("a", l)]
                for c in range(4):
                    load(f"silu_in{c % 2}", (l, c), tm[:, c % 2, :], sg_d[c],
                         [(f"gate_out{c % 2}", "a", l, c),
                          (f"ma_out{c % 2}", l, 6 + c) if c < 2 else ("gated", units[18 * (c - 2) + 16]["i"])])
                    if c >= 1:
                        subtract("attn_lo", (l, c - 1), QS[:, 2 * c - 1, :], tm[:, 2 + (c - 1) % 2, :],
                                 QS[:, 2 * c - 2, :], [("attn_hi", l, c - 1)])
                subtract("attn_lo", (l, 3), QS[:, 7, :], tm[:, 3, :], QS[:, 6, :], [("attn_hi", l, 3)])
                for m in range(-2, 8):
                    if m >= 0:
                        after(("ya", l, m))
                        subtract("mix_lo", (l, m), H[:, 1, m, :], tm[:, m % 2, :], H[:, 0, m, :], [("mix_hi", l, m)])
                    n = m + 2
                    if n < 8:
                        load(f"mix_in{n % 2}", ("a", l, n), tm[:, n % 2, :], ga_d[n],
                             [(f"ma_out{n % 2}", l, n)] +
                             ([("gated", units[18 * (2 + n) + 16]["i"])] if n < 2 else [("mix_lo", l, n - 2)]))
                        load(f"mix_in{n % 2}", ("b", l, n), tm[:, 2 + n % 2, :], gb_d[n],
                             [(f"yb_out{n % 2}", l, n), ("attn_lo", l, 3)] + ([("mixed", l, n - 2)] if n >= 2 else []))
                for m in range(-2, 8):
                    if m >= 0:
                        after(("out", l, m))
                        if l < DEPTH - 1:
                            store("x_saved", (l, m), xT_d[m], X[:, m, :], [("residual", l, m)])
                    n = m + 2
                    if n < 8:
                        load(f"x_old{n % 2}", (l, n), tm[:, 2 + n % 2, :], xT_d[n],
                             [("x_stored",) if l == 0 else ("x_saved", l - 1, 7),
                              ("mixed", l, 6 + n) if n < 2 else ("residual", l, n - 2)])
            z2_free = ("residual", DEPTH - 1, 7)
            for i, (dst, src) in enumerate(((trig2, "c_trig2"), (colmask, "c_colmask"), (rowmask, "c_rowmask"),
                                            (swmask, "c_swmask"))):
                load("block2_consts", (i,), dst[:], a[src], [z2_free] if i == 0 else [])

            def ln(i, c0):
                for c in range(KC):
                    subtract("normed_lo", ("ln", i, c), H[:, 1, c, 0:SEQ], X[:, c, c0:c0 + SEQ], H[:, 0, c, 0:SEQ],
                             [("normed_hi", "ln", i, c)])
                    if i == 0:
                        store("ln_saved", (c,), xT_d[c][:, 0:SEQ], X[:, c, c0:c0 + SEQ], [("ln_normed", 0, c)])

            ln(0, META)

            def bias_tables(c):
                for hh in range(2):
                    for half in range(2):
                        src = band_d[2 * c + hh, 1 - half:15 - half].rearrange("i w k -> w i k")
                        load("bias_in", (c, hh, half), bias_e[half * GRID:(half + 1) * GRID, hh, :, :], src,
                             [("bands", HEADS - 1), z2_free] + ([("masked", phases[("n",)][16 * c - 1]["i"])] if c else []))
                pool.wait_ge(*S.at("bias_in", c, 1, 1))
                pool.wait_ge(*S.at("block2_consts", 3))
                for hh in range(2):
                    e = bias_e[:, hh, :, :]
                    pool.tensor_scalar(e, e, 1.0 / SCALE, None, ALU.mult).then_inc(*S.inc("bias_scaled", c, hh))
                    pool.wait_ge(*S.at("bias_scaled", c, hh))
                    pool.tensor_tensor(e, e, colmask[:, :, :], ALU.add).then_inc(*S.inc("bias_masked", c, hh))
                    pool.wait_ge(*S.at("bias_masked", c, hh))
                    pool.tensor_tensor(bias_i[:, hh, :, :], e[:, 2:11, :], rowmask[:, :, :], ALU.add)\
                        .then_inc(*S.inc("bias_ready", c, hh))

            for m in range(16):
                after(("m2", m))
            for c in range(4):
                bias_tables(c)
                for what in ("naq", "nak", "nav"):
                    after((what, c))
                store(f"attn_out{c % 2}", (c,), at_d[c], tm[:, c % 2, 0:SEQ],
                      [("gated", phases[("n",)][16 * c + 14]["i"])])
            after(("swk", 0))
            times_cos(("swk", 0), tm[:, 2, 0:SEQ], tm[:, 3, 0:SEQ], trig2[:, 0, :],
                      [("raw_copied", "swk", 0), ("k_split", "nak", 3)])
            after(("swv", 0))
            for c in range(4):
                after(("swq", c))
                times_cos(("swq", c), tm[:, 2, 0:SEQ], tm[:, 3, 0:SEQ], trig2[:, 0, :],
                          [("raw_copied", "swq", c), ("q_stacked", "swq", c - 1) if c else ("k_split", "swk", 0)])
                store(f"attn_out{c % 2}", (4 + c,), at_d[4 + c], tm[:, c % 2, 0:SEQ],
                      [("gated", phases[("s",)][16 * c + 14]["i"])])
            for k in range(-2, 8):
                if k >= 0:
                    subtract("branches_lo", (k,), SP2[:, 1, k, :], tm[:, k % 2, 0:SEQ], SP2[:, 0, k, :],
                             [("branches_hi", k)])
                n = k + 2
                if n < 8:
                    load(f"attn_in{n % 2}", (n,), tm[:, n % 2, 0:SEQ], at_d[n],
                         [("attn_out0", 6), ("attn_out1", 7)] if n < 2 else [("branches_lo", n - 2)])
            for m in range(-2, 8):
                if m >= 0:
                    after(("y1", m))
                    after(("y2", m))
                    subtract("mix2_lo", (m,), H[:, 1, m, 0:SEQ], tm[:, m % 2, 0:SEQ], H[:, 0, m, 0:SEQ],
                             [("mix2_hi", m)])
                n = m + 2
                if n < 8:
                    load(f"mix2_in{n % 2}", ("a", n), tm[:, n % 2, 0:SEQ], ga_d[n][:, 0:SEQ],
                         [("branches_lo", 6 + n) if n < 2 else ("mix2_lo", n - 2)])
                    load(f"mix2_in{n % 2}", ("b", n), tm[:, 2 + n % 2, 0:SEQ], gb_d[n][:, 0:SEQ],
                         [("mixed2", n - 2)] if n >= 2 else [("q_stacked", "swq", 3)])
            for m in range(8):
                load(f"h_old{m % 2}", (m,), tm[:, 2 + m % 2, 0:SEQ], xT_d[m][:, 0:SEQ],
                     [("ln_saved", 7), ("mixed2", 6 + m) if m < 2 else ("residual2", m - 2)])
                after(("out2", m))
            ln(1, 0)
            for f in range(4):
                for m in range(8):
                    after(("ff1", f, m))
                    subtract("hidden_lo", (f, m), SP2[:, 1, m, :], tm[:, m % 2, 0:SEQ], SP2[:, 0, m, :],
                             [("hidden_hi", f, m)])
                for m in range(8):
                    after(("ff2", f, m))

        @block.vector
        def _(dve):
            steps = [0]

            def step(ins):
                steps[0] += 1
                ins.then_inc(*S.inc("vector_step", steps[0]))
                dve.wait_ge(*S.at("vector_step", steps[0]))

            def wait(*events):
                for e in events:
                    dve.wait_ge(*S.at(*e))

            def rstd(key, name, src, eps, rows=slice(0, P), cols=TP):
                va, rt, out = (tm[rows, i, 0:cols] for i in chain_temps(key))
                shaped = (lambda ap: v3(ap)) if cols == TP else (lambda ap: ap)
                wait(name)
                dve.tensor_scalar(shaped(va), src, eps, None, ALU.add).then_inc(*S.inc("variance", *key))
                wait(("rooted", *key))
                step(dve.reciprocal(out, rt))
                step(dve.tensor_tensor(rt, va, out, ALU.mult))
                step(dve.scalar_tensor_tensor(rt, rt, -0.5, out, ALU.mult, ALU.mult))
                dve.scalar_tensor_tensor(out, rt, 1.5, out, ALU.add, ALU.mult).then_inc(*S.inc("rstd", *key))
                wait(("rstd", *key))

            def rotate(key, x, y, src, sin, last=None):
                wait(("rotated", *key), ("times_cos", *key))
                dve.tensor_tensor(y, src, sin, ALU.mult).then_inc(*S.inc("rot_times_sin", *key))
                wait(("rot_times_sin", *key))

            def stack_q(name, key, src, dst):
                for hh in range(2):
                    own, other = slice(hh * HD, (hh + 1) * HD), slice((1 - hh) * HD, (2 - hh) * HD)
                    wait(("q_hi", name, *key, hh))
                    dve.tensor_tensor(dst(hh, other), src[own], dst(hh, own).bitcast(F32), ALU.subtract)\
                        .then_inc(*(S.inc("q_stacked", name, *key) if hh else S.inc("q_stacking", name, *key)))

            def split_k(name, l, src):
                wait(("k_hi", name, l, 1))
                for half in range(2):
                    dve.tensor_tensor(KK[half * HD:(half + 1) * HD, 1, :], src, KK[0:HD, 0, :].bitcast(F32), ALU.subtract)\
                        .then_inc(*(S.inc("k_split", name, l) if half else S.inc("k_splitting", name, l)))

            def attention(units, mask_waits, gate):
                for k in range(len(units) + 3):
                    if k < len(units):
                        u, i = units[k], units[k]["i"]
                        wait(("logits", i), *mask_waits(u))
                        if i >= 2:
                            wait(("exped", i - 2))
                        start = TAKEN if u["sink"] is None else sink[:, 1, u["sink"]:u["sink"] + 1]
                        dve.tensor_tensor_reduce(out=Lb[:, i % 2, 0:u["n"]], in0=big[0][:, 0:u["n"]], in1=u["mask"],
                                                 scale=1.0, scalar=start, op0=ALU.add, op1=ALU.max,
                                                 accum_out=rowmax[:, i % 2:i % 2 + 1]).then_inc(*S.inc("masked", i))
                        wait(("masked", i))
                        dve.tensor_scalar(negmax[:, i % 4:i % 4 + 1], rowmax[:, i % 2:i % 2 + 1], -SCALE, None, ALU.mult)\
                            .then_inc(*S.inc("shift", i))
                    if 1 <= k <= len(units):
                        move(dve, units[k - 1], "dve")
                    if k >= 3 and (k - 3) % 2 == 1:
                        gate(units[k - 4], small[1])
                    if 2 <= k <= len(units) + 1:
                        u, i = units[k - 2], units[k - 2]["i"]
                        s, slot = rowsum[:, i % 4:i % 4 + 1], (k - 2) // 2 % 2
                        wait(("weighted", i))
                        if u["sink"] is not None:
                            wait(("sink_exped", i))
                            step(dve.tensor_tensor(s, s, sinkexp[:, i % 4:i % 4 + 1], ALU.add))
                        if i - u["hh"] - 4 >= 0:
                            wait(("out_turned", i - u["hh"] - 4))
                        step(dve.reciprocal(rowinv[:, i % 4:i % 4 + 1], s))
                        dve.tensor_scalar(Ob[:, slot, u["hh"] * HD:(u["hh"] + 1) * HD],
                                          small[u["hh"]][:, 0:HD],
                                          rowinv[:, i % 4:i % 4 + 1], None, ALU.mult).then_inc(*S.inc("normed_out", i))

            dve.memset(X[:, :, T:TP], 0.0).then_inc(*S.inc("x_padded"))
            lo64 = slice(0, HD)
            for l in range(DEPTH):
                rstd(("rms", l), ("mean_square", l), ps3(psum_of[("mean_square", l)]), EPS)
                for c in range(KC):
                    if c >= 2:
                        wait(("normed_lo", "rms", l, c - 2))
                    dve.scalar_tensor_tensor(tm[:, 1 + c % 2, :], X[:, c, :], gain[:, l, c:c + 1], tm[:, 0, :],
                                             ALU.mult, ALU.mult).then_inc(*S.inc("normed", "rms", l, c))
                sc4 = [SC[:, i * TP:(i + 1) * TP] for i in range(4)]
                wait(("normed_lo", "rms", l, KC - 1), ("rotary_tables", l))
                for c in range(4):
                    x, y = sc4[2 * (c % 2)], sc4[2 * (c % 2) + 1]
                    rstd(("head", "q", l, c), ("head_square", "q", l, c), ps3(psum_of[("head_square", "q", l, c)]), EPS)
                    rotate(("q", l, c), x, v3(y), ps3(psum_of[("rotated", "q", l, c)]), v3(trig1[:, 1, :]))
                    step(dve.tensor_tensor(x, x, y, ALU.add))
                    dve.tensor_tensor(x, x, tm[:, 2, :], ALU.mult).then_inc(*S.inc("roped", "q", l, c))
                    stack_q("q", (l, c), x, lambda hh, rows: QS[rows, 2 * c + hh, :])
                rotate(("ki", l), None, v3(tm[lo64, 3, :]), ps3(psum_of[("rotated", "ki", l)], lo64), v3(trig1[lo64, 1, :]))
                dve.tensor_tensor(tm[lo64, 2, :], tm[lo64, 2, :], tm[lo64, 3, :], ALU.add)\
                    .then_inc(*S.inc("roped", "ki", l))
                split_k("ki", l, tm[lo64, 2, :])
                wait(("w_ready", l))
                nrelu = 0
                for c in range(4):
                    rotate(("qi", l, c), None, v3(tm[:, 3, :]), ps3(psum_of[("rotated", "qi", l, c)]), v3(trig1[:, 1, :]))
                    dve.tensor_tensor(tm[:, 2, :], tm[:, 2, :], tm[:, 3, :], ALU.add)\
                        .then_inc(*S.inc("roped", "qi", l, c))
                    stack_q("qi", (l, c), tm[:, 2, :], lambda hh, rows: QIPB[rows, 2 * (c % 2) + hh, :])
                    for hh in range(2):
                        for j in range(1, NQ):
                            n, h = visible(j), 2 * c + hh
                            sc = SC[:, SCORE_AT[j]:SCORE_AT[j] + n]
                            wait(("relued", l, c, hh, j))
                            r, w = tm[:, nrelu % 2, 0:n], widx[:, j, h:h + 1]
                            if h == 0:
                                ins = dve.tensor_scalar(sc, r, w, None, ALU.mult)
                            else:
                                wait(("score_added", l, *score_units[nrelu - (NQ - 1)]))
                                ins = dve.scalar_tensor_tensor(sc, r, w, sc, ALU.mult, ALU.add)
                            ins.then_inc(*S.inc("score_added", l, c, hh, j))
                            nrelu += 1
                hidden = {j: SC[0:HD, SCORE_AT[j] + visible(j) - CHUNK:SCORE_AT[j] + visible(j)] for j in range(1, NQ)}
                wait(("score_added", l, *score_units[-1]))
                for j in range(1, NQ):
                    dve.memset(hidden[j], NEG).then_inc(*S.inc("hidden_keys", l, j))
                rounds = [(r, j) for r in range(TOPK // 8) for j in range(1, NQ)]
                for x in range(len(rounds) + 1):
                    if x < len(rounds):
                        r, j = rounds[x]
                        wait(("taken", l, r - 1, j) if r else ("hidden_keys", l, j))
                        dve.max(top8[:, j, :], SC[:, SCORE_AT[j]:SCORE_AT[j] + visible(j)])\
                            .then_inc(*S.inc("eight", l, r, j))
                    if x >= 1:
                        r, j = rounds[x - 1]
                        sc = SC[:, SCORE_AT[j]:SCORE_AT[j] + visible(j)]
                        wait(("eight", l, r, j))
                        dve.match_replace(sc, top8[:, j, :], sc, TAKEN).then_inc(*S.inc("taken", l, r, j))
                    if x == 3 * (NQ - 1):
                        rstd(("head", "k", l), ("head_square", "k", l), ps3(psum_of[("head_square", "k", l)], lo64), EPS,
                             lo64)
                        rotate(("k", l), None, v3(tm[lo64, 1, :]), ps3(psum_of[("rotated", "k", l)], lo64),
                               v3(trig1[lo64, 1, :]))
                        step(dve.tensor_tensor(tm[lo64, 1, :], tm[lo64, 1, :], tm[lo64, 2, :], ALU.add))
                        dve.tensor_tensor(tm[lo64, 1, :], tm[lo64, 1, :], tm[lo64, 0, :], ALU.mult)\
                            .then_inc(*S.inc("roped", "k", l))
                        split_k("k", l, tm[lo64, 1, :])
                for j in range(1, NQ):
                    sc = SC[:, SCORE_AT[j]:SCORE_AT[j] + visible(j)]
                    wait(("taken", l, TOPK // 8 - 1, j))
                    dve.tensor_scalar(sc, sc, TAKEN / 2, NEG, ALU.is_gt, ALU.mult).then_inc(*S.inc("mask_made", l, j))
                for j in range(1, NQ):
                    wait(("mask_made", l, j))
                    dve.memset(hidden[j], NEG).then_inc(*S.inc("mask_ready", l, j))

                def gate(u, bank):
                    c, slot = u["c"], tm[:, 2 + u["c"] % 2, :]
                    if u["q0"] == 0:
                        wait((f"silu_in{c % 2}", l, c), ("attn_lo", l, c - 2) if c >= 2 else ("ma_out1", l, 7))
                        dve.memset(slot[:, T:TP], 0.0).then_inc(*S.inc("attn_padded", l, c))
                    wait(("out_turned", u["i"]))
                    cols = slice(u["q0"], u["q0"] + u["nq"])
                    dve.tensor_tensor(slot[:, cols], bank[:, P:P + u["nq"]], tm[:, c % 2, cols], ALU.mult)\
                        .then_inc(*S.inc("gated", u["i"]))

                attention(phases[("a", l)], lambda u: [("mask_ready", l, NQ - 1), ("mask0_in", l)], gate)
                for m in range(8):
                    t = tm[:, m % 2, :]
                    wait(("projected", ("ya", l, m)), (f"mix_in{m % 2}", "b", l, m))
                    dve.tensor_tensor(v3(t), ps3(psum_of[("ya", l, m)]), v3(t), ALU.mult)\
                        .then_inc(*S.inc("mix_gated", l, m))
                    wait(("mix_gated", l, m))
                    dve.tensor_tensor(t, t, tm[:, 2 + m % 2, :], ALU.add).then_inc(*S.inc("mixed", l, m))
                for m in range(8):
                    wait(("projected", ("out", l, m)), (f"x_old{m % 2}", l, m))
                    dve.tensor_tensor(v3(X[:, m, :]), ps3(psum_of[("out", l, m)]), v3(tm[:, 2 + m % 2, :]), ALU.add)\
                        .then_inc(*S.inc("residual", l, m))

            def ln(i, c0):
                cols = slice(c0, c0 + SEQ)
                wait(("mean", i))
                for c in range(KC):
                    x = X[:, c, cols]
                    dve.tensor_tensor(x, x, ps2(psum_of[("mean", i)]), ALU.subtract).then_inc(*S.inc("centered", i, c))
                rstd(("ln", i), ("mean_square", "ln", i), ps2(psum_of[("mean_square", "ln", i)]), LN_EPS, cols=SEQ)
                for c in range(KC):
                    x = X[:, c, cols]
                    dve.scalar_tensor_tensor(x, x, ln_g[:, i, c:c + 1], tm[:, 0, 0:SEQ], ALU.mult, ALU.mult)\
                        .then_inc(*S.inc("scaled", i, c))

            ln(0, META)

            def gate2(kind):
                def gate(u, bank):
                    c = u["c"]
                    k = c + (4 if kind == "s" else 0)
                    if u["q0"] == 0 and k >= 2:
                        wait((f"attn_out{k % 2}", k - 2))
                    wait(("out_turned", u["i"]))
                    dve.tensor_copy(tm[:, c % 2, u["q0"]:u["q0"] + P], bank[:, P:2 * P]).then_inc(*S.inc("gated", u["i"]))
                return gate

            for c in range(4):
                stack_q("naq", (c,), tm[:, 3, 0:SEQ], lambda hh, rows: Q2[rows, hh, :])
                for hh in range(2):
                    for half in range(2):
                        own = slice(hh * HD, (hh + 1) * HD)
                        wait(("k_hi", "nak", c, hh, half), ("k_hi", "nak", c, hh, 1))
                        dve.tensor_tensor(K2[half * HD:(half + 1) * HD, hh, 1, :], tm[own, 2, 0:SEQ],
                                          K2[own, hh, 0, :].bitcast(F32), ALU.subtract)\
                            .then_inc(*(S.inc("k_split", "nak", c) if hh and half else S.inc("k_splitting", "nak", c, hh, half)))
                attention([u for u in phases[("n",)] if u["c"] == c],
                          lambda u: [("bias_ready", c, 1), ("ln_saved", KC - 1), ("normed_lo", "ln", 0, KC - 1)], gate2("n"))
            for c in range(-1, 4):
                key = ("swk", 0) if c < 0 else ("swq", c)
                rotate(key, None, tm[:, 3, 0:SEQ], ps2(psum_of[("rotated", *key)]), trig2[:, 1, :])
                dve.tensor_tensor(tm[:, 2, 0:SEQ], tm[:, 2, 0:SEQ], tm[:, 3, 0:SEQ], ALU.add)\
                    .then_inc(*S.inc("roped", *key))
                if c < 0:
                    for hh in range(2):
                        for half in range(2):
                            own = slice(hh * HD, (hh + 1) * HD)
                            wait(("k_hi", "swk", 0, hh, 1))
                            dve.tensor_tensor(K2[half * HD:(half + 1) * HD, hh, 1, :], tm[own, 2, 0:SEQ],
                                              K2[own, hh, 0, :].bitcast(F32), ALU.subtract)\
                                .then_inc(*(S.inc("k_split", "swk", 0) if hh and half else
                                            S.inc("k_splitting", "swk", 0, hh, half)))
                    continue
                stack_q("swq", (c,), tm[:, 2, 0:SEQ], lambda hh, rows: Q2[rows, hh, :])
                attention([u for u in phases[("s",)] if u["c"] == c], lambda u: [("sink8",)], gate2("s"))
            for m in range(8):
                t, t2 = tm[:, m % 2, 0:SEQ], tm[:, 2 + m % 2, 0:SEQ]
                wait(("projected", ("y1", m)), (f"mix2_in{m % 2}", "b", m))
                dve.tensor_tensor(t, ps2(psum_of[("y1", m)]), t, ALU.mult).then_inc(*S.inc("y1_gated", m))
                wait(("projected", ("y2", m)))
                dve.tensor_tensor(t2, ps2(psum_of[("y2", m)]), t2, ALU.mult).then_inc(*S.inc("y2_gated", m))
                wait(("y1_gated", m), ("y2_gated", m))
                dve.tensor_tensor(t, t, t2, ALU.add).then_inc(*S.inc("mixed2", m))
            for m in range(8):
                wait(("projected", ("out2", m)), (f"h_old{m % 2}", m))
                x = X[:, m, 0:SEQ]
                step(dve.scalar_tensor_tensor(x, tm[:, 2 + m % 2, 0:SEQ], ALPHA, ps2(psum_of[("out2", m)]),
                                              ALU.mult, ALU.add))
                dve.tensor_scalar(x, x, b_o[:, 0, m:m + 1], None, ALU.add).then_inc(*S.inc("residual2", m))
            wait(("residual2", 7))
            ln(1, 0)
            for f in range(4):
                for m in range(8):
                    x = X[:, m, 0:SEQ]
                    wait(("projected", ("ff2", f, m)))
                    if f == 0:
                        step(dve.scalar_tensor_tensor(x, x, ALPHA, ps2(psum_of[("ff2", f, m)]), ALU.mult, ALU.add))
                        dve.tensor_scalar(x, x, b_o[:, 1, m:m + 1], None, ALU.add).then_inc(*S.inc("residual3", f, m))
                    else:
                        wait(("residual3", f - 1, m))
                        dve.tensor_tensor(x, x, ps2(psum_of[("ff2", f, m)]), ALU.add).then_inc(*S.inc("residual3", f, m))
            wait(("residual3", 3, 7))
            ln(2, 0)

        return S.seen


def constants():
    f = np.float32
    c = {"c_ident": np.eye(P, dtype=f)}

    def rotation(half, period):
        r = np.zeros((P, P), f)
        for m in range(P):
            d = m % HD
            if d < half:
                r[m + half, m] = -1.0
            elif d < period:
                r[m - half, m] = 1.0
        return r

    c["c_rot1"], c["c_rot2"] = rotation(HD // 2, HD), rotation(8, 16)
    c["c_headmean"] = np.kron(np.eye(2), np.full((HD, HD), 1.0 / HD)).astype(f)
    c["c_allmean"] = np.full((P, P), 1.0 / D, f)

    def trig(theta, dim, length, cols):
        inv = (f(1.0) / (f(theta) ** (np.arange(0, dim, 2, dtype=f) / f(dim)))).astype(f)
        ang = (np.arange(length, dtype=f)[:, None] * inv[None, :]).astype(f)
        t = np.zeros((P, 2, cols), f)
        t[:, 0, :] = 1.0
        for p in range(P):
            d = p % HD
            if d < dim:
                t[p, 0, :length] = np.cos(ang[:, d % (dim // 2)])
                t[p, 1, :length] = np.sin(ang[:, d % (dim // 2)])
        return t

    c["c_trig1"] = trig(10000.0, HD, T, TP)
    c["c_trig2"] = trig(500000.0, 16, SEQ, SEQ)
    edge = np.ones((P, 4, 16), f)
    for g, w in enumerate(WINDOWS):
        edge[:, g, :] = w / np.minimum(np.arange(1, 17), w)
    c["c_edge"] = edge
    m0 = np.zeros((P, visible(0)), f)
    m0[0:HD, visible(0) - CHUNK:] = NEG
    c["c_mask0"] = m0
    col = np.full((P, 14, GRID), NEG, f)
    for p in range(P):
        s = min(max(p % GRID - 8, 0), GRID - 16)
        col[p, :, s:s + 16] = 0.0
    c["c_colmask"] = col
    row = np.zeros((P, 9, GRID), f)
    row[0:GRID, 8, :] = NEG
    row[GRID:, 0, :] = NEG
    c["c_rowmask"] = row
    k, q = np.arange(3 * P)[None, :] - P, np.arange(P)[:, None]
    c["c_swmask"] = np.where(np.abs(k - q) <= P, 0.0, NEG).astype(f)
    return c


def kernel(**inputs):
    import concourse.bacc as bacc
    from concourse.bass_utils import run_bass_kernel_spmd as run

    arrays = {k: np.ascontiguousarray(v) for k, v in inputs.items()}
    arrays.update(constants())

    def build(known):
        nc = bacc.Bacc("TRN2", target_bir_lowering=False, num_devices=1)
        a = {k: nc.dram_tensor(f"in_{k}", v.shape, F32, kind="ExternalInput").ap() for k, v in arrays.items()}
        a["out"] = nc.dram_tensor("out_0", (1, SEQ, D), F32, kind="ExternalOutput").ap()
        return nc, program(nc, a, known)

    _, counts = build(None)
    nc, _ = build(counts)
    r = run(nc, [{f"in_{k}": v for k, v in arrays.items()}], core_ids=[0])
    return r.results[0]["out_0"]
```

```python
from contextlib import ExitStack

import numpy as np
import concourse.bass as bass
from concourse import mybir

F32 = mybir.dt.float32
F32R = mybir.dt.float32r
ALU = mybir.AluOpType
ACT = mybir.ActivationFunctionType
P = 128
D = 1024
KC = D // P
SEQ = 1024
META = 16
T = SEQ + META
TP = 1044
PIECE1 = TP // 3
DEPTH = 2
HEADS, HD = 8, 64
CHUNK, TOPK = 64, 256
NQ = SEQ // P
WINDOWS = (2, 4, 8, 16)
EPS, LN_EPS = 1e-6, 1e-5
NEG = -1e30
TAKEN = -3e38
ALPHA = 2.0 ** 0.25
FF = 4 * D
RAW = 2
GRID = 64
BANK = 512
SCALE = HD ** -0.5
IDX_SCALE = (HEADS ** -0.5) * (HD ** -0.5)
Q0, K0, GA0, U0, GB0, QI0, KI0, MG0 = 0, 512, 640, 1152, 1664, 2176, 2688, 2760
NAQ0, NAK0, NAV0, SWQ0, SWK0, SWV0, MG2 = 0, 512, 1024, 1536, 2048, 2176, 2304


def visible(j):
    return META + P * (j + 1)


SCORE_AT = {}
_at = 0
for _j in range(1, NQ):
    SCORE_AT[_j] = _at
    _at += visible(_j)
SCORE_COLS = _at


class Signals:

    def __init__(self, ctx, nc, known):
        self.ctx, self.nc, self.known = ctx, nc, known
        self.sems, self.count, self.seen = {}, {}, {}

    def sem(self, name):
        if name not in self.sems:
            self.sems[name] = self.ctx.enter_context(self.nc.semaphore(name))
            self.count[name] = 0
        return self.sems[name]

    def inc(self, name, *key, by=1):
        s = self.sem(name)
        self.count[name] += by
        assert (name, *key) not in self.seen, (name, key)
        self.seen[(name, *key)] = self.count[name]
        return s, by

    def dma(self, name, *key):
        return self.inc(name, *key, by=16)

    def at(self, name, *key):
        if self.known is not None:
            return self.sem(name), self.known[(name, *key)]
        return self.sem(name), 1


def program(nc, a, known):
    ctx = ExitStack()
    with ctx:
        S = Signals(ctx, nc, known)

        def sb(name, shape, dt=F32, into=ctx):
            return into.enter_context(nc.sbuf_tensor(name, shape, dt))

        ident = sb("ident", [P, P])
        rot1 = sb("rot1", [P, P])
        rot2 = sb("rot2", [P, P])
        headmean = sb("headmean", [P, P])
        allmean = sb("allmean", [P, P])
        gain = sb("gain", [P, DEPTH, KC])
        qk_gain = sb("qk_gain", [P, DEPTH, 2])
        pool_b = sb("pool_b", [P, DEPTH, 4])
        pool_s = sb("pool_s", [P, DEPTH, 4])
        pool_bs = sb("pool_bs", [P, DEPTH, 4])
        edge = sb("edge", [P, 4, 16])
        ln_g = sb("ln_g", [P, 3, KC])
        ln_b = sb("ln_b", [P, 3, KC])
        b_in2 = sb("b_in2", [P, 34])
        b_ff1 = sb("b_ff1", [P, FF // P])
        b_o = sb("b_o", [P, 2, KC])
        sink = sb("sink", [P, 2, HEADS])
        top8 = sb("top8", [P, NQ, 8])
        widx = sb("widx", [P, NQ, HEADS])
        negmax = sb("negmax", [P, 4])
        rowsum = sb("rowsum", [P, 4])
        sinkexp = sb("sinkexp", [P, 4])
        rowinv = sb("rowinv", [P, 4])
        zeros = sb("zeros", [2, 64])
        raw = sb("raw", [P, RAW, KC * P])
        wsp = sb("wsp", [P, 2, 2, KC * P], F32R)
        tm = sb("tm", [P, 4, TP])
        H = sb("H", [P, 2, KC, TP], F32R)
        X = sb("X", [P, KC, TP])
        QS = sb("QS", [P, KC, TP], F32R)
        KK = sb("KK", [P, 2, TP], F32R)
        V = sb("V", [P, 9, HD])
        SC = sb("SC", [P, SCORE_COLS])

        def over(first, names):
            out, at = [], first
            for name, shape, dt in names:
                at = -(-at // 32) * 32
                out.append(nc.alloc_sbuf_tensor_at(name, shape, dt, offset=at))
                at += 4 * int(np.prod(shape[1:]))
            return out

        x_at, chunk = nc.sbuf_base - 4 * (2 * KC * TP + 2 * TP + 9 * HD + SCORE_COLS), 4 * TP
        z_at = x_at + KC * chunk
        QIPB, = over(x_at, [("QIPB", [P, KC, TP], F32R)])
        trig1, pw = over(x_at + 5 * chunk, [("trig1", [P, 2, TP], F32), ("pw", [P, 4, P], F32)])
        k_roped, = over(x_at + 4 * chunk, [("k_roped", [P, TP], F32)])
        Lb, Pb, PT, Ob, mask0 = over(x_at, [("Lb", [P, 2, 1040], F32), ("Pb", [P, 2, 9 * P], F32),
                                            ("PT", [P, 2, 9, P], F32), ("Ob", [P, 2, P], F32),
                                            ("mask0", [P, visible(0)], F32)])
        Q2, K2, V2, bias_e, bias_i, colmask, rowmask, swmask, trig2 = over(z_at, [
            ("Q2", [P, 2, SEQ], F32R), ("K2", [P, 2, 2, SEQ], F32R), ("V2", [P, NQ, P], F32),
            ("bias_e", [P, 2, 14, GRID], F32), ("bias_i", [P, 2, 9, GRID], F32), ("colmask", [P, 14, GRID], F32),
            ("rowmask", [P, 9, GRID], F32), ("swmask", [P, 3 * P], F32), ("trig2", [P, 2, SEQ], F32)])
        sb("z_rest", [P, (2 * KC * SEQ - KC * TP - 2 * TP - 9 * HD - SCORE_COLS)])
        norm_sums, = over(z_at, [("norm_sums", [P, 2, TP], F32)])
        SP2, = over(z_at, [("SP2", [P, 2, KC, SEQ], F32R)])

        big = [ctx.enter_context(nc.psum_tensor(f"big{i}", [P, 3 * BANK], F32)) for i in range(2)]
        small = [ctx.enter_context(nc.psum_tensor(f"small{i}", [P, BANK], F32)) for i in range(2)]

        def dram(name, shape):
            return nc.dram_tensor(name, shape, F32, kind="Internal").ap()

        xT_d = dram("xT_scratch", [KC, P, TP])
        ga_d = dram("gate_a_scratch", [KC, P, TP])
        gb_d = dram("gate_b_scratch", [KC, P, TP])
        sg_d = dram("silu_scratch", [4, P, TP])
        at_d = dram("attention_scratch", [KC, P, SEQ])
        rpb_d = dram("rpb_scratch", [64 + HEADS * 15 * 31 + 64])
        band_d = dram("band_scratch", [HEADS, 15, GRID, GRID])

        tm_flat = [tm[:, i, :] for i in range(4)]

        def ps3(s, rows=slice(0, P)):
            return big[s][rows, :].rearrange("p (b n) -> p b n", b=3)[:, :, 0:PIECE1]

        def v3(ap):
            return ap.rearrange("p (b n) -> p b n", b=3)

        def ps2(s, rows=slice(0, P)):
            return big[s][rows, 0:SEQ]

        pieces1 = [(i * BANK, i * PIECE1, PIECE1) for i in range(3)]
        pieces2 = [(i * BANK, i * BANK, BANK) for i in range(2)]

        loads = []

        def wsrc(w, l, col, n, rows):
            return w[l][:, col:col + n].rearrange("(k p) n -> p k n", p=P), n, rows

        for l in range(DEPTH):
            for c in range(4):
                loads.append((("q", l, c), *wsrc(a["w_in"], l, Q0 + c * P, P, 8)))
            loads.append((("ki", l), *wsrc(a["w_in"], l, KI0, 72, 8)))
            loads.append((("kv", l), *wsrc(a["w_in"], l, K0, P, 8)))
            for c in range(4):
                loads.append((("qi", l, c), *wsrc(a["w_in"], l, QI0 + c * P, P, 8)))
            loads.append((("gatea", l, 0), *wsrc(a["w_in"], l, GA0, P, 8)))
            for g in range(4):
                loads.append((("u", l, g), *wsrc(a["w_in"], l, U0 + g * P, P, 8)))
                loads.append((("gateb", l, g), *wsrc(a["w_in"], l, GB0 + g * P, P, 8)))
            for c in range(1, 4):
                loads.append((("gatea", l, c), *wsrc(a["w_in"], l, GA0 + c * P, P, 8)))
            for m in range(8):
                loads.append((("mb", l, m), *wsrc(a["w_in"], l, MG0 + D + m * P, P, 8)))
                loads.append((("yb", l, m), *wsrc(a["w_branch_b"], l, m * P, P, 4)))
            for m in range(8):
                loads.append((("ma", l, m), *wsrc(a["w_in"], l, MG0 + m * P, P, 8)))
            for m in range(8):
                loads.append((("ya", l, m), *wsrc(a["w_branch_a"], l, m * P, P, 4)))
            for m in range(8):
                loads.append((("out", l, m), *wsrc(a["w_out"], l, m * P, P, 8)))
        w2 = a["w_in_2"]
        for m in range(12):
            loads.append((("m2", m), *wsrc(w2, 0, MG2 + m * P, P, 8)))
        for c in range(4):
            for what, col in (("naq", NAQ0), ("nak", NAK0), ("nav", NAV0)):
                loads.append(((what, c), *wsrc(w2, 0, col + c * P, P, 8)))
        for what, col in (("swk", SWK0), ("swv", SWV0)):
            loads.append(((what, 0), *wsrc(w2, 0, col, P, 8)))
        for c in range(4):
            loads.append((("swq", c), *wsrc(w2, 0, SWQ0 + c * P, P, 8)))
            loads.append((("m2", 12 + c), *wsrc(w2, 0, MG2 + (12 + c) * P, P, 8)))
        for m in range(8):
            loads.append((("y1", m), *wsrc(a["w_branch_na_2"], 0, m * P, P, 4)))
            loads.append((("y2", m), *wsrc(a["w_branch_swa_2"], 0, m * P, P, 4)))
        for m in range(8):
            loads.append((("out2", m), *wsrc(a["w_out_2"], 0, m * P, P, 8)))
        for f in range(4):
            for m in range(8):
                loads.append((("ff1", f, m), *wsrc(a["w_ff1_2"], 0, (8 * f + m) * P, P, 8)))
            for m in range(8):
                src = a["w_ff2_2"][0][f * D:(f + 1) * D, m * P:(m + 1) * P].rearrange("(k p) n -> p k n", p=P)
                loads.append((("ff2", f, m), src, P, 8))
        nload = {job: n for n, (job, *_) in enumerate(loads)}

        def units_first(l):
            for c in range(4):
                for j in [-1, *range(NQ)]:
                    for hh in range(2):
                        n = META if j < 0 else visible(j)
                        q0 = 0 if j < 0 else META + P * j
                        if j <= 0:
                            mask = mask0[:, 0:n] if j == 0 else mask0[:, 0:META]
                        else:
                            mask = SC[:, SCORE_AT[j]:SCORE_AT[j] + n]
                        qa = QS[:, 2 * c + hh, q0:q0 + P]
                        keys = [(o, min(BANK, n - o)) for o in range(0, n, BANK)]
                        kparts = [[(o, w, KK[:, part, o:o + w]) for o, w in keys] for part in range(2)]
                        kts = [(kt, min(P, n - kt * P), V[0:min(P, n - kt * P), kt, :])
                               for kt in range(-(-n // P))]
                        yield dict(block=("a", l), c=c, hh=hh, n=n, q=qa, k=kparts, mask=mask, kts=kts,
                                   sink=None, q0=q0, nq=META if j < 0 else P, h=2 * c + hh)

        def na_rows(t):
            r = 2 * t
            start = [min(max(x - 4, 0), 8) for x in (r, r + 1)]
            return start[0], start[1] + 8 - start[0]

        def units_na():
            for c in range(4):
                for t in range(NQ):
                    for hh in range(2):
                        r0, rows = na_rows(t)
                        n, k0 = rows * GRID, r0 * GRID
                        i0 = r0 - 2 * t + 7
                        m = bias_i[:, hh, :, :] if rows == 9 else bias_e[:, hh, i0 - 1:i0 - 1 + rows, :]
                        m = m.rearrange("p r c -> p (r c)")
                        keys = [(o, min(BANK, n - o)) for o in range(0, n, BANK)]
                        kparts = [[(o, w, K2[:, hh, part, k0 + o:k0 + o + w]) for o, w in keys] for part in range(2)]
                        kts = [(kt, min(P, n - kt * P), V2[0:min(P, n - kt * P), k0 // P + kt, hh * HD:hh * HD + HD])
                               for kt in range(-(-n // P))]
                        yield dict(block=("n",), c=c, hh=hh, n=n, q=Q2[:, hh, t * P:t * P + P], k=kparts, mask=m,
                                   kts=kts, sink=None, q0=t * P, nq=P, h=2 * c + hh, t=t)

        def units_swa():
            for c in range(4):
                for t in range(NQ):
                    for hh in range(2):
                        lo, hi = max(t - 1, 0), min(t + 2, NQ)
                        n, g = (hi - lo) * P, c // 2
                        kparts = [[(0, n, K2[:, g, part, lo * P:hi * P])] for part in range(2)]
                        kts = [(kt, P, V2[:, lo + kt, g * HD:g * HD + HD]) for kt in range(hi - lo)]
                        m0 = (lo - t + 1) * P
                        yield dict(block=("s",), c=c, hh=hh, n=n, q=Q2[:, hh, t * P:t * P + P], k=kparts,
                                   mask=swmask[:, m0:m0 + n], kts=kts, sink=2 * c + hh, q0=t * P, nq=P,
                                   h=2 * c + hh, t=t)

        phases = {("a", 0): list(units_first(0)), ("a", 1): list(units_first(1)),
                  ("n",): list(units_na()), ("s",): list(units_swa())}
        nunit = 0
        for units in phases.values():
            for u in units:
                u["i"] = nunit
                nunit += 1
        score_units = [(c, hh, j) for c in range(4) for hh in range(2) for j in range(1, NQ)]

        def bank_owner(u, kt):
            return "dve" if kt < len(u["kts"]) // 2 else "act"

        def place(u, kt):
            return kt if bank_owner(u, kt) == "dve" else BANK // P + kt - len(u["kts"]) // 2

        def halves_even(buf):
            return lambda part, k: buf[:, 2 * k + part, :]

        def moved_events(u):
            who = {bank_owner(u, kt) for kt, _, _ in u["kts"]}
            return [(f"moved_{e}", u["i"]) for e in sorted(who)]

        def moves(u, engine):
            kts = [k for k in u["kts"] if bank_owner(u, k[0]) == engine]
            full = [k[0] for k in kts if k[1] == P]
            return ([(full[0], len(full), P)] if full else []) + [(k[0], 1, k[1]) for k in kts if k[1] < P]

        def normed_lo(kind, i, c):
            by_dve = c % 2 if kind == "rms" else c in (3, 7)
            return ("normed_lo_dve" if by_dve else "normed_lo", kind, i, c)

        def ln_normed(i, c):
            return ("ln_normed_dve" if c % 2 else "ln_normed", i, c)

        def square_sums(key, cols):
            if key == ("ln", 2):
                return [tm[:, 2, cols], tm[:, 3, cols]]
            return [norm_sums[:, i, cols] for i in range(2)]

        sc4 = [SC[:, i * TP:(i + 1) * TP] for i in range(4)]

        psum_of = {}

        block = ctx.enter_context(nc.Block())

        @block.sync
        def _(sp):
            sp.dma_start(ident[:], a["c_ident"]).then_inc(*S.dma("identity"))
            consts = [(rot1[:], a["c_rot1"]), (rot2[:], a["c_rot2"]),
                      (headmean[:], a["c_headmean"]), (allmean[:], a["c_allmean"]),
                      (edge[:], a["c_edge"]),
                      (gain[:], a["norm_gain"].rearrange("l (k p) -> p l k", p=P)),
                      (pool_b[:], a["pool_b"].rearrange("l (k p) -> p l k", p=P)),
                      (pool_s[:], a["pool_scale"].rearrange("l (k p) -> p l k", p=P)),
                      (b_in2[:], a["b_in_2"][0].rearrange("(k p) -> p k", p=P)),
                      (b_ff1[:], a["b_ff1_2"][0].rearrange("(k p) -> p k", p=P)),
                      (b_o[:, 0, :], a["b_out_2"][0].rearrange("(k p) -> p k", p=P)),
                      (b_o[:, 1, :], a["b_ff2_2"][0].rearrange("(k p) -> p k", p=P)),
                      (sink[:, 0, :], bass.AP(a["swa_sink_2"].tensor, 0, [[0, P], [1, HEADS]]))]
            for i, name in enumerate(("ln0", "ln1", "ln2")):
                for dst, part in ((ln_g, "g"), (ln_b, "b")):
                    src = a[f"{name}_{part}_2"]
                    src = src if i == 0 else src[0]
                    consts.append((dst[:, i, :], src.rearrange("(k p) -> p k", p=P)))
            for half in range(2):
                for which, name in enumerate(("q_norm_gain", "k_norm_gain")):
                    consts.append((qk_gain[half * HD:(half + 1) * HD, :, which], a[name].rearrange("l d -> d l")))
            for i, (dst, src) in enumerate(consts):
                sp.dma_start(dst, src, allow_slow_non_contiguous=True).then_inc(*S.dma("constants", i))
            for n, (job, src, cols, rows) in enumerate(loads):
                if n == RAW:
                    sp.wait_ge(*S.at("constants", len(consts) - 1))
                    sp.nop().then_inc(*S.inc("constants_here"))
                if n >= RAW:
                    sp.wait_ge(*S.at("weight_lo", n - RAW))
                sp.dma_start(raw[:, n % RAW, :].rearrange("p (k n) -> p k n", k=KC)[:, 0:rows, 0:cols], src)\
                    .then_inc(*S.dma(f"weights{n % RAW}", n))
            sp.wait_ge(*S.at("output0", 6))
            sp.wait_ge(*S.at("output1", 7))

        @block.tensor
        def _(pe):
            free = {0: None, 1: None}
            turn = [0]

            def claim(key, emptied_by):
                s = psum_of[key] = turn[0] % 2
                turn[0] += 1
                if free[s] is not None:
                    for e in free[s]:
                        pe.wait_ge(*S.at(*e))
                free[s] = emptied_by
                return s

            def project(job, rhs, pieces, emptied_by, parts=None):
                n = nload[job]
                _, _, cols, rows = loads[n]
                s = claim(job, emptied_by)
                pe.wait_ge(*S.at("weight_lo", n))
                w = [wsp[:, n % 2, part, :].rearrange("p (k n) -> p k n", k=KC) for part in range(2)]
                mm = None
                for k in range(rows):
                    if parts is not None:
                        pe.wait_ge(*S.at(*parts(k)))
                    for i, (wp, xp) in enumerate(((0, 0), (0, 1), (1, 0))):
                        for o, t0, width in pieces:
                            mm = pe.matmul(big[s][0:cols, o:o + width], w[wp][:, k, 0:cols],
                                           rhs(xp, k)[:, t0:t0 + width],
                                           start=(k == 0 and i == 0), stop=(k == rows - 1 and i == 2))
                mm.then_inc(*S.inc("projected", job))

            def plain(name, key, lhsT, rhs_list, pieces, emptied_by, waits, rows=P):
                s = claim((name, *key), emptied_by)
                mm = None
                for i, rhs in enumerate(rhs_list):
                    pe.wait_ge(*S.at(*waits[i]))
                    for o, t0, width in pieces:
                        mm = pe.matmul(big[s][0:rows, o:o + width], lhsT, rhs[:, t0:t0 + width],
                                       start=(i == 0), stop=(i == len(rhs_list) - 1))
                    if i < len(rhs_list) - 1:
                        mm.then_inc(*S.inc(name + "_part", *key, i))
                mm.then_inc(*S.inc(name, *key))

            def attention(units):
                def scores(u):
                    if u["i"] >= 1 and u is not units[0]:
                        pe.wait_ge(*S.at("masked", u["i"] - 1))
                    mm = None
                    for part in range(2):
                        for o, w, k in u["k"][part]:
                            mm = pe.matmul(big[0][:, o:o + w], u["q"], k, start=(part == 0), stop=(part == 1))
                    mm.then_inc(*S.inc("logits", u["i"]))

                def transposes(u, prev):
                    pe.wait_ge(*S.at("exped", u["i"]))
                    if prev is not None:
                        for e in moved_events(prev):
                            pe.wait_ge(*S.at(*e))
                    for kt, rows, _ in u["kts"]:
                        at = place(u, kt) * P
                        mm = pe.transpose(big[1][:, at:at + P], Pb[:, u["i"] % 2, kt * P:(kt + 1) * P],
                                          ident[:])
                    mm.then_inc(*S.inc("turned", u["i"]))

                def values(u, index):
                    for e in moved_events(u):
                        pe.wait_ge(*S.at(*e))
                    if index >= 2:
                        pe.wait_ge(*S.at("normed_out", u["i"] - 2))
                    if index >= 3 and u["hh"] == 1:
                        pe.wait_ge(*S.at("gated", u["i"] - 3))
                    for i, (kt, rows, v) in enumerate(u["kts"]):
                        mm = pe.matmul(small[u["hh"]][:, 0:HD], PT[0:rows, u["i"] % 2, kt, :], v,
                                       start=(i == 0), stop=(i == len(u["kts"]) - 1))
                    mm.then_inc(*S.inc("weighted", u["i"]))

                def turn_back(u0, u1, pair):
                    pe.wait_ge(*S.at("normed_out", u1["i"]))
                    pe.transpose(small[1][:, P:2 * P], Ob[:, pair % 2, :], ident[:])\
                        .then_inc(*S.inc("out_turned", u0["i"]))

                if units[0]["i"] > 0:
                    pe.wait_ge(*S.at("gated", units[0]["i"] - 2))
                for s in range(2):
                    for e in free[s] or []:
                        pe.wait_ge(*S.at(*e))
                for index in range(len(units) + 3):
                    if index < len(units):
                        scores(units[index])
                    if 1 <= index <= len(units):
                        transposes(units[index - 1], units[index - 2] if index >= 2 else None)
                    if index >= 3 and (index - 3) % 2 == 1:
                        turn_back(units[index - 4], units[index - 3], (index - 3) // 2)
                    if 2 <= index <= len(units) + 1:
                        values(units[index - 2], index - 2)
                last = units[-1]
                free[0] = [("masked", last["i"])]
                free[1] = moved_events(last)

            pe.wait_ge(*S.at("identity"))
            for j in range(NQ + 1):
                s = claim(("x", j), [("x_turned", j)])
                pe.wait_ge(*S.at(f"x_in{j % 4}", j))
                rows = META if j == 0 else P
                for c in range(KC):
                    mm = pe.transpose(big[s][:, c * P:c * P + rows], tm[0:rows, j % 4, c * P:(c + 1) * P],
                                      ident[0:rows, 0:rows])
                mm.then_inc(*S.inc("x_transposed", j))
            pe.wait_ge(*S.at("constants_here"))

            def mean_square(key, cols, pieces):
                sums = square_sums(key, cols)
                plain("mean_square", key, allmean[:], [*sums, tm[:, 1, cols], tm[:, 0, cols], tm[:, 1, cols]], pieces,
                      [("variance", *key)],
                      [("square_sum", *key, 4), ("square_sum_odd", *key, 3)] + [("squared", *key, c) for c in (5, 6, 7)])

            hi_lo = lambda buf: (lambda part, k: buf[:, part, k, :])
            halves = lambda buf: (lambda part, k: buf[:, 4 * part + k, :])
            for l in range(DEPTH):
                mean_square(("rms", l), slice(0, TP), pieces1)

                def head_norm_and_rotate(key, y, rows, sq):
                    if sq is not None:
                        plain("head_square", key, headmean[0:rows, 0:rows], [sq], pieces1,
                              [("variance", "head", *key)], [("head_squared", *key)], rows)
                    plain("rotated", key, rot1[0:rows, 0:rows], [y], pieces1, [("rot_times_sin", *key)],
                          [("raw_copied", *key)], rows)

                for c in range(5):
                    if c < 4:
                        project(("q", l, c), hi_lo(H), pieces1, [("raw_copied", "q", l, c)],
                                (lambda k: normed_lo("rms", l, k)) if c == 0 else None)
                    if c >= 1:
                        head_norm_and_rotate(("q", l, c - 1), sc4[2 * ((c - 1) % 2) + 1], P, sc4[2 * ((c - 1) % 2)])
                project(("ki", l), hi_lo(H), pieces1, [("w_copied", l)])
                project(("kv", l), hi_lo(H), pieces1, [("v_copied", l)])
                plain("rotated", ("ki", l), rot1[0:HD, 0:HD], [tm[0:HD, 3, :]], pieces1,
                      [("rot_times_sin", "ki", l)], [("raw_copied", "ki", l)], HD)
                s = claim(("w", l), [("w_ready", l)])
                pe.wait_ge(*S.at("w_copied", l))
                for j in range(1, NQ):
                    mm = pe.transpose(big[s][:, j * 8:(j + 1) * 8], tm[HD:HD + 8, 3, META + j * P:META + (j + 1) * P],
                                      ident[HD:HD + 8, HD:HD + 8])
                mm.then_inc(*S.inc("w_turned", l))
                project(("qi", l, 0), hi_lo(H), pieces1, [("raw_copied", "qi", l, 0)])
                head_norm_and_rotate(("k", l), sc4[1][0:HD], HD, sc4[0][0:HD])
                s = claim(("v", l), [("v_ready", l)])
                pe.wait_ge(*S.at("v_copied", l))
                for kt in range(9):
                    rows = min(P, T - kt * P)
                    mm = pe.transpose(big[s][0:rows, kt * HD:(kt + 1) * HD], sc4[1][HD:P, kt * P:kt * P + rows],
                                      ident[HD:P, HD:P])
                mm.then_inc(*S.inc("v_turned", l))
                for c in range(4):
                    plain("rotated", ("qi", l, c), rot1[:], [tm[:, 3, :]], pieces1,
                          [("rot_times_sin", "qi", l, c)], [("raw_copied", "qi", l, c)])
                    if c < 3:
                        project(("qi", l, c + 1), hi_lo(H), pieces1, [("raw_copied", "qi", l, c + 1)])
                    else:
                        project(("gatea", l, 0), hi_lo(H), pieces1, [("gatea_silu", l, 0)])
                    pe.wait_ge(*S.at("q_stacked", "qi", l, c))
                    pe.wait_ge(*S.at("k_split", "ki", l))
                    for hh in range(2):
                        for j in range(1, NQ):
                            n = visible(j)
                            s = claim(("index", l, c, hh, j), [("relued", l, c, hh, j)])
                            for part in range(2):
                                for o in range(0, n, BANK):
                                    w = min(BANK, n - o)
                                    mm = pe.matmul(big[s][:, o:o + w],
                                                   QIPB[:, 2 * (c % 2) + hh, META + j * P:META + (j + 1) * P],
                                                   KK[:, part, o:o + w], start=(part == 0), stop=(part == 1))
                            mm.then_inc(*S.inc("index_scores", l, c, hh, j))

                def pool_mix(g):
                    pe.wait_ge(*S.at("pool_weights", l))
                    plain("pool_mixed", (l, g), pw[:, g, :], [tm[:, 0, :]], pieces1, [("pool_scaled", l, g)],
                          [("pooled", l, g)])

                for g in range(4):
                    project(("u", l, g), hi_lo(H), pieces1, [("u_copied", l, g)])
                    if g:
                        pool_mix(g - 1)
                    project(("gateb", l, g), hi_lo(H), pieces1, [("gateb_silu", l, g)])
                for c in range(1, 4):
                    project(("gatea", l, c), hi_lo(H), pieces1, [("gatea_silu", l, c)])
                    if c == 1:
                        pool_mix(3)
                for m in range(8):
                    project(("mb", l, m), hi_lo(H), pieces1, [("mb_sigmoid", l, m)])
                    project(("yb", l, m), halves(QIPB), pieces1, [("yb_copied", l, m)],
                            (lambda k: ("pool_lo", l, k)) if m == 0 else None)
                for m in range(8):
                    project(("ma", l, m), hi_lo(H), pieces1, [("ma_sigmoid", l, m)])
                pe.wait_ge(*S.at("q_stacked", "q", l, 3))
                pe.wait_ge(*S.at("k_split", "k", l))
                pe.wait_ge(*S.at("v_ready", l))
                attention(phases[("a", l)])
                for m in range(8):
                    project(("ya", l, m), halves_even(QS), pieces1, [("mix_gated", l, m)],
                            (lambda k: ("attn_lo", l, k)) if m == 0 else None)
                for m in range(8):
                    project(("out", l, m), hi_lo(H), pieces1, [("residual", l, m)],
                            (lambda k: ("mix_lo", l, k)) if m == 0 else None)

            def layer_norm(i):
                sums = square_sums(("ln", i), slice(0, SEQ))
                last = (("residual", DEPTH - 1, 7), ("residual2", 7), ("residual3", 3, 7))[i]
                x7 = X[:, 7, META:META + SEQ] if i == 0 else X[:, 7, 0:SEQ]
                plain("mean", (i,), allmean[:], [sums[0], x7], pieces2, [("centered", i, KC - 1)],
                      [("x_sum", i, KC - 2), last])
                mean_square(("ln", i), slice(0, SEQ), pieces2)

            layer_norm(0)
            for m in range(12):
                project(("m2", m), hi_lo(H), pieces2, [("m2_sigmoid", m)],
                        (lambda k: normed_lo("ln", 0, k)) if m == 0 else None)

            def turn_values(what, c):
                s = claim(("v", what, c), [("v_ready", what, c)])
                pe.wait_ge(*S.at("v_biased", what, c))
                for kt in range(NQ):
                    mm = pe.transpose(big[s][:, kt * P:(kt + 1) * P], tm[:, (c + 1) % 2, kt * P:(kt + 1) * P], ident[:])
                mm.then_inc(*S.inc("v_turned", what, c))

            def before_na(c):
                project(("naq", c), hi_lo(H), pieces2, [("raw_copied", "naq", c)])
                project(("nak", c), hi_lo(H), pieces2, [("raw_copied", "nak", c)])
                project(("nav", c), hi_lo(H), pieces2, [("v_biased", "nav", c)])
                turn_values("nav", c)
                for e in (("q_stacked", "naq", c), ("k_split", "nak", c), ("v_ready", "nav", c)):
                    pe.wait_ge(*S.at(*e))

            def rotate2(key):
                plain("rotated", key, rot2[:], [tm[:, 3, :]], pieces2, [("rot_times_sin", *key)],
                      [("raw_copied", *key)])

            def by_chunk(kind, before):
                units = phases[(kind,)]
                for c in range(4):
                    part = [u for u in units if u["c"] == c]
                    before(c)
                    attention(part)

            by_chunk("n", before_na)
            project(("swk", 0), hi_lo(H), pieces2, [("raw_copied", "swk", 0)])
            rotate2(("swk", 0))
            project(("swv", 0), hi_lo(H), pieces2, [("v_biased", "swv", 0)])
            turn_values("swv", 0)

            def before_swa(c):
                project(("swq", c), hi_lo(H), pieces2, [("raw_copied", "swq", c)])
                rotate2(("swq", c))
                project(("m2", 12 + c), hi_lo(H), pieces2, [("m2_sigmoid", 12 + c)])
                for e in (("q_stacked", "swq", c), ("k_split", "swk", 0), ("v_ready", "swv", 0)):
                    pe.wait_ge(*S.at(*e))

            by_chunk("s", before_swa)
            for m in range(8):
                project(("y1", m), lambda part, k: SP2[:, part, k, :], pieces2, [("y1_gated", m)],
                        (lambda k: ("branches_lo", k)) if m == 0 else None)
                project(("y2", m), lambda part, k: SP2[:, part, 4 + k, :], pieces2, [("y2_gated", m)],
                        (lambda k: ("branches_lo", 4 + k)) if m == 0 else None)
            for m in range(8):
                project(("out2", m), hi_lo(H), pieces2, [("residual2", m)],
                        (lambda k: ("mix2_lo", k)) if m == 0 else None)
            layer_norm(1)
            for f in range(4):
                for m in range(8):
                    project(("ff1", f, m), hi_lo(H), pieces2, [("hidden_relu", f, m)],
                            (lambda k: normed_lo("ln", 1, k)) if f == m == 0 else None)
                for m in range(8):
                    project(("ff2", f, m), hi_lo(SP2), pieces2, [("residual3", f, m)],
                            (lambda k: ("hidden_lo", f, k)) if m == 0 else None)
            layer_norm(2)
            for t in range(NQ):
                s = claim(("final", t), [("out_copied", t)])
                for c in (KC - 2, KC - 1):
                    pe.wait_ge(*S.at(*ln_normed(2, c)))
                for c in range(KC):
                    mm = pe.transpose(big[s][:, c * P:(c + 1) * P], X[:, c, t * P:(t + 1) * P], ident[:])
                mm.then_inc(*S.inc("final_turned", t))


        def chain_temps(key):
            if key[0] in ("rms", "ln"):
                return [tm[:, i, :] for i in (2, 3, 0)]
            if key[1] == "q":
                return [tm[:, i, :] for i in (0, 1, 2)]
            return [tm[:, 0, :], tm[:, 1, :], sc4[2]]

        def weight_hi(act, n):
            if n < len(loads):
                job, _, cols, rows = loads[n]
                if n >= 2:
                    act.wait_ge(*S.at("projected", loads[n - 2][0]))
                act.wait_ge(*S.at(f"weights{n % RAW}", n))
                view = lambda ap: ap.rearrange("p (k n) -> p k n", k=KC)[:, 0:rows, 0:cols]
                act.activation(view(wsp[:, n % 2, 0, :]), view(raw[:, n % RAW, :]), ACT.Copy)\
                    .then_inc(*S.inc("weight_hi", n))

        def act_attention(act, units, per_chunk, chunk_done):
            for k in range(len(units) + 4):
                if k < len(units):
                    u, i = units[k], units[k]["i"]
                    act.wait_ge(*S.at("masked", i))
                    if i >= 2:
                        act.wait_ge(*S.at("turned", i - 2))
                    if i >= 4:
                        act.wait_ge(*S.at("normed_out", i - 4))
                    act.activation(Pb[:, i % 2, 0:u["n"]], Lb[:, i % 2, 0:u["n"]], ACT.Exp, bias=negmax[:, i % 4:i % 4 + 1],
                                   scale=-1.0, accum_out=rowsum[:, i % 4:i % 4 + 1]).then_inc(*S.inc("exped", i))
                    if u["sink"] is not None:
                        act.activation(sinkexp[:, i % 4:i % 4 + 1], negmax[:, i % 4:i % 4 + 1], ACT.Exp,
                                       bias=sink[:, 0, u["sink"]:u["sink"] + 1]).then_inc(*S.inc("sink_exped", i))
                if 1 <= k <= len(units):
                    move(act, units[k - 1], "act")
                if chunk_done and k >= per_chunk + 3 and (k - 3) % per_chunk == 0:
                    chunk_done((k - 3) // per_chunk - 1)

        def move(eng, u, who):
            parts, i = moves(u, who), u["i"]
            if not parts:
                return
            eng.wait_ge(*S.at("turned", i))
            if i >= 2:
                eng.wait_ge(*S.at("weighted", i - 2))
            for x, (kt, count, rows) in enumerate(parts):
                dst = PT[0:rows, i % 2, kt:kt + count, :]
                at = place(u, kt) * P
                src = big[1][0:rows, at:at + count * P].rearrange("p (k n) -> p k n", k=count)
                ins = eng.activation(dst, src, ACT.Copy) if who == "act" else eng.tensor_copy(dst, src)
                ins.then_inc(*(S.inc(f"moved_{who}", i) if x == len(parts) - 1 else S.inc(f"moved_{who}", i, "part", x)))

        @block.scalar
        def _(act):

            def after(job):
                weight_hi(act, nload[job] + 2)

            def root(key, rows=slice(0, P), cols=TP):
                sq, rt, y = chain_temps(key)
                act.wait_ge(*S.at("variance", *key))
                rt, sq, y = rt[rows, 0:cols], sq[rows, 0:cols], y[rows, 0:cols]
                act.activation(rt, sq, ACT.Ln).then_inc(*S.inc("rstd_part", *key, 0))
                act.wait_ge(*S.at("rstd_part", *key, 0))
                act.activation(y, rt, ACT.Exp, scale=-0.5).then_inc(*S.inc("rstd_part", *key, 1))
                act.wait_ge(*S.at("rstd_part", *key, 1))
                act.activation(rt, y, ACT.Square).then_inc(*S.inc("rough_squared", *key))

            for j in range(NQ + 1):
                act.wait_ge(*S.at("x_transposed", j))
                t0, rows = (0, META) if j == 0 else (META + (j - 1) * P, P)
                act.activation(X[:, :, t0:t0 + rows],
                               big[j % 2][:, 0:KC * P].rearrange("p (k n) -> p k n", k=KC)[:, :, 0:rows],
                               ACT.Copy).then_inc(*S.inc("x_turned", j))
            weight_hi(act, 0)
            weight_hi(act, 1)
            act.wait_ge(*S.at("constants_here"))
            for l in range(DEPTH):
                for i in range(4):
                    act.activation(pool_bs[:, l, i:i + 1], pool_b[:, l, i:i + 1], ACT.Copy,
                                   scale=pool_s[:, l, i:i + 1]).then_inc(*S.inc("pool_bias", l, i))
            act.activation(sink[:, 1, :], sink[:, 0, :], ACT.Copy, scale=-1.0).then_inc(*S.inc("minus_sink"))

            def split_hi(name, key, dst, src, waits):
                for w in waits:
                    act.wait_ge(*S.at(*w))
                act.activation(dst, src, ACT.Copy).then_inc(*S.inc(name, *key))

            def square(key, c, x, cols, waits):
                for w in waits:
                    act.wait_ge(*S.at(*w))
                if c == 7:
                    act.wait_ge(*S.at("mean_square_part", *key, 2))
                elif c >= 4:
                    act.wait_ge(*S.at("square_sum_odd" if c % 2 else "square_sum", *key, c - 2))
                dst = square_sums(key, cols)[c] if c < 2 else tm[:, c % 2, cols]
                act.activation(dst, x, ACT.Square).then_inc(*S.inc("squared", *key, c))

            for l in range(DEPTH):
                for c in range(KC):
                    if l == 0:
                        waits = [("x_turned", NQ), ("x_padded",)]
                    else:
                        act.wait_ge(*S.at("residual", l - 1, c))
                        after(("out", l - 1, c))
                        waits = [("mix_lo", l - 1, 4 + c)] if 2 <= c < 4 else []
                    square(("rms", l), c, X[:, c, :], slice(0, TP), waits)
                root(("rms", l))
                for c in range(KC):
                    split_hi("normed_hi", ("rms", l, c), H[:, 0, c, :], tm[:, 1 + c % 3, :], [("normed", "rms", l, c)])


                def split_q(name, key, src, dst, k, rows=2):
                    act.wait_ge(*S.at("roped", name, *key))
                    for hh in range(2):
                        part = slice(hh * HD, (hh + 1) * HD)
                        act.activation(dst[part, k + hh, :], src[part], ACT.Copy)\
                            .then_inc(*S.inc("q_hi", name, *key, hh))

                def split_k(name, key, src, dst_lo, dst_hi):
                    act.wait_ge(*S.at("roped", name, *key))
                    for half, dst in enumerate((dst_lo, dst_hi)):
                        act.activation(dst, src, ACT.Copy).then_inc(*S.inc("k_hi", name, *key, half))

                for c in range(5):
                    if c < 4:
                        s, x, y = psum_of[("q", l, c)], sc4[2 * (c % 2)], sc4[2 * (c % 2) + 1]
                        act.wait_ge(*S.at("projected", ("q", l, c)))
                        if c >= 2:
                            act.wait_ge(*S.at("q_stacked", "q", l, c - 2))
                        act.activation(v3(x), ps3(s), ACT.Square).then_inc(*S.inc("head_squared", "q", l, c))
                        act.activation(v3(y), ps3(s), ACT.Copy, scale=qk_gain[:, l, 0:1])\
                            .then_inc(*S.inc("raw_copied", "q", l, c))
                        after(("q", l, c))
                    if c >= 1:
                        root(("head", "q", l, c - 1))
                        split_q("q", (l, c - 1), sc4[2 * ((c - 1) % 2)], QS, 2 * (c - 1))
                s, lo64 = psum_of[("ki", l)], slice(0, HD)
                act.wait_ge(*S.at("projected", ("ki", l)))
                act.activation(v3(tm[lo64, 3, :]), ps3(s, lo64), ACT.Copy).then_inc(*S.inc("raw_copied", "ki", l))
                act.activation(v3(tm[HD:HD + 8, 3, :]), ps3(s, slice(HD, HD + 8)), ACT.Copy)\
                    .then_inc(*S.inc("w_copied", l))
                after(("ki", l))
                s = psum_of[("kv", l)]
                act.wait_ge(*S.at("projected", ("kv", l)))
                act.wait_ge(*S.at("q_stacked", "q", l, 2))
                act.activation(v3(sc4[0][lo64]), ps3(s, lo64), ACT.Square).then_inc(*S.inc("head_squared", "k", l))
                act.activation(v3(sc4[1][lo64]), ps3(s, lo64), ACT.Copy, scale=qk_gain[lo64, l, 1:2])\
                    .then_inc(*S.inc("raw_copied", "k", l))
                act.activation(v3(sc4[1][HD:P]), ps3(s, slice(HD, P)), ACT.Copy).then_inc(*S.inc("v_copied", l))
                after(("kv", l))
                split_k("ki", (l,), tm[lo64, 2, :], KK[0:HD, 0, :], KK[HD:P, 0, :])
                act.wait_ge(*S.at("w_turned", l))
                act.activation(widx[:, 1:NQ, :],
                               big[psum_of[("w", l)]][:, 8:NQ * 8].rearrange("p (j h) -> p j h", h=8), ACT.Copy,
                               scale=IDX_SCALE).then_inc(*S.inc("w_ready", l))

                def take_qi(c):
                    act.wait_ge(*S.at("projected", ("qi", l, c)))
                    act.wait_ge(*S.at("q_stacked", "qi", l, c - 1) if c else S.at("k_split", "ki", l))
                    act.activation(v3(tm[:, 3, :]), ps3(psum_of[("qi", l, c)]), ACT.Copy)\
                        .then_inc(*S.inc("raw_copied", "qi", l, c))
                    after(("qi", l, c))

                def gate_a(c, slot, wait):
                    act.wait_ge(*S.at("projected", ("gatea", l, c)))
                    act.wait_ge(*S.at(*wait))
                    act.activation(v3(tm[:, slot, :]), ps3(psum_of[("gatea", l, c)]), ACT.Silu)\
                        .then_inc(*S.inc("gatea_silu", l, c))
                    act.wait_ge(*S.at("gatea_silu", l, c))
                    act.dma_start(sg_d[c], tm[:, slot, :]).then_inc(*S.dma(f"gate_out{c % 2}", "a", l, c))
                    after(("gatea", l, c))

                take_qi(0)
                root(("head", "k", l), lo64)
                s = psum_of[("v", l)]
                act.wait_ge(*S.at("v_turned", l))
                act.activation(V[:, 0:8, :], big[s][:, 0:8 * HD].rearrange("p (k d) -> p k d", k=8), ACT.Copy)\
                    .then_inc(*S.inc("v_part", l))
                act.activation(V[0:META, 8, :], big[s][0:META, 8 * HD:9 * HD], ACT.Copy).then_inc(*S.inc("v_ready", l))
                nrelu = 0
                for c in range(4):
                    if c == 0:
                        act.wait_ge(*(S.at("x_saved", l - 1, 7) if l else S.at("x_stored")))
                    split_q("qi", (l, c), tm[:, 2, :], QIPB, 2 * (c % 2))
                    if c < 3:
                        take_qi(c + 1)
                    else:
                        gate_a(0, 3, ("roped", "qi", l, 3))
                    for hh in range(2):
                        for j in range(1, NQ):
                            n = visible(j)
                            act.wait_ge(*S.at("index_scores", l, c, hh, j))
                            if nrelu >= 2:
                                act.wait_ge(*S.at("score_added", l, *score_units[nrelu - 2]))
                            elif nrelu == 0:
                                act.wait_ge(*S.at("roped", "k", l))
                            act.activation(tm[:, nrelu % 2, 0:n], big[psum_of[("index", l, c, hh, j)]][:, 0:n], ACT.Relu)\
                                .then_inc(*S.inc("relued", l, c, hh, j))
                            nrelu += 1
                act.wait_ge(*S.at("index_scores", l, 3, 1, NQ - 1))
                split_k("k", (l,), k_roped[lo64, :], KK[0:HD, 0, :], KK[HD:P, 0, :])

                def pool_scale(g):
                    act.wait_ge(*S.at("pool_mixed", l, g))
                    act.wait_ge(*S.at("pool_bias", l, g))
                    act.activation(v3(tm[:, 1, :]), ps3(psum_of[("pool_mixed", l, g)]), ACT.Identity,
                                   scale=pool_s[:, l, g:g + 1], bias=pool_bs[:, l, g:g + 1])\
                        .then_inc(*S.inc("pool_scaled", l, g))
                    split_hi("pool_hi", (l, g), QIPB[:, g, :], tm[:, 1, :], [("pool_gated", l, g)])

                for g in range(4):
                    act.wait_ge(*S.at("projected", ("u", l, g)))
                    act.wait_ge(*S.at("score_added", l, *score_units[-1]) if g == 0 else S.at("pool_mixed", l, g - 1))
                    act.activation(v3(tm[:, 0, :]), ps3(psum_of[("u", l, g)]), ACT.Copy).then_inc(*S.inc("u_copied", l, g))
                    after(("u", l, g))
                    if g:
                        pool_scale(g - 1)
                    act.wait_ge(*S.at("projected", ("gateb", l, g)))
                    act.wait_ge(*S.at("pool_gated", l, g - 1) if g else S.at("gate_out0", "a", l, 0))
                    act.activation(v3(tm[:, 3, :]), ps3(psum_of[("gateb", l, g)]), ACT.Silu)\
                        .then_inc(*S.inc("gateb_silu", l, g))
                    after(("gateb", l, g))
                act.wait_ge(*S.at("projected", ("gatea", l, 1)))
                pool_scale(3)
                gate_a(1, 1, ("pool_lo", l, 3))
                gate_a(2, 0, ("pool_mixed", l, 3))
                gate_a(3, 1, ("gate_out1", "a", l, 1))
                for m in range(8):
                    act.wait_ge(*S.at("projected", ("mb", l, m)))
                    act.wait_ge(*S.at("yb_gated", l, m - 2) if m >= 2 else S.at(f"gate_out{m}", "a", l, m + 2))
                    act.activation(v3(tm[:, m % 2, :]), ps3(psum_of[("mb", l, m)]), ACT.Sigmoid)\
                        .then_inc(*S.inc("mb_sigmoid", l, m))
                    after(("mb", l, m))
                    act.wait_ge(*S.at("projected", ("yb", l, m)))
                    if m >= 2:
                        act.wait_ge(*S.at(f"yb_out{m % 2}", l, m - 2))
                    act.activation(v3(tm[:, 2 + m % 2, :]), ps3(psum_of[("yb", l, m)]), ACT.Copy)\
                        .then_inc(*S.inc("yb_copied", l, m))
                    after(("yb", l, m))
                for m in range(8):
                    act.wait_ge(*S.at("projected", ("ma", l, m)))
                    act.wait_ge(*S.at("yb_gated", l, 6 + m) if m < 2 else S.at(f"ma_out{m % 2}", l, m - 2))
                    act.activation(v3(tm[:, m % 2, :]), ps3(psum_of[("ma", l, m)]), ACT.Sigmoid)\
                        .then_inc(*S.inc("ma_sigmoid", l, m))
                    act.wait_ge(*S.at("ma_sigmoid", l, m))
                    act.dma_start(ga_d[m], tm[:, m % 2, :]).then_inc(*S.dma(f"ma_out{m % 2}", l, m))
                    after(("ma", l, m))

                def first_chunk_done(c):
                    split_hi("attn_hi", (l, c), QS[:, 2 * c, :], tm[:, 2 + c % 2, :],
                             [("gated", phases[("a", l)][18 * c + 16]["i"])])

                act_attention(act, phases[("a", l)], 18, first_chunk_done)
                for m in range(8):
                    act.wait_ge(*S.at("projected", ("ya", l, m)))
                    after(("ya", l, m))
                    split_hi("mix_hi", (l, m), H[:, 0, m, :], tm[:, m % 2, :], [("mixed", l, m)])

            def ln(i, c0, waits):
                for c in range(KC):
                    square(("ln", i), c, X[:, c, c0:c0 + SEQ], slice(0, SEQ),
                           [("centered", i, c)] + (waits if c < 4 else []))
                root(("ln", i), cols=SEQ)
                for c in range(KC):
                    if c % 2 == 0:
                        act.wait_ge(*S.at("scaled", i, c))
                        act.activation(X[:, c, c0:c0 + SEQ], X[:, c, c0:c0 + SEQ], ACT.Identity,
                                       bias=ln_b[:, i, c:c + 1]).then_inc(*S.inc("ln_normed", i, c))
                    if i < 2:
                        split_hi("normed_hi", ("ln", i, c), H[:, 0, c, 0:SEQ], X[:, c, c0:c0 + SEQ],
                                 [ln_normed(i, c)])

            for c in range(KC):
                act.wait_ge(*S.at("residual", DEPTH - 1, c))
                after(("out", DEPTH - 1, c))
            ln(0, META, [])
            def gate_m2(m, slot, wait):
                act.wait_ge(*S.at("projected", ("m2", m)))
                act.wait_ge(*S.at(*wait))
                act.activation(tm[:, slot, 0:SEQ], ps2(psum_of[("m2", m)]), ACT.Sigmoid,
                               bias=b_in2[:, MG2 // P + m:MG2 // P + m + 1]).then_inc(*S.inc("m2_sigmoid", m))
                act.wait_ge(*S.at("m2_sigmoid", m))
                act.dma_start((ga_d if m < 8 else gb_d)[m % 8][:, 0:SEQ], tm[:, slot, 0:SEQ])\
                    .then_inc(*S.dma(f"m2_out{slot}", m))
                after(("m2", m))

            for m in range(12):
                gate_m2(m, m % 2, (f"m2_out{m % 2}", m - 2) if m >= 2 else ("scaled", 0, KC - 1))

            def biased(what, c, col, slot, name, waits):
                act.wait_ge(*S.at("projected", (what, c)))
                for w in waits:
                    act.wait_ge(*S.at(*w))
                act.activation(tm[:, slot, 0:SEQ], ps2(psum_of[(what, c)]), ACT.Identity,
                               bias=b_in2[:, col // P + c:col // P + c + 1]).then_inc(*S.inc(name, what, c))
                after((what, c))

            def store_free(c, kind):
                k = c - 1 + (4 if kind == "s" else 0)
                return [(f"attn_out{k % 2}", k)] if k >= 0 else [("m2_out0", 10), ("m2_out1", 11)]

            def split_k2(what, c, src, waits):
                for w in waits:
                    act.wait_ge(*S.at(*w))
                for hh in range(2):
                    for half in range(2):
                        act.activation(K2[half * HD:(half + 1) * HD, hh, 0, :], src[hh * HD:(hh + 1) * HD, 0:SEQ], ACT.Copy)\
                            .then_inc(*S.inc("k_hi", what, c, hh, half))

            def split_q2(what, c, src, waits):
                for w in waits:
                    act.wait_ge(*S.at(*w))
                for hh in range(2):
                    part = slice(hh * HD, (hh + 1) * HD)
                    act.activation(Q2[part, hh, :], src[part, 0:SEQ], ACT.Copy).then_inc(*S.inc("q_hi", what, c, hh))

            def take_v(what, c):
                act.wait_ge(*S.at("v_turned", what, c))
                act.activation(V2[:, :, :], ps2(psum_of[("v", what, c)]).rearrange("p (k d) -> p k d", k=NQ), ACT.Copy)\
                    .then_inc(*S.inc("v_ready", what, c))

            for c in range(4):
                last = [("k_split", "nak", c - 1)] if c else []
                biased("naq", c, NAQ0, 3, "raw_copied", last + ([("q_stacked", "naq", c - 1)] if c else []))
                split_q2("naq", c, tm[:, 3, :], [("raw_copied", "naq", c)])
                biased("nak", c, NAK0, 2, "raw_copied", last)
                split_k2("nak", c, tm[:, 2, :], [("raw_copied", "nak", c)])
                biased("nav", c, NAV0, (c + 1) % 2, "v_biased", store_free(c, "n"))
                take_v("nav", c)
                act_attention(act, [u for u in phases[("n",)] if u["c"] == c], 16, None)
            biased("swk", 0, SWK0, 3, "raw_copied", [("q_stacked", "naq", 3), ("k_split", "nak", 3)])
            biased("swv", 0, SWV0, 1, "v_biased", store_free(0, "s"))
            split_k2("swk", 0, tm[:, 2, :], [("roped", "swk", 0)])
            take_v("swv", 0)
            for c in range(4):
                biased("swq", c, SWQ0, 3, "raw_copied", [("k_split", "swk", 0)] if c == 0 else [("q_stacked", "swq", c - 1)])
                split_q2("swq", c, tm[:, 2, :], [("roped", "swq", c)])
                gate_m2(12 + c, (c + 1) % 2, (f"attn_out{(c + 1) % 2}", 3 + c) if c else ("v_ready", "swv", 0))
                act_attention(act, [u for u in phases[("s",)] if u["c"] == c], 16, None)
            for k in range(8):
                split_hi("branches_hi", (k,), SP2[:, 0, k, :], tm[:, k % 2, 0:SEQ], [(f"attn_in{k % 2}", k)])
            for m in range(8):
                for job in (("y1", m), ("y2", m)):
                    act.wait_ge(*S.at("projected", job))
                    after(job)
                split_hi("mix2_hi", (m,), H[:, 0, m, 0:SEQ], tm[:, m % 2, 0:SEQ], [("mixed2", m)])
            for m in range(8):
                t = tm[:, 2 + m % 2, 0:SEQ]
                act.wait_ge(*S.at(f"h_old{m % 2}", m))
                act.activation(t, t, ACT.Identity, scale=ALPHA, bias=b_o[:, 0, m:m + 1]).then_inc(*S.inc("h_scaled", m))
                act.wait_ge(*S.at("projected", ("out2", m)))
                after(("out2", m))
            ln(1, 0, [("residual2", 7)])
            for f in range(4):
                for m in range(8):
                    act.wait_ge(*S.at("projected", ("ff1", f, m)))
                    n = f * 8 + m
                    if n >= 2:
                        act.wait_ge(*S.at("hidden_lo", (n - 2) // 8, (n - 2) % 8))
                    else:
                        act.wait_ge(*S.at("scaled", 1, KC - 1))
                    act.activation(tm[:, n % 2, 0:SEQ], ps2(psum_of[("ff1", f, m)]), ACT.Relu, bias=b_ff1[:, n:n + 1])\
                        .then_inc(*S.inc("hidden_relu", f, m))
                    after(("ff1", f, m))
                    act.wait_ge(*S.at("hidden_relu", f, m))
                    act.activation(tm[:, n % 2, 0:SEQ], tm[:, n % 2, 0:SEQ], ACT.Square)\
                        .then_inc(*S.inc("hidden_squared", f, m))
                    split_hi("hidden_hi", (f, m), SP2[:, 0, m, :], tm[:, n % 2, 0:SEQ], [("hidden_squared", f, m)])
                for m in range(8):
                    act.wait_ge(*S.at("projected", ("ff2", f, m)))
                    after(("ff2", f, m))
            ln(2, 0, [("hidden_lo", 3, 7), ("residual3", 3, 7)])
            for t in range(NQ):
                act.wait_ge(*S.at("final_turned", t))
                if t >= 2:
                    act.wait_ge(*S.at(f"output{t % 2}", t - 2))
                else:
                    act.wait_ge(*S.at("scaled", 2, KC - 1))
                act.activation(tm[:, t % 2, 0:D], ps2(psum_of[("final", t)]), ACT.Copy).then_inc(*S.inc("out_copied", t))
                act.wait_ge(*S.at("out_copied", t))
                act.dma_start(a["out"][0, t * P:(t + 1) * P, :], tm[:, t % 2, 0:D]).then_inc(*S.dma(f"output{t % 2}", t))

        @block.gpsimd
        def _(pool):
            def lo_part(ins, name, *key):
                ins.then_inc(*S.inc(name, *key))

            def subtract(name, key, dst, src, hi, waits):
                for w in waits:
                    pool.wait_ge(*S.at(*w))
                pool.tensor_tensor(dst, src, hi.bitcast(F32), ALU.subtract).then_inc(*S.inc(name, *key))

            def weight_lo(n):
                if n < len(loads):
                    _, _, cols, rows = loads[n]
                    view = lambda ap: ap.rearrange("p (k n) -> p k n", k=KC)[:, 0:rows, 0:cols]
                    subtract("weight_lo", (n,), view(wsp[:, n % 2, 1, :]), view(raw[:, n % RAW, :]),
                             view(wsp[:, n % 2, 0, :]), [("weight_hi", n)])

            def after(job):
                weight_lo(nload[job] + 2)

            def load(name, key, dst, src, waits):
                for w in waits:
                    pool.wait_ge(*S.at(*w))
                pool.dma_start(dst, src).then_inc(*S.dma(name, *key))

            store = load

            for j in range(NQ + 1):
                src = a["meta_tokens"] if j == 0 else a["x"][0, (j - 1) * P:j * P, :]
                load(f"x_in{j % 4}", (j,), tm[0:(META if j == 0 else P), j % 4, 0:D], src,
                     [("x_transposed", j - 4)] if j >= 4 else [])
            store("x_stored", (), xT_d.rearrange("k p n -> p k n"), X[:, :, :], [("x_turned", NQ), ("x_padded",)])
            weight_lo(0)
            weight_lo(1)

            def times_cos(key, dst, src, trig, waits):
                for w in waits:
                    pool.wait_ge(*S.at(*w))
                pool.tensor_tensor(dst, src, trig, ALU.mult).then_inc(*S.inc("times_cos", *key))

            def bands():
                pool.memset(zeros[:, :], 0.0).then_inc(*S.inc("zeros"))
                n_rpb = HEADS * 15 * 31
                store("rpb_pad", (0,), rpb_d[0:64].rearrange("(a n) -> a n", a=1), zeros[0:1, :], [("zeros",)])
                store("rpb_pad", (1,), rpb_d[64 + n_rpb:].rearrange("(a n) -> a n", a=1), zeros[0:1, :], [])
                store("rpb_pad", (2,), rpb_d[64:64 + n_rpb].rearrange("(a n) -> a n", a=8),
                      a["na_rpb_2"][0].rearrange("h i j -> h (i j)"), [])
                for h in range(HEADS):
                    src = bass.AP(rpb_d.tensor, 64 + h * 15 * 31 + 15, [[31, 15], [-1, GRID], [1, GRID]])
                    store("bands", (h,), band_d[h], src, [("rpb_pad", 2)])

            def add_square(key, cols, c):
                total = square_sums(key, cols)[1]
                pool.wait_ge(*S.at("squared", *key, 1))
                pool.wait_ge(*S.at("squared", *key, c))
                pool.tensor_tensor(total, total, tm[:, 1, cols], ALU.add).then_inc(*S.inc("square_sum_odd", *key, c))

            lo64 = slice(0, HD)
            for l in range(DEPTH):
                if l == 0:
                    add_square(("rms", l), slice(0, TP), 3)
                for c in range(0, KC, 2):
                    subtract("normed_lo", ("rms", l, c), H[:, 1, c, :], tm[:, 1 + c % 3, :], H[:, 0, c, :],
                             [("normed_hi", "rms", l, c)])
                x_read = [("normed", "rms", l, KC - 1), ("x_saved", l - 1, 7) if l else ("x_stored",)]
                load("pool_weights", (l,), pw[:, :, :], a["pool_w"][l].rearrange("g c d -> c g d"), x_read)
                load("rotary_tables", (l,), trig1[:, :, :], a["c_trig1"], [])
                if l == 0:
                    bands()
                pool.wait_ge(*S.at("rotary_tables", l))
                for c in range(5):
                    if c < 4:
                        after(("q", l, c))
                    if c >= 1:
                        x, y = sc4[2 * ((c - 1) % 2)], sc4[2 * ((c - 1) % 2) + 1]
                        times_cos(("q", l, c - 1), x, y, trig1[:, 0, :],
                                  [("raw_copied", "q", l, c - 1), ("head_square", "q", l, c - 1)])
                after(("ki", l))
                times_cos(("ki", l), tm[lo64, 2, :], tm[lo64, 3, :], trig1[lo64, 0, :],
                          [("raw_copied", "ki", l), ("q_stacked", "q", l, 3)])
                after(("kv", l))
                times_cos(("k", l), sc4[3][lo64], sc4[1][lo64], trig1[lo64, 0, :], [("raw_copied", "k", l)])
                after(("qi", l, 0))
                for c in range(4):
                    times_cos(("qi", l, c), tm[:, 2, :], tm[:, 3, :], trig1[:, 0, :],
                              [("raw_copied", "qi", l, c)])
                    after(("qi", l, c + 1) if c < 3 else ("gatea", l, 0))

                def pool_gate(g):
                    pool.wait_ge(*S.at("pool_scaled", l, g))
                    pool.wait_ge(*S.at("gateb_silu", l, g))
                    pool.tensor_tensor(tm[:, 1, :], tm[:, 1, :], tm[:, 3, :], ALU.mult)\
                        .then_inc(*S.inc("pool_gated", l, g))
                    subtract("pool_lo", (l, g), QIPB[:, 4 + g, :], tm[:, 1, :], QIPB[:, g, :],
                             [("pool_hi", l, g), ("k_split", "k", l)])

                for g, w in enumerate(WINDOWS):
                    after(("u", l, g))
                    if g:
                        pool_gate(g - 1)
                    pool.wait_ge(*S.at("u_copied", l, g))
                    if g:
                        pool.wait_ge(*S.at("pool_lo", l, g - 1))
                    src, d, slot = tm[:, 0, :], 1, 1
                    while d < w:
                        dst = tm[:, slot, :]
                        pool.tensor_copy(dst[:, 0:d], src[:, 0:d]).then_inc(*S.inc("window_step", l, g, "edge", d))
                        pool.tensor_tensor(dst[:, d:TP], src[:, d:TP], src[:, 0:TP - d], ALU.add)\
                            .then_inc(*S.inc("window_step", l, g, "sum", d))
                        pool.wait_ge(*S.at("window_step", l, g, "edge", d))
                        pool.wait_ge(*S.at("window_step", l, g, "sum", d))
                        src, d, slot = dst, 2 * d, 3 - slot
                    pool.tensor_tensor(src[:, 0:16], src[:, 0:16], edge[:, g, :], ALU.mult)\
                        .then_inc(*S.inc("window_step", l, g, "count"))
                    pool.wait_ge(*S.at("window_step", l, g, "count"))
                    pool.tensor_scalar(src, src, 1.0 / w, None, ALU.mult).then_inc(*S.inc("window_step", l, g, "mean"))
                    pool.wait_ge(*S.at("window_step", l, g, "mean"))
                    pool.tensor_tensor(tm[:, 0, :], src, tm[:, 0, :], ALU.subtract).then_inc(*S.inc("pooled", l, g))
                    after(("gateb", l, g))
                pool_gate(3)
                for c in range(1, 4):
                    after(("gatea", l, c))
                for m in range(8):
                    after(("mb", l, m))
                    after(("yb", l, m))
                    pool.wait_ge(*S.at("mb_sigmoid", l, m))
                    pool.wait_ge(*S.at("yb_copied", l, m))
                    y = tm[:, 2 + m % 2, :]
                    pool.tensor_tensor(y, y, tm[:, m % 2, :], ALU.mult).then_inc(*S.inc("yb_gated", l, m))
                    store(f"yb_out{m % 2}", (l, m), gb_d[m], y, [("yb_gated", l, m)])
                for m in range(8):
                    after(("ma", l, m))
                load("mask0_in", (l,), mask0[:, :], a["c_mask0"], [("projected", ("yb", l, 7))])
                units = phases[("a", l)]
                for c in range(4):
                    load(f"silu_in{c % 2}", (l, c), tm[:, c % 2, :], sg_d[c],
                         [(f"gate_out{c % 2}", "a", l, c),
                          (f"ma_out{c % 2}", l, 6 + c) if c < 2 else ("gated", units[18 * (c - 2) + 16]["i"])])
                    if c >= 1:
                        subtract("attn_lo", (l, c - 1), QS[:, 2 * c - 1, :], tm[:, 2 + (c - 1) % 2, :],
                                 QS[:, 2 * c - 2, :], [("attn_hi", l, c - 1)])
                subtract("attn_lo", (l, 3), QS[:, 7, :], tm[:, 3, :], QS[:, 6, :], [("attn_hi", l, 3)])
                for m in range(-2, 8):
                    if m >= 0:
                        after(("ya", l, m))
                        subtract("mix_lo", (l, m), H[:, 1, m, :], tm[:, m % 2, :], H[:, 0, m, :], [("mix_hi", l, m)])
                    n = m + 2
                    if n < 8:
                        load(f"mix_in{n % 2}", ("a", l, n), tm[:, n % 2, :], ga_d[n],
                             [(f"ma_out{n % 2}", l, n)] +
                             ([("gated", units[18 * (2 + n) + 16]["i"])] if n < 2 else [("mix_lo", l, n - 2)]))
                        load(f"mix_in{n % 2}", ("b", l, n), tm[:, 2 + n % 2, :], gb_d[n],
                             [(f"yb_out{n % 2}", l, n), ("attn_lo", l, 3)] + ([("mixed", l, n - 2)] if n >= 2 else []))
                for m in range(-2, 8):
                    if m >= 0:
                        after(("out", l, m))
                        if l < DEPTH - 1:
                            store("x_saved", (l, m), xT_d[m], X[:, m, :], [("residual", l, m)])
                            if m == 3:
                                add_square(("rms", l + 1), slice(0, TP), m)
                    n = m + 2
                    if n < 8:
                        load(f"x_old{n % 2}", (l, n), tm[:, 2 + n % 2, :], xT_d[n],
                             [("x_stored",) if l == 0 else ("x_saved", l - 1, 7),
                              ("mixed", l, 6 + n) if n < 2 else ("residual", l, n - 2)])
            z2_free = ("residual", DEPTH - 1, 7)
            for i, (dst, src) in enumerate(((trig2, "c_trig2"), (colmask, "c_colmask"), (rowmask, "c_rowmask"),
                                            (swmask, "c_swmask"))):
                load("block2_consts", (i,), dst[:], a[src], [z2_free] if i == 0 else [])

            def ln(i, c0):
                add_square(("ln", i), slice(0, SEQ), 3)
                for c in range(KC if i < 2 else 0):
                    if normed_lo("ln", i, c)[0] == "normed_lo":
                        subtract("normed_lo", ("ln", i, c), H[:, 1, c, 0:SEQ], X[:, c, c0:c0 + SEQ], H[:, 0, c, 0:SEQ],
                                 [("normed_hi", "ln", i, c)])
                for c in range(KC if i == 0 else 0):
                    store("ln_saved", (c,), xT_d[c][:, 0:SEQ], X[:, c, c0:c0 + SEQ], [ln_normed(0, c)])

            ln(0, META)

            def bias_tables(c):
                for hh in range(2):
                    for half in range(2):
                        src = band_d[2 * c + hh, 1 - half:15 - half].rearrange("i w k -> w i k")
                        load("bias_in", (c, hh, half), bias_e[half * GRID:(half + 1) * GRID, hh, :, :], src,
                             [("bands", HEADS - 1), z2_free] + ([("masked", phases[("n",)][16 * c - 1]["i"])] if c else []))
                pool.wait_ge(*S.at("bias_in", c, 1, 1))
                pool.wait_ge(*S.at("block2_consts", 3))
                for hh in range(2):
                    e = bias_e[:, hh, :, :]
                    pool.tensor_scalar(e, e, 1.0 / SCALE, None, ALU.mult).then_inc(*S.inc("bias_step", c, hh, "scaled"))
                    pool.wait_ge(*S.at("bias_step", c, hh, "scaled"))
                    pool.tensor_tensor(e, e, colmask[:, :, :], ALU.add).then_inc(*S.inc("bias_step", c, hh, "masked"))
                    pool.wait_ge(*S.at("bias_step", c, hh, "masked"))
                    pool.tensor_tensor(bias_i[:, hh, :, :], e[:, 2:11, :], rowmask[:, :, :], ALU.add)\
                        .then_inc(*S.inc("bias_ready", c, hh))

            for m in range(12):
                after(("m2", m))
            for c in range(4):
                bias_tables(c)
                for what in ("naq", "nak", "nav"):
                    after((what, c))
                store(f"attn_out{c % 2}", (c,), at_d[c], tm[:, c % 2, 0:SEQ],
                      [("gated", phases[("n",)][16 * c + 14]["i"])])
            after(("swk", 0))
            times_cos(("swk", 0), tm[:, 2, 0:SEQ], tm[:, 3, 0:SEQ], trig2[:, 0, :],
                      [("raw_copied", "swk", 0), ("k_split", "nak", 3)])
            after(("swv", 0))
            for c in range(4):
                after(("swq", c))
                times_cos(("swq", c), tm[:, 2, 0:SEQ], tm[:, 3, 0:SEQ], trig2[:, 0, :],
                          [("raw_copied", "swq", c), ("q_stacked", "swq", c - 1) if c else ("k_split", "swk", 0)])
                after(("m2", 12 + c))
                store(f"attn_out{c % 2}", (4 + c,), at_d[4 + c], tm[:, c % 2, 0:SEQ],
                      [("gated", phases[("s",)][16 * c + 14]["i"])])
            for k in range(-2, 8):
                if k >= 0:
                    subtract("branches_lo", (k,), SP2[:, 1, k, :], tm[:, k % 2, 0:SEQ], SP2[:, 0, k, :],
                             [("branches_hi", k)])
                n = k + 2
                if n < 8:
                    load(f"attn_in{n % 2}", (n,), tm[:, n % 2, 0:SEQ], at_d[n],
                         [("attn_out0", 6), ("attn_out1", 7), ("m2_out0", 15), ("m2_out1", 14)] if n < 2
                         else [("branches_lo", n - 2)])
            for m in range(-2, 8):
                if m >= 0:
                    after(("y1", m))
                    after(("y2", m))
                    subtract("mix2_lo", (m,), H[:, 1, m, 0:SEQ], tm[:, m % 2, 0:SEQ], H[:, 0, m, 0:SEQ],
                             [("mix2_hi", m)])
                n = m + 2
                if n < 8:
                    load(f"mix2_in{n % 2}", ("a", n), tm[:, n % 2, 0:SEQ], ga_d[n][:, 0:SEQ],
                         [("branches_lo", 6 + n) if n < 2 else ("mix2_lo", n - 2)])
                    load(f"mix2_in{n % 2}", ("b", n), tm[:, 2 + n % 2, 0:SEQ], gb_d[n][:, 0:SEQ],
                         [("mixed2", n - 2)] if n >= 2 else [("q_stacked", "swq", 3)])
            for m in range(8):
                load(f"h_old{m % 2}", (m,), tm[:, 2 + m % 2, 0:SEQ], xT_d[m][:, 0:SEQ],
                     [("ln_saved", 7), ("mixed2", 6 + m) if m < 2 else ("residual2", m - 2)])
                after(("out2", m))
            ln(1, 0)
            for f in range(4):
                for m in range(8):
                    after(("ff1", f, m))
                    subtract("hidden_lo", (f, m), SP2[:, 1, m, :], tm[:, m % 2, 0:SEQ], SP2[:, 0, m, :],
                             [("hidden_hi", f, m)])
                for m in range(8):
                    after(("ff2", f, m))
            ln(2, 0)

        @block.vector
        def _(dve):
            steps = [0]

            def step(ins):
                steps[0] += 1
                ins.then_inc(*S.inc("vector_step", steps[0]))
                dve.wait_ge(*S.at("vector_step", steps[0]))

            def wait(*events):
                for e in events:
                    dve.wait_ge(*S.at(*e))

            def rstd(key, name, src, eps, rows=slice(0, P), cols=TP):
                va, rt, out = (t[rows, 0:cols] for t in chain_temps(key))
                shaped = (lambda ap: v3(ap)) if cols == TP else (lambda ap: ap)
                wait(name)
                dve.tensor_scalar(shaped(va), src, eps, None, ALU.add).then_inc(*S.inc("variance", *key))
                wait(("rough_squared", *key))
                step(dve.scalar_tensor_tensor(rt, rt, -0.5, va, ALU.mult, ALU.mult))
                dve.scalar_tensor_tensor(out, rt, 1.5, out, ALU.add, ALU.mult).then_inc(*S.inc("rstd", *key))
                wait(("rstd", *key))

            def rotate(key, x, y, src, sin, last=None):
                wait(("rotated", *key), ("times_cos", *key))
                dve.tensor_tensor(y, src, sin, ALU.mult).then_inc(*S.inc("rot_times_sin", *key))
                wait(("rot_times_sin", *key))

            def stack_q(name, key, src, dst):
                for hh in range(2):
                    own, other = slice(hh * HD, (hh + 1) * HD), slice((1 - hh) * HD, (2 - hh) * HD)
                    wait(("q_hi", name, *key, hh))
                    dve.tensor_tensor(dst(hh, other), src[own], dst(hh, own).bitcast(F32), ALU.subtract)\
                        .then_inc(*(S.inc("q_stacked", name, *key) if hh else S.inc("q_stacking", name, *key)))

            def split_k(name, l, src):
                wait(("k_hi", name, l, 1))
                for half in range(2):
                    dve.tensor_tensor(KK[half * HD:(half + 1) * HD, 1, :], src, KK[0:HD, 0, :].bitcast(F32), ALU.subtract)\
                        .then_inc(*(S.inc("k_split", name, l) if half else S.inc("k_splitting", name, l)))

            def attention(units, mask_waits, gate):
                for k in range(len(units) + 3):
                    if k < len(units):
                        u, i = units[k], units[k]["i"]
                        wait(("logits", i), *mask_waits(u))
                        if i >= 2:
                            wait(("exped", i - 2))
                        if i >= 4:
                            wait(("normed_out", i - 4))
                        start = -TAKEN if u["sink"] is None else sink[:, 1, u["sink"]:u["sink"] + 1]
                        dve.tensor_tensor_reduce(out=Lb[:, i % 2, 0:u["n"]], in0=big[0][:, 0:u["n"]], in1=u["mask"],
                                                 scale=-SCALE, scalar=start, op0=ALU.add, op1=ALU.min,
                                                 accum_out=negmax[:, i % 4:i % 4 + 1]).then_inc(*S.inc("masked", i))
                    if 1 <= k <= len(units):
                        move(dve, units[k - 1], "dve")
                    if k >= 3 and (k - 3) % 2 == 1:
                        gate(units[k - 4], small[1])
                    if 2 <= k <= len(units) + 1:
                        u, i = units[k - 2], units[k - 2]["i"]
                        s, slot = rowsum[:, i % 4:i % 4 + 1], (k - 2) // 2 % 2
                        wait(("weighted", i))
                        if u["sink"] is not None:
                            wait(("sink_exped", i))
                            step(dve.tensor_tensor(s, s, sinkexp[:, i % 4:i % 4 + 1], ALU.add))
                        if i - u["hh"] - 4 >= 0:
                            wait(("out_turned", i - u["hh"] - 4))
                        step(dve.reciprocal(rowinv[:, i % 4:i % 4 + 1], s))
                        dve.tensor_scalar(Ob[:, slot, u["hh"] * HD:(u["hh"] + 1) * HD],
                                          small[u["hh"]][:, 0:HD],
                                          rowinv[:, i % 4:i % 4 + 1], None, ALU.mult).then_inc(*S.inc("normed_out", i))

            def subtract_lo(kind, i, c, x, cols):
                wait(("normed_hi", kind, i, c))
                dve.tensor_tensor(H[:, 1, c, cols], x, H[:, 0, c, cols].bitcast(F32), ALU.subtract)\
                    .then_inc(*S.inc("normed_lo_dve", kind, i, c))

            def add_square(key, cols, c):
                total = square_sums(key, cols)[0]
                wait(("squared", *key, c), ("square_sum", *key, c - 2) if c > 2 else ("squared", *key, 0))
                dve.tensor_tensor(total, total, tm[:, 0, cols], ALU.add).then_inc(*S.inc("square_sum", *key, c))

            def sum_x(i, c, x, event):
                if 1 <= c < KC - 1:
                    total = square_sums(("ln", i), slice(0, SEQ))[0]
                    wait(event(c), ("x_sum", i, c - 1) if c > 1 else event(0))
                    dve.tensor_tensor(total, total if c > 1 else x(0), x(c), ALU.add).then_inc(*S.inc("x_sum", i, c))

            X0 = lambda c: X[:, c, META:META + SEQ]
            X2 = lambda c: X[:, c, 0:SEQ]

            dve.memset(X[:, :, T:TP], 0.0).then_inc(*S.inc("x_padded"))
            lo64 = slice(0, HD)
            for l in range(DEPTH):
                if l == 0:
                    for c in (2, 4):
                        add_square(("rms", l), slice(0, TP), c)
                rstd(("rms", l), ("mean_square", "rms", l), ps3(psum_of[("mean_square", "rms", l)]), EPS)
                for c in range(KC):
                    if c >= 3:
                        wait(normed_lo("rms", l, c - 3))
                    dve.scalar_tensor_tensor(tm[:, 1 + c % 3, :], X[:, c, :], gain[:, l, c:c + 1], tm[:, 0, :],
                                             ALU.mult, ALU.mult).then_inc(*S.inc("normed", "rms", l, c))
                    if c in (2, 4, 6):
                        subtract_lo("rms", l, c - 1, tm[:, 1 + (c - 1) % 3, :], slice(0, TP))
                subtract_lo("rms", l, 7, tm[:, 1 + 7 % 3, :], slice(0, TP))
                wait(("normed_lo", "rms", l, 6), ("normed_lo_dve", "rms", l, 7), ("rotary_tables", l))
                for c in range(4):
                    x, y = sc4[2 * (c % 2)], sc4[2 * (c % 2) + 1]
                    rstd(("head", "q", l, c), ("head_square", "q", l, c), ps3(psum_of[("head_square", "q", l, c)]), EPS)
                    rotate(("q", l, c), x, v3(y), ps3(psum_of[("rotated", "q", l, c)]), v3(trig1[:, 1, :]))
                    step(dve.tensor_tensor(x, x, y, ALU.add))
                    dve.tensor_tensor(x, x, tm[:, 2, :], ALU.mult).then_inc(*S.inc("roped", "q", l, c))
                    stack_q("q", (l, c), x, lambda hh, rows: QS[rows, 2 * c + hh, :])
                rotate(("ki", l), None, v3(tm[lo64, 3, :]), ps3(psum_of[("rotated", "ki", l)], lo64), v3(trig1[lo64, 1, :]))
                dve.tensor_tensor(tm[lo64, 2, :], tm[lo64, 2, :], tm[lo64, 3, :], ALU.add)\
                    .then_inc(*S.inc("roped", "ki", l))
                split_k("ki", l, tm[lo64, 2, :])
                rstd(("head", "k", l), ("head_square", "k", l), ps3(psum_of[("head_square", "k", l)], lo64), EPS, lo64)
                rotate(("k", l), None, v3(sc4[1][lo64]), ps3(psum_of[("rotated", "k", l)], lo64), v3(trig1[lo64, 1, :]))
                step(dve.tensor_tensor(sc4[3][lo64], sc4[3][lo64], sc4[1][lo64], ALU.add))
                wait(("x_saved", l - 1, 7) if l else ("x_stored",))
                dve.tensor_tensor(k_roped[lo64, :], sc4[3][lo64], sc4[2][lo64], ALU.mult).then_inc(*S.inc("roped", "k", l))
                wait(("w_ready", l), ("v_turned", l), ("roped", "k", l))
                nrelu = 0
                for c in range(4):
                    rotate(("qi", l, c), None, v3(tm[:, 3, :]), ps3(psum_of[("rotated", "qi", l, c)]), v3(trig1[:, 1, :]))
                    dve.tensor_tensor(tm[:, 2, :], tm[:, 2, :], tm[:, 3, :], ALU.add)\
                        .then_inc(*S.inc("roped", "qi", l, c))
                    stack_q("qi", (l, c), tm[:, 2, :], lambda hh, rows: QIPB[rows, 2 * (c % 2) + hh, :])
                    for hh in range(2):
                        for j in range(1, NQ):
                            n, h = visible(j), 2 * c + hh
                            sc = SC[:, SCORE_AT[j]:SCORE_AT[j] + n]
                            wait(("relued", l, c, hh, j))
                            r, w = tm[:, nrelu % 2, 0:n], widx[:, j, h:h + 1]
                            if h == 0:
                                ins = dve.tensor_scalar(sc, r, w, None, ALU.mult)
                            else:
                                wait(("score_added", l, *score_units[nrelu - (NQ - 1)]))
                                ins = dve.scalar_tensor_tensor(sc, r, w, sc, ALU.mult, ALU.add)
                            ins.then_inc(*S.inc("score_added", l, c, hh, j))
                            nrelu += 1
                split_k("k", l, k_roped[lo64, :])
                hidden = {j: SC[0:HD, SCORE_AT[j] + visible(j) - CHUNK:SCORE_AT[j] + visible(j)] for j in range(1, NQ)}
                wait(("score_added", l, *score_units[-1]))
                for j in range(1, NQ):
                    dve.memset(hidden[j], NEG).then_inc(*S.inc("hidden_keys", l, j))
                rounds = [(r, j) for r in range(TOPK // 8) for j in range(1, NQ)]
                for x in range(len(rounds) + 1):
                    if x < len(rounds):
                        r, j = rounds[x]
                        wait(("taken", l, r - 1, j) if r else ("hidden_keys", l, j))
                        dve.max(top8[:, j, :], SC[:, SCORE_AT[j]:SCORE_AT[j] + visible(j)])\
                            .then_inc(*S.inc("eight", l, r, j))
                    if x >= 1:
                        r, j = rounds[x - 1]
                        sc = SC[:, SCORE_AT[j]:SCORE_AT[j] + visible(j)]
                        wait(("eight", l, r, j))
                        dve.match_replace(sc, top8[:, j, :], sc, TAKEN).then_inc(*S.inc("taken", l, r, j))
                for j in range(1, NQ):
                    sc = SC[:, SCORE_AT[j]:SCORE_AT[j] + visible(j)]
                    wait(("taken", l, TOPK // 8 - 1, j))
                    dve.tensor_scalar(sc, sc, TAKEN / 2, NEG, ALU.is_gt, ALU.mult).then_inc(*S.inc("mask_made", l, j))
                for j in range(1, NQ):
                    wait(("mask_made", l, j))
                    dve.memset(hidden[j], NEG).then_inc(*S.inc("mask_ready", l, j))

                def gate(u, bank):
                    c, slot = u["c"], tm[:, 2 + u["c"] % 2, :]
                    if u["q0"] == 0:
                        wait((f"silu_in{c % 2}", l, c), ("attn_lo", l, c - 2) if c >= 2 else ("ma_out1", l, 7))
                        dve.memset(slot[:, T:TP], 0.0).then_inc(*S.inc("attn_padded", l, c))
                    wait(("out_turned", u["i"]))
                    cols = slice(u["q0"], u["q0"] + u["nq"])
                    dve.tensor_tensor(slot[:, cols], bank[:, P:P + u["nq"]], tm[:, c % 2, cols], ALU.mult)\
                        .then_inc(*S.inc("gated", u["i"]))

                attention(phases[("a", l)], lambda u: [("mask_ready", l, NQ - 1), ("mask0_in", l)], gate)
                for m in range(8):
                    t = tm[:, m % 2, :]
                    wait(("projected", ("ya", l, m)), (f"mix_in{m % 2}", "b", l, m))
                    dve.tensor_tensor(v3(t), ps3(psum_of[("ya", l, m)]), v3(t), ALU.mult)\
                        .then_inc(*S.inc("mix_gated", l, m))
                    wait(("mix_gated", l, m))
                    dve.tensor_tensor(t, t, tm[:, 2 + m % 2, :], ALU.add).then_inc(*S.inc("mixed", l, m))
                for m in range(8):
                    wait(("projected", ("out", l, m)), (f"x_old{m % 2}", l, m))
                    dve.tensor_tensor(v3(X[:, m, :]), ps3(psum_of[("out", l, m)]), v3(tm[:, 2 + m % 2, :]), ALU.add)\
                        .then_inc(*S.inc("residual", l, m))
                    if l == DEPTH - 1:
                        sum_x(0, m, X0, lambda c: ("residual", l, c))
                    elif m in (3, 5):
                        add_square(("rms", l + 1), slice(0, TP), m - 1)

            def ln(i, c0):
                cols = slice(c0, c0 + SEQ)
                wait(("mean", i))
                for c in range(KC):
                    x = X[:, c, cols]
                    dve.tensor_tensor(x, x, ps2(psum_of[("mean", i)]), ALU.subtract).then_inc(*S.inc("centered", i, c))
                    if c in (4, 6):
                        add_square(("ln", i), slice(0, SEQ), c - 2)
                rstd(("ln", i), ("mean_square", "ln", i), ps2(psum_of[("mean_square", "ln", i)]), LN_EPS, cols=SEQ)
                for c in range(KC):
                    x = X[:, c, cols]
                    dve.scalar_tensor_tensor(x, x, ln_g[:, i, c:c + 1], tm[:, 0, 0:SEQ], ALU.mult, ALU.mult)\
                        .then_inc(*S.inc("scaled", i, c))
                    if c % 2:
                        wait(("scaled", i, c))
                        dve.tensor_scalar(x, x, ln_b[:, i, c:c + 1], None, ALU.add).then_inc(*S.inc("ln_normed_dve", i, c))
                    if i < 2 and c == 5:
                        subtract_lo("ln", i, 3, X[:, 3, cols], slice(0, SEQ))
                if i < 2:
                    subtract_lo("ln", i, 7, X[:, 7, cols], slice(0, SEQ))

            ln(0, META)

            def gate2(kind):
                def gate(u, bank):
                    c = u["c"]
                    k = c + (4 if kind == "s" else 0)
                    if u["q0"] == 0 and k >= 2:
                        wait((f"attn_out{k % 2}", k - 2))
                    if u["q0"] == 0 and k >= 5:
                        wait((f"m2_out{k % 2}", 12 + k - 5))
                    wait(("out_turned", u["i"]))
                    dve.tensor_copy(tm[:, c % 2, u["q0"]:u["q0"] + P], bank[:, P:2 * P]).then_inc(*S.inc("gated", u["i"]))
                return gate

            for c in range(4):
                stack_q("naq", (c,), tm[:, 3, 0:SEQ], lambda hh, rows: Q2[rows, hh, :])
                for hh in range(2):
                    for half in range(2):
                        own = slice(hh * HD, (hh + 1) * HD)
                        wait(("k_hi", "nak", c, hh, half), ("k_hi", "nak", c, hh, 1))
                        dve.tensor_tensor(K2[half * HD:(half + 1) * HD, hh, 1, :], tm[own, 2, 0:SEQ],
                                          K2[own, hh, 0, :].bitcast(F32), ALU.subtract)\
                            .then_inc(*(S.inc("k_split", "nak", c) if hh and half else S.inc("k_splitting", "nak", c, hh, half)))
                attention([u for u in phases[("n",)] if u["c"] == c],
                          lambda u: [("bias_ready", c, 1), ("ln_saved", KC - 1), ("normed_lo", "ln", 0, 6)], gate2("n"))
            for c in range(-1, 4):
                key = ("swk", 0) if c < 0 else ("swq", c)
                rotate(key, None, tm[:, 3, 0:SEQ], ps2(psum_of[("rotated", *key)]), trig2[:, 1, :])
                dve.tensor_tensor(tm[:, 2, 0:SEQ], tm[:, 2, 0:SEQ], tm[:, 3, 0:SEQ], ALU.add)\
                    .then_inc(*S.inc("roped", *key))
                if c < 0:
                    for hh in range(2):
                        for half in range(2):
                            own = slice(hh * HD, (hh + 1) * HD)
                            wait(("k_hi", "swk", 0, hh, 1))
                            dve.tensor_tensor(K2[half * HD:(half + 1) * HD, hh, 1, :], tm[own, 2, 0:SEQ],
                                              K2[own, hh, 0, :].bitcast(F32), ALU.subtract)\
                                .then_inc(*(S.inc("k_split", "swk", 0) if hh and half else
                                            S.inc("k_splitting", "swk", 0, hh, half)))
                    continue
                stack_q("swq", (c,), tm[:, 2, 0:SEQ], lambda hh, rows: Q2[rows, hh, :])
                attention([u for u in phases[("s",)] if u["c"] == c], lambda u: [("minus_sink",)], gate2("s"))
            for m in range(8):
                t, t2 = tm[:, m % 2, 0:SEQ], tm[:, 2 + m % 2, 0:SEQ]
                wait(("projected", ("y1", m)), (f"mix2_in{m % 2}", "b", m))
                dve.tensor_tensor(t, ps2(psum_of[("y1", m)]), t, ALU.mult).then_inc(*S.inc("y1_gated", m))
                wait(("projected", ("y2", m)))
                dve.tensor_tensor(t2, ps2(psum_of[("y2", m)]), t2, ALU.mult).then_inc(*S.inc("y2_gated", m))
                wait(("y1_gated", m), ("y2_gated", m))
                dve.tensor_tensor(t, t, t2, ALU.add).then_inc(*S.inc("mixed2", m))
            for m in range(8):
                wait(("projected", ("out2", m)), ("h_scaled", m))
                dve.tensor_tensor(X[:, m, 0:SEQ], tm[:, 2 + m % 2, 0:SEQ], ps2(psum_of[("out2", m)]), ALU.add)\
                    .then_inc(*S.inc("residual2", m))
                sum_x(1, m, X2, lambda c: ("residual2", c))
            ln(1, 0)
            for f in range(4):
                for m in range(8):
                    x = X[:, m, 0:SEQ]
                    wait(("projected", ("ff2", f, m)))
                    if f == 0:
                        step(dve.scalar_tensor_tensor(x, x, ALPHA, ps2(psum_of[("ff2", f, m)]), ALU.mult, ALU.add))
                        dve.tensor_scalar(x, x, b_o[:, 1, m:m + 1], None, ALU.add).then_inc(*S.inc("residual3", f, m))
                    else:
                        wait(("residual3", f - 1, m))
                        dve.tensor_tensor(x, x, ps2(psum_of[("ff2", f, m)]), ALU.add).then_inc(*S.inc("residual3", f, m))
                    if f == 3:
                        sum_x(2, m, X2, lambda c: ("residual3", 3, c))
            ln(2, 0)

        return S.seen


def constants():
    f = np.float32
    c = {"c_ident": np.eye(P, dtype=f)}

    def rotation(half, period):
        r = np.zeros((P, P), f)
        for m in range(P):
            d = m % HD
            if d < half:
                r[m + half, m] = -1.0
            elif d < period:
                r[m - half, m] = 1.0
        return r

    c["c_rot1"], c["c_rot2"] = rotation(HD // 2, HD), rotation(8, 16)
    c["c_headmean"] = np.kron(np.eye(2), np.full((HD, HD), 1.0 / HD)).astype(f)
    c["c_allmean"] = np.full((P, P), 1.0 / D, f)

    def trig(theta, dim, length, cols):
        inv = (f(1.0) / (f(theta) ** (np.arange(0, dim, 2, dtype=f) / f(dim)))).astype(f)
        ang = (np.arange(length, dtype=f)[:, None] * inv[None, :]).astype(f)
        t = np.zeros((P, 2, cols), f)
        t[:, 0, :] = 1.0
        for p in range(P):
            d = p % HD
            if d < dim:
                t[p, 0, :length] = np.cos(ang[:, d % (dim // 2)])
                t[p, 1, :length] = np.sin(ang[:, d % (dim // 2)])
        return t

    c["c_trig1"] = trig(10000.0, HD, T, TP)
    c["c_trig2"] = trig(500000.0, 16, SEQ, SEQ)
    edge = np.ones((P, 4, 16), f)
    for g, w in enumerate(WINDOWS):
        edge[:, g, :] = w / np.minimum(np.arange(1, 17), w)
    c["c_edge"] = edge
    m0 = np.zeros((P, visible(0)), f)
    m0[0:HD, visible(0) - CHUNK:] = NEG
    c["c_mask0"] = m0
    col = np.full((P, 14, GRID), NEG, f)
    for p in range(P):
        s = min(max(p % GRID - 8, 0), GRID - 16)
        col[p, :, s:s + 16] = 0.0
    c["c_colmask"] = col
    row = np.zeros((P, 9, GRID), f)
    row[0:GRID, 8, :] = NEG
    row[GRID:, 0, :] = NEG
    c["c_rowmask"] = row
    k, q = np.arange(3 * P)[None, :] - P, np.arange(P)[:, None]
    c["c_swmask"] = np.where(np.abs(k - q) <= P, 0.0, NEG).astype(f)
    return c


def kernel(**inputs):
    import concourse.bacc as bacc
    from concourse.bass_utils import run_bass_kernel_spmd as run

    arrays = {k: np.ascontiguousarray(v) for k, v in inputs.items()}
    arrays.update(constants())

    def build(known):
        nc = bacc.Bacc("TRN2", target_bir_lowering=False, num_devices=1)
        a = {k: nc.dram_tensor(f"in_{k}", v.shape, F32, kind="ExternalInput").ap() for k, v in arrays.items()}
        a["out"] = nc.dram_tensor("out_0", (1, SEQ, D), F32, kind="ExternalOutput").ap()
        return nc, program(nc, a, known)

    _, counts = build(None)
    nc, _ = build(counts)
    r = run(nc, [{f"in_{k}": v for k, v in arrays.items()}], core_ids=[0])
    return r.results[0]["out_0"]
```

```python
from contextlib import ExitStack

import numpy as np
import concourse.bass as bass
from concourse import mybir

F32 = mybir.dt.float32
F32R = mybir.dt.float32r
ALU = mybir.AluOpType
ACT = mybir.ActivationFunctionType
P = 128
D = 1024
KC = D // P
SEQ = 1024
META = 16
T = SEQ + META
TP = 1044
PIECE1 = TP // 3
DEPTH = 2
HEADS, HD = 8, 64
CHUNK, TOPK = 64, 256
NQ = SEQ // P
WINDOWS = (2, 4, 8, 16)
EPS, LN_EPS = 1e-6, 1e-5
NEG = -1e30
TAKEN = -3e38
ALPHA = 2.0 ** 0.25
FF = 4 * D
RAW = 2
GRID = 64
BANK = 512
SCALE = HD ** -0.5
IDX_SCALE = (HEADS ** -0.5) * (HD ** -0.5)
Q0, K0, GA0, U0, GB0, QI0, KI0, MG0 = 0, 512, 640, 1152, 1664, 2176, 2688, 2760
NAQ0, NAK0, NAV0, SWQ0, SWK0, SWV0, MG2 = 0, 512, 1024, 1536, 2048, 2176, 2304


def visible(j):
    return META + P * (j + 1)


SCORE_AT = {}
_at = 0
for _j in range(1, NQ):
    SCORE_AT[_j] = _at
    _at += visible(_j)
SCORE_COLS = _at


M2_FIRST, M2_BEFORE, M2_BESIDE = 9, (9, 11, 13, 15), (10, 12, 14)


class Signals:

    def __init__(self, ctx, nc, known):
        self.ctx, self.nc, self.known = ctx, nc, known
        self.sems, self.count, self.seen = {}, {}, {}

    def sem(self, name):
        if name not in self.sems:
            self.sems[name] = self.ctx.enter_context(self.nc.semaphore(name))
            self.count[name] = 0
        return self.sems[name]

    def inc(self, name, *key, by=1):
        s = self.sem(name)
        self.count[name] += by
        assert (name, *key) not in self.seen, (name, key)
        self.seen[(name, *key)] = self.count[name]
        return s, by

    def dma(self, name, *key):
        return self.inc(name, *key, by=16)

    def at(self, name, *key):
        if self.known is not None:
            return self.sem(name), self.known[(name, *key)]
        return self.sem(name), 1


def program(nc, a, known):
    ctx = ExitStack()
    with ctx:
        S = Signals(ctx, nc, known)

        def sb(name, shape, dt=F32, into=ctx):
            return into.enter_context(nc.sbuf_tensor(name, shape, dt))

        ident = sb("ident", [P, P])
        rot1 = sb("rot1", [P, P])
        rot2 = sb("rot2", [P, P])
        headmean = sb("headmean", [P, P])
        allmean = sb("allmean", [P, P])
        gain = sb("gain", [P, DEPTH, KC])
        qk_gain = sb("qk_gain", [P, DEPTH, 2])
        pool_b = sb("pool_b", [P, DEPTH, 4])
        pool_s = sb("pool_s", [P, DEPTH, 4])
        pool_bs = sb("pool_bs", [P, DEPTH, 4])
        edge = sb("edge", [P, 4, 16])
        ln_g = sb("ln_g", [P, 3, KC])
        ln_b = sb("ln_b", [P, 3, KC])
        b_in2 = sb("b_in2", [P, 34])
        b_ff1 = sb("b_ff1", [P, FF // P])
        b_o = sb("b_o", [P, 2, KC])
        sink = sb("sink", [P, 2, HEADS])
        top8 = sb("top8", [P, NQ, 8])
        widx = sb("widx", [P, NQ, HEADS])
        negmax = sb("negmax", [P, 4])
        rowsum = sb("rowsum", [P, 4])
        sinkexp = sb("sinkexp", [P, 4])
        rowinv = sb("rowinv", [P, 4])
        zeros = sb("zeros", [2, 64])
        raw = sb("raw", [P, RAW, KC * P])
        wsp = sb("wsp", [P, 2, 2, KC * P], F32R)
        tm = sb("tm", [P, 4, TP])
        H = sb("H", [P, 2, KC, TP], F32R)
        X = sb("X", [P, KC, TP])
        QS = sb("QS", [P, KC, TP], F32R)
        KK = sb("KK", [P, 2, TP], F32R)
        V = sb("V", [P, 9, HD])
        SC = sb("SC", [P, SCORE_COLS])

        def over(first, names):
            out, at = [], first
            for name, shape, dt in names:
                at = -(-at // 32) * 32
                out.append(nc.alloc_sbuf_tensor_at(name, shape, dt, offset=at))
                at += 4 * int(np.prod(shape[1:]))
            return out

        x_at, chunk = nc.sbuf_base - 4 * (2 * KC * TP + 2 * TP + 9 * HD + SCORE_COLS), 4 * TP
        z_at = x_at + KC * chunk
        QIPB, = over(x_at, [("QIPB", [P, KC, TP], F32R)])
        trig1, pw = over(x_at + 5 * chunk, [("trig1", [P, 2, TP], F32), ("pw", [P, 4, P], F32)])
        qi_first, = over(x_at + 2 * chunk, [("qi_first", [P, 2, TP], F32)])
        k_roped, = over(x_at + 4 * chunk, [("k_roped", [P, TP], F32)])
        Lb, Pb, PT, Ob, mask0, kept = over(x_at, [("Lb", [P, 2, 1040], F32), ("Pb", [P, 2, 9 * P], F32),
                                            ("PT", [P, 2, 9, P], F32), ("Ob", [P, 2, P], F32),
                                            ("mask0", [P, visible(0)], F32), ("kept", [P, SEQ], F32)])
        Q2, K2, V2, bias_e, bias_i, colmask, rowmask, swmask, trig2 = over(z_at, [
            ("Q2", [P, 2, SEQ], F32R), ("K2", [P, 2, 2, SEQ], F32R), ("V2", [P, NQ, P], F32),
            ("bias_e", [P, 2, 14, GRID], F32), ("bias_i", [P, 2, 9, GRID], F32), ("colmask", [P, 14, GRID], F32),
            ("rowmask", [P, 9, GRID], F32), ("swmask", [P, 3 * P], F32), ("trig2", [P, 2, SEQ], F32)])
        sb("z_rest", [P, (2 * KC * SEQ - KC * TP - 2 * TP - 9 * HD - SCORE_COLS)])
        norm_sums, = over(z_at, [("norm_sums", [P, 8, TP], F32)])
        norm_sums_h, = over(x_at - 2 * KC * chunk, [("norm_sums_h", [P, 8, TP], F32)])
        SP2, = over(z_at, [("SP2", [P, 2, KC, SEQ], F32R)])

        big = [ctx.enter_context(nc.psum_tensor(f"big{i}", [P, 3 * BANK], F32)) for i in range(2)]
        small2 = ctx.enter_context(nc.psum_tensor("small2", [P, 2 * BANK], F32))
        small = [small2[:, i * BANK:(i + 1) * BANK] for i in range(2)]

        def dram(name, shape):
            return nc.dram_tensor(name, shape, F32, kind="Internal").ap()

        xT_d = dram("xT_scratch", [KC, P, TP])
        ga_d = dram("gate_a_scratch", [KC, P, TP])
        gb_d = dram("gate_b_scratch", [KC, P, TP])
        sg_d = dram("silu_scratch", [4, P, TP])
        at_d = dram("attention_scratch", [KC, P, SEQ])
        rpb_d = dram("rpb_scratch", [64 + HEADS * 15 * 31 + 64])
        band_d = dram("band_scratch", [HEADS, 15, GRID, GRID])

        tm_flat = [tm[:, i, :] for i in range(4)]

        def ps3(s, rows=slice(0, P)):
            return big[s][rows, :].rearrange("p (b n) -> p b n", b=3)[:, :, 0:PIECE1]

        def v3(ap):
            return ap.rearrange("p (b n) -> p b n", b=3)

        def ps2(s, rows=slice(0, P)):
            return big[s][rows, 0:SEQ]

        pieces1 = [(i * BANK, i * PIECE1, PIECE1) for i in range(3)]
        pieces2 = [(i * BANK, i * BANK, BANK) for i in range(2)]
        pieces_seq = [(i * BANK, META + i * BANK, BANK) for i in range(2)]

        loads = []

        def wsrc(w, l, col, n, rows):
            return w[l][:, col:col + n].rearrange("(k p) n -> p k n", p=P), n, rows

        for l in range(DEPTH):
            for c in range(4):
                loads.append((("q", l, c), *wsrc(a["w_in"], l, Q0 + c * P, P, 8)))
            loads.append((("ki", l), *wsrc(a["w_in"], l, KI0, 72, 8)))
            loads.append((("kv", l), *wsrc(a["w_in"], l, K0, P, 8)))
            for c in range(4):
                loads.append((("qi", l, c), *wsrc(a["w_in"], l, QI0 + c * P, P, 8)))
            loads.append((("gatea", l, 0), *wsrc(a["w_in"], l, GA0, P, 8)))
            for g in range(4):
                loads.append((("u", l, g), *wsrc(a["w_in"], l, U0 + g * P, P, 8)))
                loads.append((("gateb", l, g), *wsrc(a["w_in"], l, GB0 + g * P, P, 8)))
            for c in range(1, 4):
                loads.append((("gatea", l, c), *wsrc(a["w_in"], l, GA0 + c * P, P, 8)))
            for m in range(8):
                loads.append((("mb", l, m), *wsrc(a["w_in"], l, MG0 + D + m * P, P, 8)))
                loads.append((("yb", l, m), *wsrc(a["w_branch_b"], l, m * P, P, 4)))
            for m in range(8):
                loads.append((("ma", l, m), *wsrc(a["w_in"], l, MG0 + m * P, P, 8)))
            for m in range(8):
                loads.append((("ya", l, m), *wsrc(a["w_branch_a"], l, m * P, P, 4)))
            for m in range(8):
                loads.append((("out", l, m), *wsrc(a["w_out"], l, m * P, P, 8)))
        w2 = a["w_in_2"]
        for m in range(M2_FIRST):
            loads.append((("m2", m), *wsrc(w2, 0, MG2 + m * P, P, 8)))
        for c in range(4):
            for what, col in (("nak", NAK0), ("naq", NAQ0), ("nav", NAV0)):
                loads.append(((what, c), *wsrc(w2, 0, col + c * P, P, 8)))
        for what, col in (("swk", SWK0), ("swv", SWV0)):
            loads.append(((what, 0), *wsrc(w2, 0, col, P, 8)))
        for c in range(4):
            loads.append((("swq", c), *wsrc(w2, 0, SWQ0 + c * P, P, 8)))
            for m in M2_BEFORE[c:c + 1] + M2_BESIDE[c:c + 1]:
                loads.append((("m2", m), *wsrc(w2, 0, MG2 + m * P, P, 8)))
        for m in range(8):
            loads.append((("y1", m), *wsrc(a["w_branch_na_2"], 0, m * P, P, 4)))
            loads.append((("y2", m), *wsrc(a["w_branch_swa_2"], 0, m * P, P, 4)))
        for m in range(8):
            loads.append((("out2", m), *wsrc(a["w_out_2"], 0, m * P, P, 8)))
        for f in range(4):
            for m in range(8):
                loads.append((("ff1", f, m), *wsrc(a["w_ff1_2"], 0, (8 * f + m) * P, P, 8)))
            for m in range(8):
                src = a["w_ff2_2"][0][f * D:(f + 1) * D, m * P:(m + 1) * P].rearrange("(k p) n -> p k n", p=P)
                loads.append((("ff2", f, m), src, P, 8))
        nload = {job: n for n, (job, *_) in enumerate(loads)}

        def units_first(l):
            for c in range(4):
                for j in (7, -1, 6, 0, 5, 1, 4, 2, 3):
                    for hh in range(2):
                        n = META if j < 0 else visible(j)
                        q0 = 0 if j < 0 else META + P * j
                        if j <= 0:
                            mask = mask0[:, 0:n] if j == 0 else mask0[:, 0:META]
                        else:
                            mask = SC[:, SCORE_AT[j]:SCORE_AT[j] + n]
                        qa = QS[:, 2 * c + hh, q0:q0 + P]
                        keys = [(o, min(BANK, n - o)) for o in range(0, n, BANK)]
                        kparts = [[(o, w, KK[:, part, o:o + w]) for o, w in keys] for part in range(2)]
                        kts = [(kt, min(P, n - kt * P), V[0:min(P, n - kt * P), kt, :])
                               for kt in range(-(-n // P))]
                        yield dict(block=("a", l), c=c, hh=hh, n=n, q=qa, k=kparts, mask=mask, kts=kts,
                                   sink=None, q0=q0, nq=META if j < 0 else P, h=2 * c + hh,
                                   first=j == 7)

        def na_rows(t):
            r = 2 * t
            start = [min(max(x - 4, 0), 8) for x in (r, r + 1)]
            return start[0], start[1] + 8 - start[0]

        def units_na():
            for c in range(4):
                for t in range(NQ):
                    for hh in range(2):
                        r0, rows = na_rows(t)
                        n, k0 = rows * GRID, r0 * GRID
                        i0 = r0 - 2 * t + 7
                        m = bias_i[:, hh, :, :] if rows == 9 else bias_e[:, hh, i0 - 1:i0 - 1 + rows, :]
                        m = m.rearrange("p r c -> p (r c)")
                        keys = [(o, min(BANK, n - o)) for o in range(0, n, BANK)]
                        kparts = [[(o, w, K2[:, hh, part, k0 + o:k0 + o + w]) for o, w in keys] for part in range(2)]
                        kts = [(kt, min(P, n - kt * P), V2[0:min(P, n - kt * P), k0 // P + kt, hh * HD:hh * HD + HD])
                               for kt in range(-(-n // P))]
                        yield dict(block=("n",), c=c, hh=hh, n=n, q=Q2[:, hh, t * P:t * P + P], k=kparts, mask=m,
                                   kts=kts, sink=None, q0=t * P, nq=P, h=2 * c + hh, t=t)

        def units_swa():
            for c in range(4):
                for t in range(NQ):
                    for hh in range(2):
                        lo, hi = max(t - 1, 0), min(t + 2, NQ)
                        n, g = (hi - lo) * P, c // 2
                        kparts = [[(0, n, K2[:, g, part, lo * P:hi * P])] for part in range(2)]
                        kts = [(kt, P, V2[:, lo + kt, g * HD:g * HD + HD]) for kt in range(hi - lo)]
                        m0 = (lo - t + 1) * P
                        yield dict(block=("s",), c=c, hh=hh, n=n, q=Q2[:, hh, t * P:t * P + P], k=kparts,
                                   mask=swmask[:, m0:m0 + n], kts=kts, sink=2 * c + hh, q0=t * P, nq=P,
                                   h=2 * c + hh, t=t)

        phases = {("a", 0): list(units_first(0)), ("a", 1): list(units_first(1)),
                  ("n",): list(units_na()), ("s",): list(units_swa())}
        nunit = 0
        for units in phases.values():
            for u in units:
                u["i"] = nunit
                nunit += 1
        score_units = [(c, hh, j) for c in range(4) for hh in range(2) for j in range(1, NQ)]

        def bank_owner(u, kt):
            return "dve" if kt < len(u["kts"]) // 2 else "act"

        def place(u, kt):
            return kt if bank_owner(u, kt) == "dve" else BANK // P + kt - len(u["kts"]) // 2

        def halves_even(buf):
            return lambda part, k: buf[:, 2 * k + part, :]

        def moved_events(u):
            who = {bank_owner(u, kt) for kt, _, _ in u["kts"]}
            return [(f"moved_{e}", u["i"]) for e in sorted(who)]

        def moves(u, engine):
            kts = [k for k in u["kts"] if bank_owner(u, k[0]) == engine]
            full = [k[0] for k in kts if k[1] == P]
            return ([(full[0], len(full), P)] if full else []) + [(k[0], 1, k[1]) for k in kts if k[1] < P]

        def norm_cols(key, h):
            if key[0] == "rms":
                return slice(0, 2 * PIECE1) if h == 0 else slice(2 * PIECE1, TP)
            return slice(h * BANK, (h + 1) * BANK)

        def half_pieces(key, h):
            if key[0] == "rms":
                return pieces1[0:2] if h == 0 else pieces1[2:3]
            return pieces2[h:h + 1]

        def norm_x(key, c, h):
            cols = norm_cols(key, h)
            shift = META if key == ("ln", 0) else 0
            return X[:, c, cols.start + shift:cols.stop + shift]

        def norm_input(key, c, h=None):
            base = ("residual", key[1] - 1, c) if key[0] == "rms" else \
                (("residual", DEPTH - 1, c), ("residual2", c), ("residual3", 3, c))[key[1]]
            return base if c < 6 else (*base, h)

        def norm_temp(key, slot, h):
            return (norm_sums_h if key in (("ln", 1), ("ln", 2)) else norm_sums)[:, slot, norm_cols(key, h)]

        def normed_lo(kind, i, h, c):
            by_dve = c % 2 if kind == "rms" else c in (0, 7)
            return ("normed_lo_dve" if by_dve else "normed_lo", kind, i, h, c)

        def ln_normed(i, h, c):
            return ("ln_normed_dve" if c % 2 else "ln_normed", i, h, c)

        sc4 = [SC[:, i * TP:(i + 1) * TP] for i in range(4)]

        def qi_temps(c):
            return (tm[:, 3, :], tm[:, 2, :]) if c else (qi_first[:, 0, :], qi_first[:, 1, :])

        psum_of = {}

        block = ctx.enter_context(nc.Block())

        @block.sync
        def _(sp):
            sp.dma_start(ident[:], a["c_ident"]).then_inc(*S.dma("identity"))
            consts = [(rot1[:], a["c_rot1"]), (rot2[:], a["c_rot2"]),
                      (headmean[:], a["c_headmean"]), (allmean[:], a["c_allmean"]),
                      (edge[:], a["c_edge"]),
                      (gain[:], a["norm_gain"].rearrange("l (k p) -> p l k", p=P)),
                      (pool_b[:], a["pool_b"].rearrange("l (k p) -> p l k", p=P)),
                      (pool_s[:], a["pool_scale"].rearrange("l (k p) -> p l k", p=P)),
                      (b_in2[:], a["b_in_2"][0].rearrange("(k p) -> p k", p=P)),
                      (b_ff1[:], a["b_ff1_2"][0].rearrange("(k p) -> p k", p=P)),
                      (b_o[:, 0, :], a["b_out_2"][0].rearrange("(k p) -> p k", p=P)),
                      (b_o[:, 1, :], a["b_ff2_2"][0].rearrange("(k p) -> p k", p=P)),
                      (sink[:, 0, :], bass.AP(a["swa_sink_2"].tensor, 0, [[0, P], [1, HEADS]]))]
            for i, name in enumerate(("ln0", "ln1", "ln2")):
                for dst, part in ((ln_g, "g"), (ln_b, "b")):
                    src = a[f"{name}_{part}_2"]
                    src = src if i == 0 else src[0]
                    consts.append((dst[:, i, :], src.rearrange("(k p) -> p k", p=P)))
            for half in range(2):
                for which, name in enumerate(("q_norm_gain", "k_norm_gain")):
                    consts.append((qk_gain[half * HD:(half + 1) * HD, :, which], a[name].rearrange("l d -> d l")))
            for i, (dst, src) in enumerate(consts):
                sp.dma_start(dst, src, allow_slow_non_contiguous=True).then_inc(*S.dma("constants", i))
            for n, (job, src, cols, rows) in enumerate(loads):
                if n == RAW:
                    sp.wait_ge(*S.at("constants", len(consts) - 1))
                    sp.nop().then_inc(*S.inc("constants_here"))
                if n >= RAW:
                    sp.wait_ge(*S.at("weight_lo", n - RAW))
                sp.dma_start(raw[:, n % RAW, :].rearrange("p (k n) -> p k n", k=KC)[:, 0:rows, 0:cols], src)\
                    .then_inc(*S.dma(f"weights{n % RAW}", n))
            for t in range(NQ - 4, NQ):
                sp.wait_ge(*S.at(f"output{t % 4}", t))

        @block.tensor
        def _(pe):
            free = {0: None, 1: None}
            turn = [0]

            def claim(key, emptied_by):
                s = psum_of[key] = turn[0] % 2
                turn[0] += 1
                if free[s] is not None:
                    for e in free[s]:
                        pe.wait_ge(*S.at(*e))
                free[s] = emptied_by
                return s

            def project(job, rhs, pieces, emptied_by, parts=None):
                claim(job, emptied_by)
                products(job, rhs, pieces, parts).then_inc(*S.inc("projected", job))

            def project_half(job, h, rhs, pieces, emptied_by, parts=None):
                if h == 0:
                    claim(job, emptied_by)
                products(job, rhs, pieces, parts).then_inc(*S.inc("projected", job, *([] if h else [0])))

            def products(job, rhs, pieces, parts, chunks=None, dst=None):
                n = nload[job]
                _, _, cols, rows = loads[n]
                if dst is None:
                    dst = lambda o, width: big[psum_of[job]][0:cols, o:o + width]
                pe.wait_ge(*S.at("weight_lo", n))
                w = [wsp[:, n % 2, part, :].rearrange("p (k n) -> p k n", k=KC) for part in range(2)]
                mm = None
                for k in chunks or range(rows):
                    if parts is not None:
                        pe.wait_ge(*S.at(*parts(k)))
                    for i, (wp, xp) in enumerate(((0, 0), (0, 1), (1, 0))):
                        for o, t0, width in pieces:
                            mm = pe.matmul(dst(o, width), w[wp][:, k, 0:cols],
                                           rhs(xp, k)[:, t0:t0 + width],
                                           start=(k == 0 and i == 0), stop=(k == rows - 1 and i == 2))
                return mm

            def plain(name, key, lhsT, rhs_list, pieces, emptied_by, waits, rows=P):
                s = claim((name, *key), emptied_by)
                mm = None
                for i, rhs in enumerate(rhs_list):
                    pe.wait_ge(*S.at(*waits[i]))
                    for o, t0, width in pieces:
                        mm = pe.matmul(big[s][0:rows, o:o + width], lhsT, rhs[:, t0:t0 + width],
                                       start=(i == 0), stop=(i == len(rhs_list) - 1))
                mm.then_inc(*S.inc(name, *key))

            def attention(units, values_ready, beside=None):
                def scores(u):
                    if u["i"] >= 1 and u is not units[0]:
                        pe.wait_ge(*S.at("masked", u["i"] - 1))
                    mm = None
                    for part in range(2):
                        for o, w, k in u["k"][part]:
                            mm = pe.matmul(big[0][:, o:o + w], u["q"], k, start=(part == 0), stop=(part == 1))
                    mm.then_inc(*S.inc("logits", u["i"]))

                def transposes(u, prev):
                    pe.wait_ge(*S.at("exped", u["i"]))
                    if prev is not None:
                        for e in moved_events(prev):
                            pe.wait_ge(*S.at(*e))
                    for kt, rows, _ in u["kts"]:
                        at = place(u, kt) * P
                        mm = pe.transpose(big[1][:, at:at + P], Pb[:, u["i"] % 2, kt * P:(kt + 1) * P],
                                          ident[:])
                    mm.then_inc(*S.inc("turned", u["i"]))

                def values(u, index):
                    if index == 0:
                        pe.wait_ge(*S.at(*values_ready))
                    for e in moved_events(u):
                        pe.wait_ge(*S.at(*e))
                    if index >= 2:
                        pe.wait_ge(*S.at("normed_out", u["i"] - 2))
                    if index >= 3 and u["hh"] == 1:
                        pe.wait_ge(*S.at("gated", u["i"] - 3))
                    for i, (kt, rows, v) in enumerate(u["kts"]):
                        mm = pe.matmul(small[u["hh"]][:, 0:HD], PT[0:rows, u["i"] % 2, kt, :], v,
                                       start=(i == 0), stop=(i == len(u["kts"]) - 1))
                    mm.then_inc(*S.inc("weighted", u["i"]))

                def turn_back(u0, u1, pair):
                    pe.wait_ge(*S.at("normed_out", u1["i"]))
                    pe.transpose(small[1][:, P:2 * P], Ob[:, pair % 2, :], ident[:])\
                        .then_inc(*S.inc("out_turned", u0["i"]))

                if units[0]["i"] > 0:
                    pe.wait_ge(*S.at("gated", units[0]["i"] - 2))
                for s in range(2):
                    for e in free[s] or []:
                        pe.wait_ge(*S.at(*e))
                for index in range(len(units) + 4):
                    if 2 <= index <= len(units) + 1:
                        transposes(units[index - 2], units[index - 3] if index >= 3 else None)
                    if index < len(units):
                        scores(units[index])
                    if index >= 4 and (index - 4) % 2 == 1:
                        turn_back(units[index - 5], units[index - 4], (index - 4) // 2)
                    if 3 <= index <= len(units) + 2:
                        values(units[index - 3], index - 3)
                    if beside is not None and index < len(units) and index % 2:
                        mm = products(("m2", beside), hi_lo(H), pieces2, None, [index // 2],
                                      lambda o, width: big[o // BANK][:, 2 * BANK:3 * BANK])
                        if index == len(units) - 1:
                            mm.then_inc(*S.inc("projected", ("m2", beside)))
                last = units[-1]
                free[0] = [("masked", last["i"])]
                free[1] = moved_events(last)
                if beside is not None:
                    for s in range(2):
                        free[s].append(("gate_kept", beside, s))

            pe.wait_ge(*S.at("identity"))
            for j in range(NQ + 1):
                s = claim(("x", j), [("x_turned", j)])
                pe.wait_ge(*S.at(f"x_in{j % 4}", j))
                rows = META if j == 0 else P
                for c in range(KC):
                    mm = pe.transpose(big[s][:, c * P:c * P + rows], tm[0:rows, j % 4, c * P:(c + 1) * P],
                                      ident[0:rows, 0:rows])
                mm.then_inc(*S.inc("x_transposed", j))
            pe.wait_ge(*S.at("constants_here"))

            def average(name, key, h, parts, pieces):
                for i, (rhs, ready) in enumerate(parts):
                    pe.wait_ge(*S.at(*ready))
                    for o, t0, width in pieces:
                        mm = pe.matmul(small2[:, o:o + width], allmean[:], rhs[:, t0:t0 + width],
                                       start=(i == 0), stop=(i == len(parts) - 1))
                mm.then_inc(*S.inc(name, *key, h))

            def mean(i, h):
                key = ("ln", i)
                if h:
                    pe.wait_ge(*S.at("centered", i, 0, KC - 1))
                average("mean", (i,), h, [(norm_temp(key, 0, h), ("x_sum", i, 5))] +
                        [(norm_x(key, c, h), norm_input(key, c, h)) for c in (6, 7)], [(0, 0, BANK)])

            def mean_square(key, h):
                if h:
                    pe.wait_ge(*S.at("variance", *key, 0))
                if key == ("rms", 1):
                    parts = [(0, ("square_sum", *key, 5)), (6, ("squared", *key, h, 6)), (7, ("squared", *key, h, 7))]
                else:
                    parts = [(0, ("pair_sum", *key, h, 0)), (2, ("pair_sum", *key, h, 2)),
                             (4, ("pair_sum_dve", *key, h, 4)), (6, ("squared", *key, h, 6)), (7, ("squared", *key, h, 7))]
                pieces = [(BANK, 0, BANK)] if key[0] == "ln" else \
                    [(0, 0, PIECE1), (BANK, PIECE1, PIECE1)][0:2 - h]
                average("mean_square", key, h, [(norm_temp(key, slot, h), ready) for slot, ready in parts], pieces)

            def norm_first(key, jobs, rhs, pieces):
                a, b = jobs
                for job, c in ((a, 6), (b, 7)):
                    project_half(job, 0, rhs, pieces(0), [norm_input(key, c, 1)])
                if key[0] == "ln":
                    mean(key[1], 0)
                project_half(a, 1, rhs, pieces(1), None)
                mean_square(key, 0)
                project_half(b, 1, rhs, pieces(1), None)
                if key[0] == "ln":
                    mean(key[1], 1)

            def norm_users(key, jobs, emptied_by):
                for h in range(2):
                    for n, job in enumerate(jobs):
                        if h == 0 and n == 1 and key != ("rms", 1):
                            mean_square(key, 1)
                        project_half(job, h, hi_lo(H), half_pieces(key, h), emptied_by[n],
                                     (lambda k: normed_lo(*key, h, k)) if n == 0 else None)

            hi_lo = lambda buf: (lambda part, k: buf[:, part, k, :])
            halves = lambda buf: (lambda part, k: buf[:, 4 * part + k, :])
            for l in range(DEPTH):
                key = ("rms", l)
                mean_square(key, l)
                norm_users(key, [("q", l, 0), ("q", l, 1)], [[("raw_copied", "q", l, c)] for c in range(2)])

                def head_norm_and_rotate(key, y, rows, sq):
                    if sq is not None:
                        plain("head_square", key, headmean[0:rows, 0:rows], [sq], pieces1,
                              [("variance", "head", *key)], [("head_squared", *key)], rows)
                    plain("rotated", key, rot1[0:rows, 0:rows], [y], pieces1, [("rot_times_sin", *key)],
                          [("raw_copied", *key)], rows)

                for c in range(5):
                    if c in (2, 3):
                        project(("q", l, c), hi_lo(H), pieces1, [("raw_copied", "q", l, c)])
                    elif c == 4:
                        project(("ki", l), hi_lo(H), pieces1, [("w_copied", l)])
                    if c >= 1:
                        head_norm_and_rotate(("q", l, c - 1), sc4[2 * ((c - 1) % 2) + 1], P, sc4[2 * ((c - 1) % 2)])
                project(("kv", l), hi_lo(H), pieces1, [("v_copied", l)])
                plain("rotated", ("ki", l), rot1[0:HD, 0:HD], [tm[0:HD, 3, :]], pieces1,
                      [("rot_times_sin", "ki", l)], [("raw_copied", "ki", l)], HD)
                s = claim(("w", l), [("w_ready", l)])
                pe.wait_ge(*S.at("w_copied", l))
                for j in range(1, NQ):
                    mm = pe.transpose(big[s][:, j * 8:(j + 1) * 8], tm[HD:HD + 8, 3, META + j * P:META + (j + 1) * P],
                                      ident[HD:HD + 8, HD:HD + 8])
                mm.then_inc(*S.inc("w_turned", l))
                project(("qi", l, 0), hi_lo(H), pieces1, [("raw_copied", "qi", l, 0)])
                head_norm_and_rotate(("k", l), sc4[1][0:HD], HD, sc4[0][0:HD])
                s = claim(("v", l), [("v_ready", l)])
                pe.wait_ge(*S.at("v_copied", l))
                for kt in range(9):
                    rows = min(P, T - kt * P)
                    mm = pe.transpose(big[s][0:rows, kt * HD:(kt + 1) * HD], sc4[1][HD:P, kt * P:kt * P + rows],
                                      ident[HD:P, HD:P])
                mm.then_inc(*S.inc("v_turned", l))
                for c in range(4):
                    plain("rotated", ("qi", l, c), rot1[:], [qi_temps(c)[0]], pieces1,
                          [("rot_times_sin", "qi", l, c)], [("raw_copied", "qi", l, c)])
                    if c < 3:
                        project(("qi", l, c + 1), hi_lo(H), pieces1, [("raw_copied", "qi", l, c + 1)])
                    else:
                        project(("gatea", l, 0), hi_lo(H), pieces1, [("gatea_silu", l, 0)])
                    pe.wait_ge(*S.at("q_stacked", "qi", l, c))
                    pe.wait_ge(*S.at("k_split", "ki", l))
                    for hh in range(2):
                        for j in range(1, NQ):
                            n = visible(j)
                            s = claim(("index", l, c, hh, j), [("relued", l, c, hh, j)])
                            for part in range(2):
                                for o in range(0, n, BANK):
                                    w = min(BANK, n - o)
                                    mm = pe.matmul(big[s][:, o:o + w],
                                                   QIPB[:, 2 * (c % 2) + hh, META + j * P:META + (j + 1) * P],
                                                   KK[:, part, o:o + w], start=(part == 0), stop=(part == 1))
                            mm.then_inc(*S.inc("index_scores", l, c, hh, j))

                def pool_mix(g):
                    pe.wait_ge(*S.at("pool_weights", l))
                    plain("pool_mixed", (l, g), pw[:, g, :], [tm[:, 0, :]], pieces1, [("pool_scaled", l, g)],
                          [("pooled", l, g)])

                for g in range(4):
                    project(("u", l, g), hi_lo(H), pieces1, [("u_copied", l, g)])
                    if g:
                        pool_mix(g - 1)
                    project(("gateb", l, g), hi_lo(H), pieces1, [("gateb_silu", l, g)])
                for c in range(1, 4):
                    project(("gatea", l, c), hi_lo(H), pieces1, [("gatea_silu", l, c)])
                    if c == 1:
                        pool_mix(3)
                for m in range(8):
                    project(("mb", l, m), hi_lo(H), pieces1, [("mb_sigmoid", l, m)])
                    project(("yb", l, m), halves(QIPB), pieces1, [("yb_copied", l, m)],
                            (lambda k: ("pool_lo", l, k)) if m == 0 else None)
                for m in range(8):
                    project(("ma", l, m), hi_lo(H), pieces1, [("ma_sigmoid", l, m)])
                pe.wait_ge(*S.at("q_stacked", "q", l, 3))
                pe.wait_ge(*S.at("k_split", "k", l))
                attention(phases[("a", l)], ("v_ready", l))
                for m in range(8):
                    project(("ya", l, m), halves_even(QS), pieces1, [("mix_gated", l, m)],
                            (lambda k: ("attn_lo", l, k)) if m == 0 else None)
                for m in range(6):
                    project(("out", l, m), hi_lo(H), pieces1 if l < DEPTH - 1 else pieces_seq, [("residual", l, m)],
                            (lambda k: ("mix_lo", l, k)) if m == 0 else None)
                if l < DEPTH - 1:
                    norm_first(("rms", l + 1), [("out", l, 6), ("out", l, 7)], hi_lo(H),
                               lambda h: half_pieces(("rms", l + 1), h))
                else:
                    norm_first(("ln", 0), [("out", l, 6), ("out", l, 7)], hi_lo(H), lambda h: pieces_seq[h:h + 1])

            norm_users(("ln", 0), [("m2", 0), ("m2", 1)], [[("m2_sigmoid", m)] for m in range(2)])
            for m in range(2, M2_FIRST):
                project(("m2", m), hi_lo(H), pieces2, [("m2_sigmoid", m)])

            def turn_values(what, c):
                s = claim(("v", what, c), [("v_ready", what, c)])
                pe.wait_ge(*S.at("v_biased", what, c))
                for kt in range(NQ):
                    mm = pe.transpose(big[s][:, kt * P:(kt + 1) * P], tm[:, (c + 1) % 2, kt * P:(kt + 1) * P], ident[:])
                mm.then_inc(*S.inc("v_turned", what, c))

            def before_na(c):
                project(("nak", c), hi_lo(H), pieces2, [("raw_copied", "nak", c)])
                project(("naq", c), hi_lo(H), pieces2, [("raw_copied", "naq", c)])
                project(("nav", c), hi_lo(H), pieces2, [("v_biased", "nav", c)])
                turn_values("nav", c)
                for e in (("q_stacked", "naq", c), ("k_split", "nak", c)):
                    pe.wait_ge(*S.at(*e))

            def rotate2(key):
                plain("rotated", key, rot2[:], [tm[:, 3, :]], pieces2, [("rot_times_sin", *key)],
                      [("raw_copied", *key)])

            def by_chunk(kind, before):
                units = phases[(kind,)]
                for c in range(4):
                    part = [u for u in units if u["c"] == c]
                    before(c)
                    if kind == "n":
                        attention(part, ("v_ready", "nav", c))
                    else:
                        attention(part, ("v_ready", "swv", 0), M2_BESIDE[c] if c < 3 else None)

            by_chunk("n", before_na)
            project(("swk", 0), hi_lo(H), pieces2, [("raw_copied", "swk", 0)])
            rotate2(("swk", 0))
            project(("swv", 0), hi_lo(H), pieces2, [("v_biased", "swv", 0)])
            turn_values("swv", 0)

            def before_swa(c):
                project(("swq", c), hi_lo(H), pieces2, [("raw_copied", "swq", c)])
                rotate2(("swq", c))
                project(("m2", M2_BEFORE[c]), hi_lo(H), pieces2, [("m2_sigmoid", M2_BEFORE[c])])
                for e in (("q_stacked", "swq", c), ("k_split", "swk", 0)):
                    pe.wait_ge(*S.at(*e))

            by_chunk("s", before_swa)
            for m in range(8):
                project(("y1", m), lambda part, k: H[:, part, k, :], pieces2, [("y1_gated", m)],
                        (lambda k: ("branches_lo", k)) if m == 0 else None)
                project(("y2", m), lambda part, k: H[:, part, 4 + k, :], pieces2, [("y2_gated", m)],
                        (lambda k: ("branches_lo", 4 + k)) if m == 0 else None)
            for m in range(6):
                project(("out2", m), hi_lo(SP2), pieces2, [("residual2", m)],
                        (lambda k: ("mix2_lo", k)) if m == 0 else None)
            norm_first(("ln", 1), [("out2", 6), ("out2", 7)], hi_lo(SP2), lambda h: half_pieces(("ln", 1), h))
            norm_users(("ln", 1), [("ff1", 0, 0), ("ff1", 0, 1)], [[("hidden_relu", 0, m)] for m in range(2)])
            for f in range(4):
                for m in range(2 if f == 0 else 0, 8):
                    project(("ff1", f, m), hi_lo(H), pieces2, [("hidden_relu", f, m)])
                for m in range(8 if f < 3 else 6):
                    project(("ff2", f, m), hi_lo(SP2), pieces2, [("residual3", f, m)],
                            (lambda k: ("hidden_lo", f, k)) if m == 0 else None)
            norm_first(("ln", 2), [("ff2", 3, 6), ("ff2", 3, 7)], hi_lo(SP2), lambda h: half_pieces(("ln", 2), h))
            for t in range(NQ):
                if t == 1:
                    mean_square(("ln", 2), 1)
                s = claim(("final", t), [("out_copied", t)])
                for c in (KC - 2, KC - 1):
                    pe.wait_ge(*S.at(*ln_normed(2, t // 4, c)))
                for c in range(KC):
                    mm = pe.transpose(big[s][:, c * P:(c + 1) * P], X[:, c, t * P:(t + 1) * P], ident[:])
                mm.then_inc(*S.inc("final_turned", t))


        def chain_temps(key):
            if key[0] in ("rms", "ln"):
                return [tm[:, i, :] for i in (2, 3, 0)]
            if key[1] == "q":
                return [tm[:, i, :] for i in (0, 1, 2)]
            return [tm[:, 0, :], tm[:, 1, :], sc4[2]]

        def weight_hi(act, n):
            if n < len(loads):
                job, _, cols, rows = loads[n]
                if n >= 2:
                    act.wait_ge(*S.at("projected", loads[n - 2][0]))
                act.wait_ge(*S.at(f"weights{n % RAW}", n))
                view = lambda ap: ap.rearrange("p (k n) -> p k n", k=KC)[:, 0:rows, 0:cols]
                act.activation(view(wsp[:, n % 2, 0, :]), view(raw[:, n % RAW, :]), ACT.Copy)\
                    .then_inc(*S.inc("weight_hi", n))

        def act_attention(act, units, per_chunk, chunk_done, between=None):
            for k in range(len(units) + 5):
                if between:
                    between(k)
                if 2 <= k <= len(units) + 1:
                    move(act, units[k - 2], "act")
                if k < len(units):
                    u, i = units[k], units[k]["i"]
                    act.wait_ge(*S.at("masked", i))
                    if i >= 2:
                        act.wait_ge(*S.at("turned", i - 2))
                    if i >= 4:
                        act.wait_ge(*S.at("normed_out", i - 4))
                    act.activation(Pb[:, i % 2, 0:u["n"]], Lb[:, i % 2, 0:u["n"]], ACT.Exp, bias=negmax[:, i % 4:i % 4 + 1],
                                   scale=-1.0, accum_out=rowsum[:, i % 4:i % 4 + 1]).then_inc(*S.inc("exped", i))
                    if u["sink"] is not None:
                        act.activation(sinkexp[:, i % 4:i % 4 + 1], negmax[:, i % 4:i % 4 + 1], ACT.Exp,
                                       bias=sink[:, 0, u["sink"]:u["sink"] + 1]).then_inc(*S.inc("sink_exped", i))
                if chunk_done and k >= per_chunk + 4 and (k - 4) % per_chunk == 0:
                    chunk_done((k - 4) // per_chunk - 1)

        def move(eng, u, who):
            parts, i = moves(u, who), u["i"]
            if not parts:
                return
            eng.wait_ge(*S.at("turned", i))
            if i >= 2:
                eng.wait_ge(*S.at("weighted", i - 2))
            for x, (kt, count, rows) in enumerate(parts):
                dst = PT[0:rows, i % 2, kt:kt + count, :]
                at = place(u, kt) * P
                src = big[1][0:rows, at:at + count * P].rearrange("p (k n) -> p k n", k=count)
                ins = eng.activation(dst, src, ACT.Copy) if who == "act" else eng.tensor_copy(dst, src)
                ins.then_inc(*(S.inc(f"moved_{who}", i) if x == len(parts) - 1 else S.inc(f"moved_{who}", i, "part", x)))

        @block.scalar
        def _(act):

            def after(job):
                weight_hi(act, nload[job] + 2)

            def root(key, rows=slice(0, P), cols=slice(0, TP)):
                sq, rt, y = chain_temps(key)
                act.wait_ge(*S.at("variance", *key))
                rt, sq, y = rt[rows, cols], sq[rows, cols], y[rows, cols]
                act.activation(rt, sq, ACT.Ln).then_inc(*S.inc("rstd_part", *key, 0))
                act.wait_ge(*S.at("rstd_part", *key, 0))
                act.activation(y, rt, ACT.Exp, scale=-0.5).then_inc(*S.inc("rstd_part", *key, 1))
                act.wait_ge(*S.at("rstd_part", *key, 1))
                act.activation(rt, y, ACT.Square).then_inc(*S.inc("rstd_part", *key, 2))


            def split_hi(name, key, dst, src, waits):
                for w in waits:
                    act.wait_ge(*S.at(*w))
                act.activation(dst, src, ACT.Copy).then_inc(*S.inc(name, *key))

            def square(key, h, c, *waits):
                for w in waits:
                    act.wait_ge(*S.at(*w))
                act.activation(norm_temp(key, c, h), norm_x(key, c, h), ACT.Square).then_inc(*S.inc("squared", *key, h, c))

            def normed_rms(l, h, chunks=range(KC)):
                cols = norm_cols(("rms", l), h)
                for c in chunks:
                    split_hi("normed_hi", ("rms", l, h, c), H[:, 0, c, cols], tm[:, 1 + c % 3, cols],
                             [("normed", "rms", l, h, c)])

            for l in range(DEPTH):
                key = ("rms", l)
                if l == 0:
                    for c in range(KC):
                        square(key, 0, c, ("x_turned", 6))
                    weight_hi(act, 0)
                    root((*key, 0), cols=norm_cols(key, 0))
                else:
                    for c in range(6):
                        act.wait_ge(*S.at(*norm_input(key, c)))
                        after(("out", l - 1, c))
                        act.activation(norm_sums[:, c, :], X[:, c, :], ACT.Square).then_inc(*S.inc("squared", *key, c))
                    square(key, 0, 6, norm_input(key, 6, 0))
                    square(key, 0, 7, norm_input(key, 7, 0))
                    after(("out", l - 1, 6))
                    square(key, 1, 6, norm_input(key, 6, 1))
                    root((*key, 0), cols=norm_cols(key, 0))
                    square(key, 1, 7, norm_input(key, 7, 1))
                    after(("out", l - 1, 7))
                normed_rms(l, 0, range(3))
                if l == 0:
                    weight_hi(act, 1)
                normed_rms(l, 0, range(3, KC))
                if l == 0:
                    for c in range(KC):
                        square(key, 1, c, ("x_turned", NQ), ("x_padded",))
                root((*key, 1), cols=norm_cols(key, 1))
                normed_rms(l, 1)
                if l == 0:
                    act.wait_ge(*S.at("constants_here"))
                    for i in range(DEPTH * 4):
                        act.activation(pool_bs[:, i // 4, i % 4:i % 4 + 1], pool_b[:, i // 4, i % 4:i % 4 + 1], ACT.Copy,
                                       scale=pool_s[:, i // 4, i % 4:i % 4 + 1]).then_inc(*S.inc("pool_bias", i // 4, i % 4))
                    act.activation(sink[:, 1, :], sink[:, 0, :], ACT.Copy, scale=-1.0).then_inc(*S.inc("minus_sink"))

                def split_q(name, key, src, dst, k, rows=2):
                    act.wait_ge(*S.at("roped", name, *key))
                    for hh in range(2):
                        part = slice(hh * HD, (hh + 1) * HD)
                        act.activation(dst[part, k + hh, :], src[part], ACT.Copy)\
                            .then_inc(*S.inc("q_hi", name, *key, hh))

                def split_k(name, key, src, dst_lo, dst_hi):
                    act.wait_ge(*S.at("roped", name, *key))
                    for half, dst in enumerate((dst_lo, dst_hi)):
                        act.activation(dst, src, ACT.Copy).then_inc(*S.inc("k_hi", name, *key, half))

                for c in range(5):
                    if c < 4:
                        s, x, y = psum_of[("q", l, c)], sc4[2 * (c % 2)], sc4[2 * (c % 2) + 1]
                        act.wait_ge(*S.at("projected", ("q", l, c)))
                        if c >= 2:
                            act.wait_ge(*S.at("q_stacked", "q", l, c - 2))
                        act.activation(v3(x), ps3(s), ACT.Square).then_inc(*S.inc("head_squared", "q", l, c))
                        act.activation(v3(y), ps3(s), ACT.Copy, scale=qk_gain[:, l, 0:1])\
                            .then_inc(*S.inc("raw_copied", "q", l, c))
                        after(("q", l, c))
                    else:
                        s, lo64 = psum_of[("ki", l)], slice(0, HD)
                        act.wait_ge(*S.at("projected", ("ki", l)))
                        act.activation(v3(tm[lo64, 3, :]), ps3(s, lo64), ACT.Copy).then_inc(*S.inc("raw_copied", "ki", l))
                        act.activation(v3(tm[HD:HD + 8, 3, :]), ps3(s, slice(HD, HD + 8)), ACT.Copy)\
                            .then_inc(*S.inc("w_copied", l))
                        after(("ki", l))
                    if c >= 1:
                        root(("head", "q", l, c - 1))
                        split_q("q", (l, c - 1), sc4[2 * ((c - 1) % 2)], QS, 2 * (c - 1))
                s = psum_of[("kv", l)]
                act.wait_ge(*S.at("projected", ("kv", l)))
                act.wait_ge(*S.at("q_stacked", "q", l, 2))
                act.activation(v3(sc4[0][lo64]), ps3(s, lo64), ACT.Square).then_inc(*S.inc("head_squared", "k", l))
                act.activation(v3(sc4[1][lo64]), ps3(s, lo64), ACT.Copy, scale=qk_gain[lo64, l, 1:2])\
                    .then_inc(*S.inc("raw_copied", "k", l))
                act.activation(v3(sc4[1][HD:P]), ps3(s, slice(HD, P)), ACT.Copy).then_inc(*S.inc("v_copied", l))
                after(("kv", l))
                split_k("ki", (l,), tm[lo64, 2, :], KK[0:HD, 0, :], KK[HD:P, 0, :])
                act.wait_ge(*S.at("w_turned", l))
                act.activation(widx[:, 1:NQ, :],
                               big[psum_of[("w", l)]][:, 8:NQ * 8].rearrange("p (j h) -> p j h", h=8), ACT.Copy,
                               scale=IDX_SCALE).then_inc(*S.inc("w_ready", l))

                def take_qi(c):
                    act.wait_ge(*S.at("projected", ("qi", l, c)))
                    if c == 0:
                        act.wait_ge(*(S.at("x_saved", l - 1, 7) if l else S.at("x_stored")))
                    elif c == 1:
                        act.wait_ge(*S.at("k_split", "ki", l))
                    else:
                        act.wait_ge(*S.at("q_stacked", "qi", l, c - 1))
                    act.activation(v3(qi_temps(c)[0]), ps3(psum_of[("qi", l, c)]), ACT.Copy)\
                        .then_inc(*S.inc("raw_copied", "qi", l, c))
                    after(("qi", l, c))

                def gate_a(c, slot, wait):
                    act.wait_ge(*S.at("projected", ("gatea", l, c)))
                    act.wait_ge(*S.at(*wait))
                    act.activation(v3(tm[:, slot, :]), ps3(psum_of[("gatea", l, c)]), ACT.Silu)\
                        .then_inc(*S.inc("gatea_silu", l, c))
                    act.wait_ge(*S.at("gatea_silu", l, c))
                    act.dma_start(sg_d[c], tm[:, slot, :]).then_inc(*S.dma(f"gate_out{c % 2}", "a", l, c))
                    after(("gatea", l, c))

                take_qi(0)
                root(("head", "k", l), lo64)
                s = psum_of[("v", l)]
                act.wait_ge(*S.at("v_turned", l))
                act.activation(V[:, 0:8, :], big[s][:, 0:8 * HD].rearrange("p (k d) -> p k d", k=8), ACT.Copy)\
                    .then_inc(*S.inc("v_part", l))
                act.activation(V[0:META, 8, :], big[s][0:META, 8 * HD:9 * HD], ACT.Copy).then_inc(*S.inc("v_ready", l))
                nrelu = 0
                for c in range(4):
                    if c == 1:
                        act.wait_ge(*S.at("q_stacked", "qi", l, 0))
                    split_q("qi", (l, c), qi_temps(c)[1], QIPB, 2 * (c % 2))
                    if c < 3:
                        take_qi(c + 1)
                    else:
                        gate_a(0, 3, ("roped", "qi", l, 3))
                    for hh in range(2):
                        for j in range(1, NQ):
                            n = visible(j)
                            act.wait_ge(*S.at("index_scores", l, c, hh, j))
                            if nrelu >= 2:
                                act.wait_ge(*S.at("score_added", l, *score_units[nrelu - 2]))
                            elif nrelu == 0:
                                act.wait_ge(*S.at("roped", "k", l))
                            act.activation(tm[:, nrelu % 2, 0:n], big[psum_of[("index", l, c, hh, j)]][:, 0:n], ACT.Relu)\
                                .then_inc(*S.inc("relued", l, c, hh, j))
                            nrelu += 1
                act.wait_ge(*S.at("index_scores", l, 3, 1, NQ - 1))
                split_k("k", (l,), k_roped[lo64, :], KK[0:HD, 0, :], KK[HD:P, 0, :])

                def pool_scale(g):
                    act.wait_ge(*S.at("pool_mixed", l, g))
                    act.wait_ge(*S.at("pool_bias", l, g))
                    act.activation(v3(tm[:, 1, :]), ps3(psum_of[("pool_mixed", l, g)]), ACT.Identity,
                                   scale=pool_s[:, l, g:g + 1], bias=pool_bs[:, l, g:g + 1])\
                        .then_inc(*S.inc("pool_scaled", l, g))
                    split_hi("pool_hi", (l, g), QIPB[:, g, :], tm[:, 1, :], [("pool_gated", l, g)])

                for g in range(4):
                    act.wait_ge(*S.at("projected", ("u", l, g)))
                    act.wait_ge(*S.at("score_added", l, *score_units[-1]) if g == 0 else S.at("pool_mixed", l, g - 1))
                    act.activation(v3(tm[:, 0, :]), ps3(psum_of[("u", l, g)]), ACT.Copy).then_inc(*S.inc("u_copied", l, g))
                    after(("u", l, g))
                    if g:
                        pool_scale(g - 1)
                    act.wait_ge(*S.at("projected", ("gateb", l, g)))
                    act.wait_ge(*S.at("pool_gated", l, g - 1) if g else S.at("gate_out0", "a", l, 0))
                    act.activation(v3(tm[:, 3, :]), ps3(psum_of[("gateb", l, g)]), ACT.Silu)\
                        .then_inc(*S.inc("gateb_silu", l, g))
                    after(("gateb", l, g))
                gate_a(1, 2, ("pooled", l, 3))
                pool_scale(3)
                gate_a(2, 0, ("pool_mixed", l, 3))
                gate_a(3, 2, ("gate_out1", "a", l, 1))
                for m in range(8):
                    act.wait_ge(*S.at("projected", ("mb", l, m)))
                    act.wait_ge(*(S.at("yb_gated", l, m - 2) if m >= 2 else S.at("pool_lo", l, 3) if m else
                                  S.at("gate_out0", "a", l, 2)))
                    act.activation(v3(tm[:, m % 2, :]), ps3(psum_of[("mb", l, m)]), ACT.Sigmoid)\
                        .then_inc(*S.inc("mb_sigmoid", l, m))
                    after(("mb", l, m))
                    act.wait_ge(*S.at("projected", ("yb", l, m)))
                    if m >= 2:
                        act.wait_ge(*S.at(f"yb_out{m % 2}", l, m - 2))
                    elif m == 0:
                        act.wait_ge(*S.at("gate_out1", "a", l, 3))
                    act.activation(v3(tm[:, 2 + m % 2, :]), ps3(psum_of[("yb", l, m)]), ACT.Copy)\
                        .then_inc(*S.inc("yb_copied", l, m))
                    after(("yb", l, m))
                for m in range(8):
                    act.wait_ge(*S.at("projected", ("ma", l, m)))
                    act.wait_ge(*S.at("yb_gated", l, 6 + m) if m < 2 else S.at(f"ma_out{m % 2}", l, m - 2))
                    act.activation(v3(tm[:, m % 2, :]), ps3(psum_of[("ma", l, m)]), ACT.Sigmoid)\
                        .then_inc(*S.inc("ma_sigmoid", l, m))
                    act.wait_ge(*S.at("ma_sigmoid", l, m))
                    act.dma_start(ga_d[m], tm[:, m % 2, :]).then_inc(*S.dma(f"ma_out{m % 2}", l, m))
                    after(("ma", l, m))

                def first_chunk_done(c):
                    split_hi("attn_hi", (l, c), QS[:, 2 * c, :], tm[:, 2 + c % 2, :],
                             [("gated", phases[("a", l)][18 * c + 16]["i"])])

                act_attention(act, phases[("a", l)], 18, first_chunk_done)
                for m in range(8):
                    act.wait_ge(*S.at("projected", ("ya", l, m)))
                    after(("ya", l, m))
                    split_hi("mix_hi", (l, m), H[:, 0, m, :], tm[:, m % 2, :], [("mixed", l, m)])

            def ln(i, jobs, copies=()):
                key = ("ln", i)

                def finish(h, between=None):
                    for c in range(KC):
                        if c == 3 and between:
                            between()
                        x = norm_x(key, c, h)
                        if c % 2 == 0:
                            act.wait_ge(*S.at("scaled", i, h, c))
                            act.activation(x, x, ACT.Identity, bias=ln_b[:, i, c:c + 1]).then_inc(*S.inc("ln_normed", i, h, c))
                        if i < 2:
                            split_hi("normed_hi", ("ln", i, h, c), H[:, 0, c, norm_cols(key, h)], x, [ln_normed(i, h, c)])

                for c in range(KC):
                    square(key, 0, c, ("centered", i, 0, c))
                after(jobs[0])
                root((*key, 0), cols=norm_cols(key, 0))
                finish(0, lambda: after(jobs[1]))
                for c in range(KC):
                    square(key, 1, c, ("centered", i, 1, c))
                for t in copies[0:2]:
                    copy_out(t)
                root((*key, 1), cols=norm_cols(key, 1))
                for t in copies[2:4]:
                    copy_out(t)
                finish(1)
                for t in copies[4:]:
                    copy_out(t)

            def copy_out(t):
                act.wait_ge(*S.at("final_turned", t))
                if t >= 4:
                    act.wait_ge(*S.at(f"output{t % 4}", t - 4))
                act.activation(norm_sums[:, t % 4, 0:D], ps2(psum_of[("final", t)]), ACT.Copy).then_inc(*S.inc("out_copied", t))
                act.wait_ge(*S.at("out_copied", t))
                act.dma_start(a["out"][0, t * P:(t + 1) * P, :], norm_sums[:, t % 4, 0:D])\
                    .then_inc(*S.dma(f"output{t % 4}", t))

            for c in range(6):
                act.wait_ge(*S.at("residual", DEPTH - 1, c))
                after(("out", DEPTH - 1, c))
            ln(0, [("out", DEPTH - 1, 6), ("out", DEPTH - 1, 7)])

            def gate_m2(m, slot, wait):
                act.wait_ge(*S.at("projected", ("m2", m)))
                act.wait_ge(*S.at(*wait))
                act.activation(tm[:, slot, 0:SEQ], ps2(psum_of[("m2", m)]), ACT.Sigmoid,
                               bias=b_in2[:, MG2 // P + m:MG2 // P + m + 1]).then_inc(*S.inc("m2_sigmoid", m))
                act.wait_ge(*S.at("m2_sigmoid", m))
                act.dma_start((ga_d if m < 8 else gb_d)[m % 8][:, 0:SEQ], tm[:, slot, 0:SEQ])\
                    .then_inc(*S.dma(f"m2_out{slot}", m))
                after(("m2", m))

            for m in range(M2_FIRST):
                gate_m2(m, m % 2, (f"m2_out{m % 2}", m - 2) if m >= 2 else ("scaled", 0, 1, KC - 1))

            def biased(what, c, col, slot, name, waits):
                act.wait_ge(*S.at("projected", (what, c)))
                for w in waits:
                    act.wait_ge(*S.at(*w))
                act.activation(tm[:, slot, 0:SEQ], ps2(psum_of[(what, c)]), ACT.Identity,
                               bias=b_in2[:, col // P + c:col // P + c + 1]).then_inc(*S.inc(name, what, c))
                after((what, c))

            def store_free(c, kind):
                k = c - 1 + (4 if kind == "s" else 0)
                return [(f"attn_out{k % 2}", k)] if k >= 0 else [("m2_out0", 8), ("m2_out1", 7)]

            def split_k2(what, c, src, waits):
                for w in waits:
                    act.wait_ge(*S.at(*w))
                for hh in range(2):
                    for half in range(2):
                        act.activation(K2[half * HD:(half + 1) * HD, hh, 0, :], src[hh * HD:(hh + 1) * HD, 0:SEQ], ACT.Copy)\
                            .then_inc(*S.inc("k_hi", what, c, hh, half))

            def split_q2(what, c, src, waits):
                for w in waits:
                    act.wait_ge(*S.at(*w))
                for hh in range(2):
                    part = slice(hh * HD, (hh + 1) * HD)
                    act.activation(Q2[part, hh, :], src[part, 0:SEQ], ACT.Copy).then_inc(*S.inc("q_hi", what, c, hh))

            def take_v(what, c):
                act.wait_ge(*S.at("v_turned", what, c))
                act.activation(V2[:, :, :], ps2(psum_of[("v", what, c)]).rearrange("p (k d) -> p k d", k=NQ), ACT.Copy)\
                    .then_inc(*S.inc("v_ready", what, c))

            for c in range(4):
                last = [("k_split", "nak", c - 1)] if c else []
                biased("nak", c, NAK0, 2, "raw_copied", last)
                split_k2("nak", c, tm[:, 2, :], [("raw_copied", "nak", c)])
                biased("naq", c, NAQ0, 3, "raw_copied", [("q_stacked", "naq", c - 1)] if c else [])
                split_q2("naq", c, tm[:, 3, :], [("raw_copied", "naq", c)])
                biased("nav", c, NAV0, (c + 1) % 2, "v_biased", store_free(c, "n"))
                take_v("nav", c)
                act_attention(act, [u for u in phases[("n",)] if u["c"] == c], 16, None)
            biased("swk", 0, SWK0, 3, "raw_copied", [("q_stacked", "naq", 3), ("k_split", "nak", 3)])
            biased("swv", 0, SWV0, 1, "v_biased", store_free(0, "s"))
            split_k2("swk", 0, tm[:, 2, :], [("roped", "swk", 0)])
            take_v("swv", 0)
            for c in range(4):
                biased("swq", c, SWQ0, 3, "raw_copied", [("k_split", "swk", 0)] if c == 0 else [("q_stacked", "swq", c - 1)])
                split_q2("swq", c, tm[:, 2, :], [("roped", "swq", c)])
                gate_m2(M2_BEFORE[c], (c + 1) % 2, (f"attn_out{(c + 1) % 2}", 3 + c) if c else ("v_ready", "swv", 0))

                def split_branch(k):
                    if k >= 4 and k % 2 == 0 and (k - 4) // 2 < 7:
                        b = (k - 4) // 2
                        split_hi("branches_hi", (b,), H[:, 0, b, 0:SEQ], tm[:, 2 + b % 2, 0:SEQ], [(f"attn_in{b % 2}", b)])

                def keep_gate(k):
                    if k == 16:
                        m = M2_BESIDE[c]
                        act.wait_ge(*S.at("projected", ("m2", m)))
                        if c:
                            act.wait_ge(*S.at("kept_out", M2_BESIDE[c - 1]))
                        for i in range(2):
                            act.activation(kept[:, i * BANK:(i + 1) * BANK], big[i][:, 2 * BANK:3 * BANK], ACT.Identity,
                                           bias=b_in2[:, MG2 // P + m:MG2 // P + m + 1]).then_inc(*S.inc("gate_kept", m, i))
                        act.wait_ge(*S.at("gate_kept", m, 1))
                        act.dma_start(gb_d[m - 8][:, 0:SEQ], kept[:, :]).then_inc(*S.dma("kept_out", m))
                        after(("m2", m))

                act_attention(act, [u for u in phases[("s",)] if u["c"] == c], 16, None,
                              split_branch if c == 3 else keep_gate)
            split_hi("branches_hi", (7,), H[:, 0, 7, 0:SEQ], tm[:, 1, 0:SEQ], [("gated", phases[("s",)][-2]["i"])])
            for m in range(8):
                if m + 8 in M2_BESIDE:
                    t = tm[:, 2 + m % 2, 0:SEQ]
                    act.wait_ge(*S.at(f"mix2_in{m % 2}", "b", m))
                    act.activation(t, t, ACT.Sigmoid).then_inc(*S.inc("late_sigmoid", m))
                for job in (("y1", m), ("y2", m)):
                    act.wait_ge(*S.at("projected", job))
                    after(job)
                split_hi("mix2_hi", (m,), SP2[:, 0, m, :], tm[:, m % 2, 0:SEQ], [("mixed2", m)])
            for m in range(8):
                t = tm[:, 2 + m % 2, 0:SEQ]
                act.wait_ge(*S.at(f"h_old{m % 2}", m))
                act.activation(t, t, ACT.Identity, scale=ALPHA, bias=b_o[:, 0, m:m + 1]).then_inc(*S.inc("h_scaled", m))
                if m < 6:
                    act.wait_ge(*S.at("projected", ("out2", m)))
                    after(("out2", m))
            ln(1, [("out2", 6), ("out2", 7)])
            for f in range(4):
                for m in range(8):
                    act.wait_ge(*S.at("projected", ("ff1", f, m)))
                    n = f * 8 + m
                    if n >= 2:
                        act.wait_ge(*S.at("hidden_lo", (n - 2) // 8, (n - 2) % 8))
                    else:
                        act.wait_ge(*S.at("scaled", 1, 1, KC - 1))
                    act.activation(tm[:, n % 2, 0:SEQ], ps2(psum_of[("ff1", f, m)]), ACT.Relu, bias=b_ff1[:, n:n + 1])\
                        .then_inc(*S.inc("hidden_relu", f, m))
                    after(("ff1", f, m))
                    act.wait_ge(*S.at("hidden_relu", f, m))
                    act.activation(tm[:, n % 2, 0:SEQ], tm[:, n % 2, 0:SEQ], ACT.Square)\
                        .then_inc(*S.inc("hidden_squared", f, m))
                    split_hi("hidden_hi", (f, m), SP2[:, 0, m, :], tm[:, n % 2, 0:SEQ], [("hidden_squared", f, m)])
                for m in range(8 if f < 3 else 6):
                    act.wait_ge(*S.at("projected", ("ff2", f, m)))
                    after(("ff2", f, m))
            ln(2, [("ff2", 3, 6), ("ff2", 3, 7)], range(NQ))

        @block.gpsimd
        def _(pool):
            def lo_part(ins, name, *key):
                ins.then_inc(*S.inc(name, *key))

            def subtract(name, key, dst, src, hi, waits):
                for w in waits:
                    pool.wait_ge(*S.at(*w))
                pool.tensor_tensor(dst, src, hi.bitcast(F32), ALU.subtract).then_inc(*S.inc(name, *key))

            def weight_lo(n):
                if n < len(loads):
                    _, _, cols, rows = loads[n]
                    view = lambda ap: ap.rearrange("p (k n) -> p k n", k=KC)[:, 0:rows, 0:cols]
                    subtract("weight_lo", (n,), view(wsp[:, n % 2, 1, :]), view(raw[:, n % RAW, :]),
                             view(wsp[:, n % 2, 0, :]), [("weight_hi", n)])

            def after(job):
                weight_lo(nload[job] + 2)

            def load(name, key, dst, src, waits):
                for w in waits:
                    pool.wait_ge(*S.at(*w))
                pool.dma_start(dst, src).then_inc(*S.dma(name, *key))

            store = load

            for j in range(NQ + 1):
                src = a["meta_tokens"] if j == 0 else a["x"][0, (j - 1) * P:j * P, :]
                load(f"x_in{j % 4}", (j,), tm[0:(META if j == 0 else P), j % 4, 0:D], src,
                     [("x_transposed", j - 4)] if j >= 4 else [])

            def times_cos(key, dst, src, trig, waits):
                for w in waits:
                    pool.wait_ge(*S.at(*w))
                pool.tensor_tensor(dst, src, trig, ALU.mult).then_inc(*S.inc("times_cos", *key))

            def bands():
                pool.memset(zeros[:, :], 0.0).then_inc(*S.inc("zeros"))
                n_rpb = HEADS * 15 * 31
                store("rpb_pad", (0,), rpb_d[0:64].rearrange("(a n) -> a n", a=1), zeros[0:1, :], [("zeros",)])
                store("rpb_pad", (1,), rpb_d[64 + n_rpb:].rearrange("(a n) -> a n", a=1), zeros[0:1, :], [])
                store("rpb_pad", (2,), rpb_d[64:64 + n_rpb].rearrange("(a n) -> a n", a=8),
                      a["na_rpb_2"][0].rearrange("h i j -> h (i j)"), [])
                for h in range(HEADS):
                    src = bass.AP(rpb_d.tensor, 64 + h * 15 * 31 + 15, [[31, 15], [-1, GRID], [1, GRID]])
                    store("bands", (h,), band_d[h], src, [("rpb_pad", 2)])

            def pair_sums(key, h):
                for c in (0, 2):
                    pool.wait_ge(*S.at("squared", *key, h, c + 1))
                    t = norm_temp(key, c, h)
                    pool.tensor_tensor(t, t, norm_temp(key, c + 1, h), ALU.add).then_inc(*S.inc("pair_sum", *key, h, c))

            def normed_lo_parts(key, h, chunks):
                for c in chunks:
                    if normed_lo(*key, h, c)[0] == "normed_lo":
                        cols = norm_cols(key, h)
                        x = tm[:, 1 + c % 3, cols] if key[0] == "rms" else norm_x(key, c, h)
                        subtract("normed_lo", (*key, h, c), H[:, 1, c, cols], x, H[:, 0, c, cols],
                                 [("normed_hi", *key, h, c)])

            lo64 = slice(0, HD)
            for l in range(DEPTH):
                key = ("rms", l)
                if l == 0:
                    pair_sums(key, 0)
                    weight_lo(0)
                    normed_lo_parts(key, 0, range(3))
                    weight_lo(1)
                    normed_lo_parts(key, 0, range(3, KC))
                    pair_sums(key, 1)
                    store("x_stored", (), xT_d.rearrange("k p n -> p k n"), X[:, :, :], [("x_turned", NQ), ("x_padded",)])
                else:
                    after(("out", l - 1, 6))
                    normed_lo_parts(key, 0, range(3))
                    after(("out", l - 1, 7))
                    normed_lo_parts(key, 0, range(3, KC))
                    for m in (6, 7):
                        store("x_saved", (l - 1, m), xT_d[m], X[:, m, :], [("residual", l - 1, m, 1)])
                normed_lo_parts(key, 1, range(KC))
                x_read = [("normed", "rms", l, 1, KC - 1), ("x_saved", l - 1, 7) if l else ("x_stored",)]
                load("pool_weights", (l,), pw[:, :, :], a["pool_w"][l].rearrange("g c d -> c g d"), x_read)
                load("rotary_tables", (l,), trig1[:, :, :], a["c_trig1"], [])
                pool.wait_ge(*S.at("rotary_tables", l))
                for c in range(5):
                    after(("q", l, c) if c < 4 else ("ki", l))
                    if c >= 1:
                        x, y = sc4[2 * ((c - 1) % 2)], sc4[2 * ((c - 1) % 2) + 1]
                        times_cos(("q", l, c - 1), x, y, trig1[:, 0, :],
                                  [("raw_copied", "q", l, c - 1), ("head_square", "q", l, c - 1)])
                times_cos(("ki", l), tm[lo64, 2, :], tm[lo64, 3, :], trig1[lo64, 0, :],
                          [("raw_copied", "ki", l), ("q_stacked", "q", l, 3)])
                after(("kv", l))
                times_cos(("k", l), sc4[3][lo64], sc4[1][lo64], trig1[lo64, 0, :], [("raw_copied", "k", l)])
                after(("qi", l, 0))
                for c in range(4):
                    times_cos(("qi", l, c), qi_temps(c)[1], qi_temps(c)[0], trig1[:, 0, :],
                              [("raw_copied", "qi", l, c)])
                    after(("qi", l, c + 1) if c < 3 else ("gatea", l, 0))

                def pool_gate(g):
                    pool.wait_ge(*S.at("pool_scaled", l, g))
                    pool.wait_ge(*S.at("gateb_silu", l, g))
                    pool.tensor_tensor(tm[:, 1, :], tm[:, 1, :], tm[:, 3, :], ALU.mult)\
                        .then_inc(*S.inc("pool_gated", l, g))
                    subtract("pool_lo", (l, g), QIPB[:, 4 + g, :], tm[:, 1, :], QIPB[:, g, :],
                             [("pool_hi", l, g), ("k_split", "k", l)])

                for g, w in enumerate(WINDOWS):
                    after(("u", l, g))
                    if g:
                        pool_gate(g - 1)
                    pool.wait_ge(*S.at("u_copied", l, g))
                    if g:
                        pool.wait_ge(*S.at("pool_lo", l, g - 1))
                    src, d, slot = tm[:, 0, :], 1, 1
                    while d < w:
                        dst = tm[:, slot, :]
                        pool.tensor_copy(dst[:, 0:d], src[:, 0:d]).then_inc(*S.inc("window_step", l, g, "edge", d))
                        pool.tensor_tensor(dst[:, d:TP], src[:, d:TP], src[:, 0:TP - d], ALU.add)\
                            .then_inc(*S.inc("window_step", l, g, "sum", d))
                        pool.wait_ge(*S.at("window_step", l, g, "edge", d))
                        pool.wait_ge(*S.at("window_step", l, g, "sum", d))
                        src, d, slot = dst, 2 * d, 3 - slot
                    pool.tensor_tensor(src[:, 0:16], src[:, 0:16], edge[:, g, :], ALU.mult)\
                        .then_inc(*S.inc("window_step", l, g, "count"))
                    pool.wait_ge(*S.at("window_step", l, g, "count"))
                    pool.tensor_scalar(src, src, 1.0 / w, None, ALU.mult).then_inc(*S.inc("window_step", l, g, "mean"))
                    pool.wait_ge(*S.at("window_step", l, g, "mean"))
                    pool.tensor_tensor(tm[:, 0, :], src, tm[:, 0, :], ALU.subtract).then_inc(*S.inc("pooled", l, g))
                    after(("gateb", l, g))
                pool_gate(3)
                for c in range(1, 4):
                    after(("gatea", l, c))
                for m in range(8):
                    after(("mb", l, m))
                    after(("yb", l, m))
                    pool.wait_ge(*S.at("mb_sigmoid", l, m))
                    pool.wait_ge(*S.at("yb_copied", l, m))
                    y = tm[:, 2 + m % 2, :]
                    pool.tensor_tensor(y, y, tm[:, m % 2, :], ALU.mult).then_inc(*S.inc("yb_gated", l, m))
                    store(f"yb_out{m % 2}", (l, m), gb_d[m], y, [("yb_gated", l, m)])
                for m in range(8):
                    after(("ma", l, m))
                    if m == 1:
                        load("mask0_in", (l,), mask0[:, :], a["c_mask0"], [("projected", ("yb", l, 7))])
                units = phases[("a", l)]
                for c in range(4):
                    load(f"silu_in{c % 2}", (l, c), tm[:, c % 2, :], sg_d[c],
                         [(f"gate_out{c % 2}", "a", l, c),
                          (f"ma_out{c % 2}", l, 6 + c) if c < 2 else ("gated", units[18 * (c - 2) + 16]["i"])])
                    if c == 1 and l == 0:
                        bands()
                    if c >= 1:
                        subtract("attn_lo", (l, c - 1), QS[:, 2 * c - 1, :], tm[:, 2 + (c - 1) % 2, :],
                                 QS[:, 2 * c - 2, :], [("attn_hi", l, c - 1)])
                subtract("attn_lo", (l, 3), QS[:, 7, :], tm[:, 3, :], QS[:, 6, :], [("attn_hi", l, 3)])
                for m in range(-2, 8):
                    if m >= 0:
                        after(("ya", l, m))
                        subtract("mix_lo", (l, m), H[:, 1, m, :], tm[:, m % 2, :], H[:, 0, m, :], [("mix_hi", l, m)])
                    n = m + 2
                    if n < 8:
                        load(f"mix_in{n % 2}", ("a", l, n), tm[:, n % 2, :], ga_d[n],
                             [(f"ma_out{n % 2}", l, n)] +
                             ([("gated", units[18 * (2 + n) + 16]["i"])] if n < 2 else [("mix_lo", l, n - 2)]))
                        load(f"mix_in{n % 2}", ("b", l, n), tm[:, 2 + n % 2, :], gb_d[n],
                             [(f"yb_out{n % 2}", l, n), ("attn_lo", l, 3)] + ([("mixed", l, n - 2)] if n >= 2 else []))
                for m in range(-2, 6):
                    if m >= 0:
                        after(("out", l, m))
                        if l < DEPTH - 1:
                            store("x_saved", (l, m), xT_d[m], X[:, m, :], [("residual", l, m)])
                    n = m + 2
                    if n < 8:
                        load(f"x_old{n % 2}", (l, n), tm[:, 2 + n % 2, :], xT_d[n],
                             [("x_stored",) if l == 0 else ("x_saved", l - 1, 7),
                              ("mixed", l, 6 + n) if n < 2 else ("residual", l, n - 2)])
            def ln(i, jobs):
                key = ("ln", i)
                pair_sums(key, 0)
                after(jobs[0])
                normed_lo_parts(key, 0, range(3 if i < 2 else 0))
                after(jobs[1])
                normed_lo_parts(key, 0, range(3, KC if i < 2 else 0))
                pair_sums(key, 1)
                normed_lo_parts(key, 1, range(KC if i < 2 else 0))

            ln(0, [("out", DEPTH - 1, 6), ("out", DEPTH - 1, 7)])
            z2_free = ("normed_lo_dve", "ln", 0, 1, 7)

            def bias_loads(c):
                for hh in range(2):
                    for half in range(2):
                        src = band_d[2 * c + hh, 1 - half:15 - half].rearrange("i w k -> w i k")
                        load("bias_in", (c, hh, half), bias_e[half * GRID:(half + 1) * GRID, hh, :, :], src,
                             [("bands", HEADS - 1), z2_free] + ([("masked", phases[("n",)][16 * c - 1]["i"])] if c else []))

            def bias_tables(c, hh):
                if hh == 0:
                    pool.wait_ge(*S.at("bias_in", c, 1, 1))
                    pool.wait_ge(*S.at("block2_consts", 3))
                e = bias_e[:, hh, :, :]
                pool.tensor_scalar(e, e, 1.0 / SCALE, None, ALU.mult).then_inc(*S.inc("bias_step", c, hh, "scaled"))
                pool.wait_ge(*S.at("bias_step", c, hh, "scaled"))
                pool.tensor_tensor(e, e, colmask[:, :, :], ALU.add).then_inc(*S.inc("bias_step", c, hh, "masked"))
                pool.wait_ge(*S.at("bias_step", c, hh, "masked"))
                pool.tensor_tensor(bias_i[:, hh, :, :], e[:, 2:11, :], rowmask[:, :, :], ALU.add)\
                    .then_inc(*S.inc("bias_ready", c, hh))

            for m in range(3):
                after(("m2", m))
            for c in range(KC):
                cols = slice(META, META + SEQ)
                store("ln_saved", (c,), xT_d[c][:, 0:SEQ], X[:, c, cols], [ln_normed(0, 1, c)])
            for i, (dst, src) in enumerate(((trig2, "c_trig2"), (colmask, "c_colmask"), (rowmask, "c_rowmask"),
                                            (swmask, "c_swmask"))):
                load("block2_consts", (i,), dst[:], a[src], [z2_free] if i == 0 else [])
            for m in range(3, M2_FIRST):
                after(("m2", m))
            for c in range(4):
                bias_loads(c)
                if c:
                    bias_tables(c, 0)
                after(("nak", c))
                if c == 0:
                    bias_tables(c, 0)
                bias_tables(c, 1)
                after(("naq", c))
                after(("nav", c))
                store(f"attn_out{c % 2}", (c,), at_d[c], tm[:, c % 2, 0:SEQ],
                      [("gated", phases[("n",)][16 * c + 14]["i"])])
            after(("swk", 0))
            times_cos(("swk", 0), tm[:, 2, 0:SEQ], tm[:, 3, 0:SEQ], trig2[:, 0, :],
                      [("raw_copied", "swk", 0), ("k_split", "nak", 3)])
            after(("swv", 0))
            for c in range(4):
                after(("swq", c))
                times_cos(("swq", c), tm[:, 2, 0:SEQ], tm[:, 3, 0:SEQ], trig2[:, 0, :],
                          [("raw_copied", "swq", c), ("q_stacked", "swq", c - 1) if c else ("k_split", "swk", 0)])
                for m in M2_BEFORE[c:c + 1] + M2_BESIDE[c:c + 1]:
                    after(("m2", m))
                if c < 3:
                    store(f"attn_out{c % 2}", (4 + c,), at_d[4 + c], tm[:, c % 2, 0:SEQ],
                          [("gated", phases[("s",)][16 * c + 14]["i"])])
            for k in range(-2, 7):
                if k >= 0:
                    subtract("branches_lo", (k,), H[:, 1, k, 0:SEQ], tm[:, 2 + k % 2, 0:SEQ], H[:, 0, k, 0:SEQ],
                             [("branches_hi", k)])
                n = k + 2
                if n < 7:
                    load(f"attn_in{n % 2}", (n,), tm[:, 2 + n % 2, 0:SEQ], at_d[n],
                         [("attn_out0", 6), ("attn_out1", 5), ("q_stacked", "swq", 3)] if n < 2
                         else [("branches_lo", n - 2)])

            def load_gate_b(n):
                load(f"mix2_in{n % 2}", ("b", n), tm[:, 2 + n % 2, 0:SEQ], gb_d[n][:, 0:SEQ],
                     [("mixed2", n - 2)] if n >= 2 else [("branches_lo", 6 - n), ("m2_out0", 15), ("m2_out1", 13), ("kept_out", 14)])

            def load_gate_a(n):
                load(f"mix2_in{n % 2}", ("a", n), tm[:, n % 2, 0:SEQ], ga_d[n][:, 0:SEQ],
                     [("mix2_lo", n - 2)] if n >= 2 else [("branches_lo", 7)] if n else [])

            load_gate_b(0)
            load_gate_a(0)
            load_gate_b(1)
            subtract("branches_lo", (7,), H[:, 1, 7, 0:SEQ], tm[:, 1, 0:SEQ], H[:, 0, 7, 0:SEQ], [("branches_hi", 7)])
            load_gate_a(1)
            for m in range(8):
                after(("y1", m))
                after(("y2", m))
                subtract("mix2_lo", (m,), SP2[:, 1, m, :], tm[:, m % 2, 0:SEQ], SP2[:, 0, m, :], [("mix2_hi", m)])
                if m < 6:
                    load_gate_a(m + 2)
                    load_gate_b(m + 2)
            for m in range(8):
                load(f"h_old{m % 2}", (m,), tm[:, 2 + m % 2, 0:SEQ], xT_d[m][:, 0:SEQ],
                     [("ln_saved", 7), ("mixed2", 6 + m) if m < 2 else ("residual2", m - 2)])
                if m < 6:
                    after(("out2", m))
            ln(1, [("out2", 6), ("out2", 7)])
            for f in range(4):
                for m in range(8):
                    after(("ff1", f, m))
                    subtract("hidden_lo", (f, m), SP2[:, 1, m, :], tm[:, m % 2, 0:SEQ], SP2[:, 0, m, :],
                             [("hidden_hi", f, m)])
                for m in range(8 if f < 3 else 6):
                    after(("ff2", f, m))
            ln(2, [("ff2", 3, 6), ("ff2", 3, 7)])

        @block.vector
        def _(dve):
            steps = [0]

            def step(ins):
                steps[0] += 1
                ins.then_inc(*S.inc("vector_step", steps[0]))
                dve.wait_ge(*S.at("vector_step", steps[0]))

            def wait(*events):
                for e in events:
                    dve.wait_ge(*S.at(*e))

            def rstd(key, name, src, eps, rows=slice(0, P), cols=slice(0, TP), banks=3, between=None):
                va, rt, out = (t[rows, cols] for t in chain_temps(key))
                shaped = lambda ap: ap.rearrange("p (b n) -> p b n", b=banks) if banks > 1 else ap
                wait(name)
                dve.tensor_scalar(shaped(va), src, eps, None, ALU.add).then_inc(*S.inc("variance", *key))
                if between:
                    between()
                wait(("rstd_part", *key, 2))
                step(dve.scalar_tensor_tensor(rt, rt, -0.5, va, ALU.mult, ALU.mult))
                dve.scalar_tensor_tensor(out, rt, 1.5, out, ALU.add, ALU.mult).then_inc(*S.inc("rstd", *key))
                wait(("rstd", *key))

            def rotate(key, x, y, src, sin, last=None):
                wait(("rotated", *key), ("times_cos", *key))
                dve.tensor_tensor(y, src, sin, ALU.mult).then_inc(*S.inc("rot_times_sin", *key))
                wait(("rot_times_sin", *key))

            def stack_q(name, key, src, dst):
                for hh in range(2):
                    own, other = slice(hh * HD, (hh + 1) * HD), slice((1 - hh) * HD, (2 - hh) * HD)
                    wait(("q_hi", name, *key, hh))
                    dve.tensor_tensor(dst(hh, other), src[own], dst(hh, own).bitcast(F32), ALU.subtract)\
                        .then_inc(*(S.inc("q_stacked", name, *key) if hh else S.inc("stack_part", name, *key)))

            def split_k(name, l, src):
                wait(("k_hi", name, l, 1))
                for half in range(2):
                    dve.tensor_tensor(KK[half * HD:(half + 1) * HD, 1, :], src, KK[0:HD, 0, :].bitcast(F32), ALU.subtract)\
                        .then_inc(*(S.inc("k_split", name, l) if half else S.inc("stack_part", name, l)))

            def attention(units, mask_waits, gate):
                for k in range(len(units) + 4):
                    if 2 <= k <= len(units) + 1:
                        move(dve, units[k - 2], "dve")
                    if k < len(units):
                        u, i = units[k], units[k]["i"]
                        wait(("logits", i), *mask_waits(u))
                        if i >= 2:
                            wait(("exped", i - 2))
                        if i >= 4:
                            wait(("normed_out", i - 4))
                        start = -TAKEN if u["sink"] is None else sink[:, 1, u["sink"]:u["sink"] + 1]
                        dve.tensor_tensor_reduce(out=Lb[:, i % 2, 0:u["n"]], in0=big[0][:, 0:u["n"]], in1=u["mask"],
                                                 scale=-SCALE, scalar=start, op0=ALU.add, op1=ALU.min,
                                                 accum_out=negmax[:, i % 4:i % 4 + 1]).then_inc(*S.inc("masked", i))
                    if k >= 4 and (k - 4) % 2 == 1:
                        gate(units[k - 5], small[1])
                    if 3 <= k <= len(units) + 2:
                        u, i = units[k - 3], units[k - 3]["i"]
                        s, slot = rowsum[:, i % 4:i % 4 + 1], (k - 3) // 2 % 2
                        wait(("weighted", i))
                        if u["sink"] is not None:
                            wait(("sink_exped", i))
                            step(dve.tensor_tensor(s, s, sinkexp[:, i % 4:i % 4 + 1], ALU.add))
                        if i - u["hh"] - 4 >= 0:
                            wait(("out_turned", i - u["hh"] - 4))
                        step(dve.reciprocal(rowinv[:, i % 4:i % 4 + 1], s))
                        dve.tensor_scalar(Ob[:, slot, u["hh"] * HD:(u["hh"] + 1) * HD],
                                          small[u["hh"]][:, 0:HD],
                                          rowinv[:, i % 4:i % 4 + 1], None, ALU.mult).then_inc(*S.inc("normed_out", i))

            def subtract_lo(key, h, c):
                cols = norm_cols(key, h)
                x = tm[:, 1 + c % 3, cols] if key[0] == "rms" else norm_x(key, c, h)
                wait(("normed_hi", *key, h, c))
                dve.tensor_tensor(H[:, 1, c, cols], x, H[:, 0, c, cols].bitcast(F32), ALU.subtract)\
                    .then_inc(*S.inc("normed_lo_dve", *key, h, c))

            def pair_sum(key, h):
                t = norm_temp(key, 4, h)
                wait(("squared", *key, h, 5))
                dve.tensor_tensor(t, t, norm_temp(key, 5, h), ALU.add).then_inc(*S.inc("pair_sum_dve", *key, h, 4))

            def add_square(c):
                key, total = ("rms", 1), norm_sums[:, 0, :]
                wait(("squared", *key, c), ("square_sum", *key, c - 1) if c > 1 else ("squared", *key, 0))
                dve.tensor_tensor(total, total, norm_sums[:, c, :], ALU.add).then_inc(*S.inc("square_sum", *key, c))

            def norm_rstd(key, h):
                src, banks = small2[:, BANK:2 * BANK], 1
                if key[0] == "rms":
                    src, banks = small2[:, 0:PIECE1], 1
                    if h == 0:
                        src, banks = small2[:, :].rearrange("p (b n) -> p b n", b=2)[:, :, 0:PIECE1], 2
                rstd((*key, h), ("mean_square", *key, h), src, EPS if key[0] == "rms" else LN_EPS,
                     cols=norm_cols(key, h), banks=banks)

            def normed(l, h):
                key, cols = ("rms", l), norm_cols(("rms", l), h)
                for c in range(KC):
                    if c >= 3:
                        wait(normed_lo(*key, h, c - 3))
                    dve.scalar_tensor_tensor(tm[:, 1 + c % 3, cols], X[:, c, cols], gain[:, l, c:c + 1], tm[:, 0, cols],
                                             ALU.mult, ALU.mult).then_inc(*S.inc("normed", *key, h, c))
                    if c in (2, 4, 6):
                        subtract_lo(key, h, c - 1)
                subtract_lo(key, h, 7)

            def sum_x(i, c):
                if 1 <= c < 6:
                    key = ("ln", i)
                    total = (norm_sums_h if i else norm_sums)[:, 0, 0:SEQ]
                    x = lambda c: X[:, c, META:META + SEQ] if i == 0 else X[:, c, 0:SEQ]
                    wait(norm_input(key, c), ("x_sum", i, c - 1) if c > 1 else norm_input(key, 0))
                    dve.tensor_tensor(total, total if c > 1 else x(0), x(c), ALU.add).then_inc(*S.inc("x_sum", i, c))

            dve.memset(X[:, :, T:TP], 0.0).then_inc(*S.inc("x_padded"))
            for j in range(NQ + 1):
                wait(("x_transposed", j))
                t0, rows = (0, META) if j == 0 else (META + (j - 1) * P, P)
                dve.tensor_copy(X[:, :, t0:t0 + rows],
                                big[j % 2][:, 0:KC * P].rearrange("p (k n) -> p k n", k=KC)[:, :, 0:rows])\
                    .then_inc(*S.inc("x_turned", j))
            lo64 = slice(0, HD)
            for l in range(DEPTH):
                key = ("rms", l)
                if l == 0:
                    pair_sum(key, 0)
                    norm_rstd(key, 0)
                normed(l, 0)
                if l == 0:
                    pair_sum(key, 1)
                norm_rstd(key, 1)
                normed(l, 1)
                wait(("normed_lo", "rms", l, 1, 6), ("normed_lo_dve", "rms", l, 1, 7), ("rotary_tables", l))
                for c in range(4):
                    x, y = sc4[2 * (c % 2)], sc4[2 * (c % 2) + 1]

                    def rotate_q():
                        rotate(("q", l, c), x, v3(y), ps3(psum_of[("rotated", "q", l, c)]), v3(trig1[:, 1, :]))
                        step(dve.tensor_tensor(x, x, y, ALU.add))

                    rstd(("head", "q", l, c), ("head_square", "q", l, c), ps3(psum_of[("head_square", "q", l, c)]), EPS,
                         between=rotate_q)
                    dve.tensor_tensor(x, x, tm[:, 2, :], ALU.mult).then_inc(*S.inc("roped", "q", l, c))
                    stack_q("q", (l, c), x, lambda hh, rows: QS[rows, 2 * c + hh, :])
                rotate(("ki", l), None, v3(tm[lo64, 3, :]), ps3(psum_of[("rotated", "ki", l)], lo64), v3(trig1[lo64, 1, :]))
                dve.tensor_tensor(tm[lo64, 2, :], tm[lo64, 2, :], tm[lo64, 3, :], ALU.add)\
                    .then_inc(*S.inc("roped", "ki", l))
                split_k("ki", l, tm[lo64, 2, :])
                def rotate_k():
                    rotate(("k", l), None, v3(sc4[1][lo64]), ps3(psum_of[("rotated", "k", l)], lo64), v3(trig1[lo64, 1, :]))
                    step(dve.tensor_tensor(sc4[3][lo64], sc4[3][lo64], sc4[1][lo64], ALU.add))

                rstd(("head", "k", l), ("head_square", "k", l), ps3(psum_of[("head_square", "k", l)], lo64), EPS, lo64,
                     between=rotate_k)
                wait(("x_saved", l - 1, 7) if l else ("x_stored",))
                dve.tensor_tensor(k_roped[lo64, :], sc4[3][lo64], sc4[2][lo64], ALU.mult).then_inc(*S.inc("roped", "k", l))
                wait(("w_ready", l), ("v_turned", l), ("roped", "k", l))
                nrelu = 0
                for c in range(4):
                    before, after = qi_temps(c)
                    rotate(("qi", l, c), None, v3(before), ps3(psum_of[("rotated", "qi", l, c)]), v3(trig1[:, 1, :]))
                    dve.tensor_tensor(after, after, before, ALU.add)\
                        .then_inc(*S.inc("roped", "qi", l, c))
                    stack_q("qi", (l, c), after, lambda hh, rows: QIPB[rows, 2 * (c % 2) + hh, :])
                    for hh in range(2):
                        for j in range(1, NQ):
                            n, h = visible(j), 2 * c + hh
                            sc = SC[:, SCORE_AT[j]:SCORE_AT[j] + n]
                            wait(("relued", l, c, hh, j))
                            r, w = tm[:, nrelu % 2, 0:n], widx[:, j, h:h + 1]
                            if h == 0:
                                ins = dve.tensor_scalar(sc, r, w, None, ALU.mult)
                            else:
                                wait(("score_added", l, *score_units[nrelu - (NQ - 1)]))
                                ins = dve.scalar_tensor_tensor(sc, r, w, sc, ALU.mult, ALU.add)
                            ins.then_inc(*S.inc("score_added", l, c, hh, j))
                            nrelu += 1
                split_k("k", l, k_roped[lo64, :])
                hidden = {j: SC[0:HD, SCORE_AT[j] + visible(j) - CHUNK:SCORE_AT[j] + visible(j)] for j in range(1, NQ)}
                wait(("score_added", l, *score_units[-1]))
                for j in range(1, NQ):
                    dve.memset(hidden[j], NEG).then_inc(*S.inc("mask_step", l, "hidden", j))
                rounds = [(r, j) for r in range(TOPK // 8) for j in range(1, NQ)]
                for x in range(len(rounds) + 1):
                    if x < len(rounds):
                        r, j = rounds[x]
                        wait(("taken", l, r - 1, j) if r else ("mask_step", l, "hidden", j))
                        dve.max(top8[:, j, :], SC[:, SCORE_AT[j]:SCORE_AT[j] + visible(j)])\
                            .then_inc(*S.inc("eight", l, r, j))
                    if x >= 1:
                        r, j = rounds[x - 1]
                        sc = SC[:, SCORE_AT[j]:SCORE_AT[j] + visible(j)]
                        wait(("eight", l, r, j))
                        dve.match_replace(sc, top8[:, j, :], sc, TAKEN).then_inc(*S.inc("taken", l, r, j))
                for j in range(1, NQ):
                    sc = SC[:, SCORE_AT[j]:SCORE_AT[j] + visible(j)]
                    wait(("taken", l, TOPK // 8 - 1, j))
                    dve.tensor_scalar(sc, sc, TAKEN / 2, NEG, ALU.is_gt, ALU.mult).then_inc(*S.inc("mask_step", l, "made", j))
                for j in range(1, NQ):
                    wait(("mask_step", l, "made", j))
                    dve.memset(hidden[j], NEG).then_inc(*S.inc("mask_ready", l, j))

                def gate(u, bank):
                    c, slot = u["c"], tm[:, 2 + u["c"] % 2, :]
                    if u["first"]:
                        wait((f"silu_in{c % 2}", l, c), ("attn_lo", l, c - 2) if c >= 2 else ("ma_out1", l, 7))
                        dve.memset(slot[:, T:TP], 0.0).then_inc(*S.inc("attn_padded", l, c))
                    wait(("out_turned", u["i"]))
                    cols = slice(u["q0"], u["q0"] + u["nq"])
                    dve.tensor_tensor(slot[:, cols], bank[:, P:P + u["nq"]], tm[:, c % 2, cols], ALU.mult)\
                        .then_inc(*S.inc("gated", u["i"]))

                attention(phases[("a", l)], lambda u: [("mask_ready", l, NQ - 1), ("mask0_in", l)], gate)
                for m in range(8):
                    t = tm[:, m % 2, :]
                    wait(("projected", ("ya", l, m)), (f"mix_in{m % 2}", "b", l, m))
                    dve.tensor_tensor(v3(t), ps3(psum_of[("ya", l, m)]), v3(t), ALU.mult)\
                        .then_inc(*S.inc("mix_gated", l, m))
                    wait(("mix_gated", l, m))
                    dve.tensor_tensor(t, t, tm[:, 2 + m % 2, :], ALU.add).then_inc(*S.inc("mixed", l, m))
                def residual(m, h=None):
                    key = ("rms", l + 1) if l < DEPTH - 1 else ("ln", 0)
                    s, old = big[psum_of[("out", l, m)]], tm[:, 2 + m % 2, :]
                    wait(("projected", ("out", l, m), *([0] if h == 0 else [])), (f"x_old{m % 2}", l, m))
                    if key[0] == "ln":
                        cols = slice(META, META + SEQ) if h is None else slice(META + h * BANK, META + (h + 1) * BANK)
                        at = slice(cols.start - META, cols.stop - META)
                        x, y, z = X[:, m, cols], s[:, at], old[:, cols]
                    elif h is None:
                        x, y, z = v3(X[:, m, :]), ps3(psum_of[("out", l, m)]), v3(old)
                    else:
                        cols, banks = norm_cols(key, h), slice(0, 2) if h == 0 else slice(2, 3)
                        x, y, z = (v3(ap)[:, banks] for ap in (X[:, m, :], s[:, :], old))
                        y = y[:, :, 0:PIECE1]
                    dve.tensor_tensor(x, y, z, ALU.add).then_inc(*S.inc("residual", l, m, *([] if h is None else [h])))

                for m in range(6):
                    residual(m)
                    if l == DEPTH - 1:
                        sum_x(0, m)
                    elif m >= 2:
                        add_square(m - 1)
                if l < DEPTH - 1:
                    residual(6, 0)
                    add_square(5)
                    residual(7, 0)
                    residual(6, 1)
                    norm_rstd(("rms", l + 1), 0)
                    residual(7, 1)

            def ln(i, residual):
                key = ("ln", i)

                def center(h):
                    wait(("mean", i, h))
                    for c in range(KC):
                        x = norm_x(key, c, h)
                        dve.tensor_tensor(x, x, small2[:, 0:BANK], ALU.subtract).then_inc(*S.inc("centered", i, h, c))
                    pair_sum(key, h)

                def scale(h, between=None):
                    for c in range(KC):
                        if c == 2 and between:
                            between()
                        x = norm_x(key, c, h)
                        dve.scalar_tensor_tensor(x, x, ln_g[:, i, c:c + 1], tm[:, 0, norm_cols(key, h)], ALU.mult, ALU.mult)\
                            .then_inc(*S.inc("scaled", i, h, c))
                        if c % 2:
                            wait(("scaled", i, h, c))
                            dve.tensor_scalar(x, x, ln_b[:, i, c:c + 1], None, ALU.add)\
                                .then_inc(*S.inc("ln_normed_dve", i, h, c))
                        if i < 2 and c == 2:
                            subtract_lo(key, h, 0)
                    if i < 2:
                        subtract_lo(key, h, 7)

                residual(6, 0)
                residual(7, 0)
                center(0)
                residual(6, 1)
                norm_rstd(key, 0)
                scale(0, lambda: residual(7, 1))
                center(1)
                norm_rstd(key, 1)
                scale(1)

            ln(0, residual)

            def gate2(kind):
                def gate(u, bank):
                    c = u["c"]
                    k = c + (4 if kind == "s" else 0)
                    if u["q0"] == 0 and k >= 2:
                        wait((f"attn_out{k % 2}", k - 2))
                    if u["q0"] == 0 and k >= 5:
                        wait((f"m2_out{k % 2}", M2_BEFORE[k - 5]))
                    wait(("out_turned", u["i"]))
                    dve.tensor_copy(tm[:, c % 2, u["q0"]:u["q0"] + P], bank[:, P:2 * P]).then_inc(*S.inc("gated", u["i"]))
                return gate

            for c in range(4):
                for hh in range(2):
                    for half in range(2):
                        own = slice(hh * HD, (hh + 1) * HD)
                        wait(("k_hi", "nak", c, hh, half), ("k_hi", "nak", c, hh, 1))
                        dve.tensor_tensor(K2[half * HD:(half + 1) * HD, hh, 1, :], tm[own, 2, 0:SEQ],
                                          K2[own, hh, 0, :].bitcast(F32), ALU.subtract)\
                            .then_inc(*(S.inc("k_split", "nak", c) if hh and half else S.inc("stack_part", "nak", c, hh, half)))
                stack_q("naq", (c,), tm[:, 3, 0:SEQ], lambda hh, rows: Q2[rows, hh, :])
                attention([u for u in phases[("n",)] if u["c"] == c],
                          lambda u: [("bias_ready", c, 1), ("ln_saved", KC - 1), ("normed_lo", "ln", 0, 1, 6)], gate2("n"))
            for c in range(-1, 4):
                key = ("swk", 0) if c < 0 else ("swq", c)
                rotate(key, None, tm[:, 3, 0:SEQ], ps2(psum_of[("rotated", *key)]), trig2[:, 1, :])
                dve.tensor_tensor(tm[:, 2, 0:SEQ], tm[:, 2, 0:SEQ], tm[:, 3, 0:SEQ], ALU.add)\
                    .then_inc(*S.inc("roped", *key))
                if c < 0:
                    for hh in range(2):
                        for half in range(2):
                            own = slice(hh * HD, (hh + 1) * HD)
                            wait(("k_hi", "swk", 0, hh, 1))
                            dve.tensor_tensor(K2[half * HD:(half + 1) * HD, hh, 1, :], tm[own, 2, 0:SEQ],
                                              K2[own, hh, 0, :].bitcast(F32), ALU.subtract)\
                                .then_inc(*(S.inc("k_split", "swk", 0) if hh and half else
                                            S.inc("stack_part", "swk", 0, hh, half)))
                    continue
                stack_q("swq", (c,), tm[:, 2, 0:SEQ], lambda hh, rows: Q2[rows, hh, :])
                attention([u for u in phases[("s",)] if u["c"] == c], lambda u: [("minus_sink",)], gate2("s"))
            for m in range(8):
                t, t2 = tm[:, m % 2, 0:SEQ], tm[:, 2 + m % 2, 0:SEQ]
                wait(("projected", ("y1", m)), (f"mix2_in{m % 2}", "a" if m < 2 else "b", m))
                dve.tensor_tensor(t, ps2(psum_of[("y1", m)]), t, ALU.mult).then_inc(*S.inc("y1_gated", m))
                wait(("projected", ("y2", m)))
                if m + 8 in M2_BESIDE:
                    wait(("late_sigmoid", m))
                dve.tensor_tensor(t2, ps2(psum_of[("y2", m)]), t2, ALU.mult).then_inc(*S.inc("y2_gated", m))
                wait(("y1_gated", m), ("y2_gated", m))
                dve.tensor_tensor(t, t, t2, ALU.add).then_inc(*S.inc("mixed2", m))
            def residual2(m, h=None):
                cols = slice(0, SEQ) if h is None else norm_cols(("ln", 1), h)
                wait(("projected", ("out2", m), *([0] if h == 0 else [])), ("h_scaled", m))
                dve.tensor_tensor(X[:, m, cols], tm[:, 2 + m % 2, cols], big[psum_of[("out2", m)]][:, cols], ALU.add)\
                    .then_inc(*S.inc("residual2", m, *([] if h is None else [h])))

            for m in range(6):
                residual2(m)
                sum_x(1, m)
            ln(1, residual2)

            def residual3(f, m, h=None):
                cols = slice(0, SEQ) if h is None else norm_cols(("ln", 2), h)
                x = X[:, m, cols]
                wait(("projected", ("ff2", f, m), *([0] if h == 0 else [])))
                event = S.inc("residual3", f, m, *([] if h is None else [h]))
                if f == 0:
                    step(dve.scalar_tensor_tensor(x, x, ALPHA, ps2(psum_of[("ff2", f, m)]), ALU.mult, ALU.add))
                    dve.tensor_scalar(x, x, b_o[:, 1, m:m + 1], None, ALU.add).then_inc(*event)
                else:
                    wait(("residual3", f - 1, m))
                    dve.tensor_tensor(x, x, big[psum_of[("ff2", f, m)]][:, cols], ALU.add).then_inc(*event)

            for f in range(4):
                for m in range(8 if f < 3 else 6):
                    residual3(f, m)
                    if f == 3:
                        sum_x(2, m)
            ln(2, lambda m, h: residual3(3, m, h))

        return S.seen


def constants():
    f = np.float32
    c = {"c_ident": np.eye(P, dtype=f)}

    def rotation(half, period):
        r = np.zeros((P, P), f)
        for m in range(P):
            d = m % HD
            if d < half:
                r[m + half, m] = -1.0
            elif d < period:
                r[m - half, m] = 1.0
        return r

    c["c_rot1"], c["c_rot2"] = rotation(HD // 2, HD), rotation(8, 16)
    c["c_headmean"] = np.kron(np.eye(2), np.full((HD, HD), 1.0 / HD)).astype(f)
    c["c_allmean"] = np.full((P, P), 1.0 / D, f)

    def trig(theta, dim, length, cols):
        inv = (f(1.0) / (f(theta) ** (np.arange(0, dim, 2, dtype=f) / f(dim)))).astype(f)
        ang = (np.arange(length, dtype=f)[:, None] * inv[None, :]).astype(f)
        t = np.zeros((P, 2, cols), f)
        t[:, 0, :] = 1.0
        for p in range(P):
            d = p % HD
            if d < dim:
                t[p, 0, :length] = np.cos(ang[:, d % (dim // 2)])
                t[p, 1, :length] = np.sin(ang[:, d % (dim // 2)])
        return t

    c["c_trig1"] = trig(10000.0, HD, T, TP)
    c["c_trig2"] = trig(500000.0, 16, SEQ, SEQ)
    edge = np.ones((P, 4, 16), f)
    for g, w in enumerate(WINDOWS):
        edge[:, g, :] = w / np.minimum(np.arange(1, 17), w)
    c["c_edge"] = edge
    m0 = np.zeros((P, visible(0)), f)
    m0[0:HD, visible(0) - CHUNK:] = NEG
    c["c_mask0"] = m0
    col = np.full((P, 14, GRID), NEG, f)
    for p in range(P):
        s = min(max(p % GRID - 8, 0), GRID - 16)
        col[p, :, s:s + 16] = 0.0
    c["c_colmask"] = col
    row = np.zeros((P, 9, GRID), f)
    row[0:GRID, 8, :] = NEG
    row[GRID:, 0, :] = NEG
    c["c_rowmask"] = row
    k, q = np.arange(3 * P)[None, :] - P, np.arange(P)[:, None]
    c["c_swmask"] = np.where(np.abs(k - q) <= P, 0.0, NEG).astype(f)
    return c


def kernel(**inputs):
    import concourse.bacc as bacc
    from concourse.bass_utils import run_bass_kernel_spmd as run

    arrays = {k: np.ascontiguousarray(v) for k, v in inputs.items()}
    arrays.update(constants())

    def build(known):
        nc = bacc.Bacc("TRN2", target_bir_lowering=False, num_devices=1)
        a = {k: nc.dram_tensor(f"in_{k}", v.shape, F32, kind="ExternalInput").ap() for k, v in arrays.items()}
        a["out"] = nc.dram_tensor("out_0", (1, SEQ, D), F32, kind="ExternalOutput").ap()
        return nc, program(nc, a, known)

    _, counts = build(None)
    nc, _ = build(counts)
    r = run(nc, [{f"in_{k}": v for k, v in arrays.items()}], core_ids=[0])
    return r.results[0]["out_0"]
```
